# Optimizing a Trainium2 kernel written in Bass

```python
import math
import jax, jax.numpy as jnp
from jax import lax
import numpy as np

D_MODEL = 1024
BATCH = 1
SEQ = 512
DEPTH = 2

CHUNK = 64
N_META = 16
Q_BLOCK = 128
HEAD_DIM = 64
DIFF_WIDTH = D_MODEL // 2
FOX_WIDTH = D_MODEL - DIFF_WIDTH
DIFF_HEADS = DIFF_WIDTH // (2 * HEAD_DIM)
FOX_HEADS = FOX_WIDTH // HEAD_DIM
ROT_DIM = HEAD_DIM // 4
ROPE_THETA = 500000.0
RMS_EPS = 1e-6
SUBLN_EPS = 1e-5
COL_SIZES = (DIFF_WIDTH, DIFF_WIDTH, DIFF_WIDTH, DIFF_WIDTH,
             FOX_WIDTH, FOX_WIDTH, FOX_WIDTH, FOX_HEADS, FOX_WIDTH)
D_IN = 4 * DIFF_WIDTH + 4 * FOX_WIDTH + FOX_HEADS


def rmsnorm(x, gain, eps=RMS_EPS):
    xf = x.astype(jnp.float32)
    y = xf * lax.rsqrt(jnp.mean(xf * xf, axis=-1, keepdims=True) + eps)
    return (y * gain.astype(jnp.float32)).astype(x.dtype)

def partial_rope(t, cos, sin):
    half = ROT_DIM // 2
    t1, t2, tp = t[..., :half], t[..., half:ROT_DIM], t[..., ROT_DIM:]
    cos = cos.astype(t.dtype)
    sin = sin.astype(t.dtype)
    return jnp.concatenate([t1 * cos - t2 * sin, t2 * cos + t1 * sin, tp], axis=-1)

def to_blocks(t, axis):
    shp = t.shape
    nb = shp[axis] // Q_BLOCK
    t = t.reshape(shp[:axis] + (nb, Q_BLOCK) + shp[axis + 1:])
    return jnp.moveaxis(t, axis, 0)

def from_blocks(o):
    o = jnp.moveaxis(o, 0, 2)
    b, h, nb, qb, d = o.shape
    return o.reshape(b, h, nb * qb, d)

def diff_attention(q, k, v, lam, chunk_ids):
    scale = HEAD_DIM ** -0.5
    q_blocks = to_blocks(q, 3)
    cq_blocks = chunk_ids.reshape(-1, Q_BLOCK)

    def step(blk):
        qb, cq = blk
        s = jnp.einsum('bhmqd,bhmkd->bhmqk', qb, k).astype(jnp.float32) * scale
        visible = chunk_ids[None, :] <= cq[:, None]
        s = jnp.where(visible, s, -jnp.inf)
        p = jax.nn.softmax(s, axis=-1)
        a = p[:, :, 0] - lam * p[:, :, 1]
        return jnp.einsum('bhqk,bhkd->bhqd', a.astype(v.dtype), v)

    return from_blocks(lax.map(step, (q_blocks, cq_blocks)))

def forgetting_attention(q, k, v, cum_logf, positions):
    scale = HEAD_DIM ** -0.5
    q_blocks = to_blocks(q, 2)
    c_blocks = jnp.moveaxis(cum_logf.reshape(cum_logf.shape[:2] + (-1, Q_BLOCK)), 2, 0)
    p_blocks = positions.reshape(-1, Q_BLOCK)

    def step(blk):
        qb, cq, pq = blk
        s = jnp.einsum('bhqd,bhkd->bhqk', qb, k).astype(jnp.float32) * scale
        s = s + cq[..., None] - cum_logf[:, :, None, :]
        visible = positions[None, :] <= pq[:, None]
        s = jnp.where(visible, s, -jnp.inf)
        p = jax.nn.softmax(s, axis=-1)
        return jnp.einsum('bhqk,bhkd->bhqd', p.astype(v.dtype), v)

    return from_blocks(lax.map(step, (q_blocks, c_blocks, p_blocks)))

def first_inputs(seed: int = 0) -> dict:
    key = jax.random.key(seed)
    ks = jax.random.split(key, 12)
    f32 = jnp.float32
    return {
        "x": jax.random.normal(ks[0], (BATCH, SEQ, D_MODEL), f32),
        "meta_tokens": jax.random.normal(ks[1], (N_META, D_MODEL), f32),
        "norm_gain": 1.0 + 0.02 * jax.random.normal(ks[2], (DEPTH, D_MODEL), f32),
        "w_in": jax.random.normal(ks[3], (DEPTH, D_MODEL, D_IN), f32) * D_MODEL ** -0.5,
        "forget_bias": 0.1 * jax.random.normal(ks[4], (DEPTH, FOX_HEADS), f32),
        "lambda_q1": 0.1 * jax.random.normal(ks[5], (DEPTH, HEAD_DIM), f32),
        "lambda_k1": 0.1 * jax.random.normal(ks[6], (DEPTH, HEAD_DIM), f32),
        "lambda_q2": 0.1 * jax.random.normal(ks[7], (DEPTH, HEAD_DIM), f32),
        "lambda_k2": 0.1 * jax.random.normal(ks[8], (DEPTH, HEAD_DIM), f32),
        "subln_gain": 1.0 + 0.02 * jax.random.normal(ks[9], (DEPTH, 2 * HEAD_DIM), f32),
        "w_out": jax.random.normal(ks[10], (DEPTH, D_MODEL, D_MODEL), f32) * D_MODEL ** -0.5,
        "final_gain": 1.0 + 0.02 * jax.random.normal(ks[11], (D_MODEL,), f32),
    }

def first_block(x, meta_tokens, norm_gain, w_in, forget_bias, lambda_q1, lambda_k1,
              lambda_q2, lambda_k2, subln_gain, w_out, final_gain):
    b, seq, d = x.shape
    total = N_META + seq
    lp = ((total + Q_BLOCK - 1) // Q_BLOCK) * Q_BLOCK
    meta = jnp.broadcast_to(meta_tokens.astype(x.dtype)[None], (b, N_META, d))
    h = jnp.concatenate([meta, x], axis=1)
    h = jnp.pad(h, ((0, 0), (0, lp - total), (0, 0)))

    positions = jnp.arange(lp, dtype=jnp.int32)
    chunk_ids = jnp.where(positions < N_META, 0, (positions - N_META) // CHUNK + 1)
    inv_freq = 1.0 / (ROPE_THETA ** (jnp.arange(0, ROT_DIM, 2, dtype=jnp.float32) / ROT_DIM))
    ang = positions.astype(jnp.float32)[:, None] * inv_freq[None, :]
    cos = jnp.cos(ang)[None, :, None, None, :]
    sin = jnp.sin(ang)[None, :, None, None, :]
    split_points = [int(v) for v in np.cumsum(COL_SIZES)[:-1]]

    for l in range(DEPTH):
        hn = rmsnorm(h, norm_gain[l])
        proj = hn @ w_in[l]
        dq, dk, dv, dg, fq, fk, fv, ff, fg = jnp.split(proj, split_points, axis=-1)

        dq = partial_rope(dq.reshape(b, lp, DIFF_HEADS, 2, HEAD_DIM), cos, sin)
        dk = partial_rope(dk.reshape(b, lp, DIFF_HEADS, 2, HEAD_DIM), cos, sin)
        dq = jnp.transpose(dq, (0, 2, 3, 1, 4))
        dk = jnp.transpose(dk, (0, 2, 3, 1, 4))
        dv = jnp.transpose(dv.reshape(b, lp, DIFF_HEADS, 2 * HEAD_DIM), (0, 2, 1, 3))
        lam_init = 0.8 - 0.6 * math.exp(-0.3 * l)
        lam = (jnp.exp(jnp.sum(lambda_q1[l].astype(jnp.float32) * lambda_k1[l].astype(jnp.float32)))
               - jnp.exp(jnp.sum(lambda_q2[l].astype(jnp.float32) * lambda_k2[l].astype(jnp.float32)))
               + lam_init)
        do = diff_attention(dq, dk, dv, lam, chunk_ids)
        do = rmsnorm(do, subln_gain[l], SUBLN_EPS) * (1.0 - lam_init)
        do = jnp.transpose(do, (0, 2, 1, 3)).reshape(b, lp, DIFF_WIDTH)
        do = do * jax.nn.silu(dg)

        fq = jnp.transpose(fq.reshape(b, lp, FOX_HEADS, HEAD_DIM), (0, 2, 1, 3))
        fk = jnp.transpose(fk.reshape(b, lp, FOX_HEADS, HEAD_DIM), (0, 2, 1, 3))
        fv = jnp.transpose(fv.reshape(b, lp, FOX_HEADS, HEAD_DIM), (0, 2, 1, 3))
        log_f = jax.nn.log_sigmoid(ff.astype(jnp.float32) + forget_bias[l].astype(jnp.float32))
        cum_logf = jnp.transpose(jnp.cumsum(log_f, axis=1), (0, 2, 1))
        fo = forgetting_attention(fq, fk, fv, cum_logf, positions)
        fo = jnp.transpose(fo, (0, 2, 1, 3)).reshape(b, lp, FOX_WIDTH)
        fo = fo * jax.nn.silu(fg)

        h = h + jnp.concatenate([do, fo], axis=-1) @ w_out[l]

    out = rmsnorm(h, final_gain)
    return out[:, N_META:N_META + seq]


DEPTH_2 = 1

MEM_LEN = 256
NSA_HEADS = 8
NSA_KV_HEADS = 2
NSA_GROUP = NSA_HEADS // NSA_KV_HEADS
SB_HEADS = 8
MIX_WIDTH = (NSA_HEADS + SB_HEADS) * HEAD_DIM
CMP_LEN = 32
CMP_STRIDE = 16
CMP_HIDDEN = 256
SEL_BLOCK = 64
SEL_TOPK = 16
WINDOW = 512
ROT_DIM_2 = HEAD_DIM // 4
MEM_HEADS = 4
D_FF = 2816
NORM_EPS = 1e-6
NEG = -1e30
FORCE_SCORE = 1e4

KV_W = NSA_KV_HEADS * HEAD_DIM
IN_SPLITS = [NSA_HEADS * HEAD_DIM, KV_W, KV_W, KV_W, KV_W, KV_W, KV_W, NSA_HEADS * 3,
             SB_HEADS * HEAD_DIM, SB_HEADS * HEAD_DIM, SB_HEADS * HEAD_DIM]
IN_COLS = sum(IN_SPLITS)


def rms_norm(x, g):
    x32 = x.astype(jnp.float32)
    y = x32 * lax.rsqrt(jnp.mean(x32 * x32, axis=-1, keepdims=True) + NORM_EPS)
    return (y * g.astype(jnp.float32)).astype(x.dtype)

def rope_angles(pos):
    freqs = ROPE_THETA ** (-jnp.arange(0, ROT_DIM_2, 2, dtype=jnp.float32) / ROT_DIM_2)
    return pos.astype(jnp.float32)[..., None] * freqs

def apply_rope(x, ang):
    half = ROT_DIM_2 // 2
    x1, x2, xp = x[..., :half], x[..., half:ROT_DIM_2], x[..., ROT_DIM_2:]
    c = jnp.cos(ang).astype(x.dtype)
    s = jnp.sin(ang).astype(x.dtype)
    return jnp.concatenate([x1 * c - x2 * s, x2 * c + x1 * s, xp], axis=-1)

def masked_softmax(s, mask):
    s = jnp.where(mask, s.astype(jnp.float32), NEG)
    m = jnp.max(s, axis=-1, keepdims=True)
    p = jnp.where(mask, jnp.exp(s - m), 0.0)
    return p / jnp.maximum(jnp.sum(p, axis=-1, keepdims=True), 1e-30)

def swiglu(h, wg, wu, wd):
    return (jax.nn.silu(h @ wg) * (h @ wu)) @ wd

def overlap_matrix(n_cmp, n_sel):
    cs = np.arange(n_cmp)[:, None] * CMP_STRIDE
    ss = np.arange(n_sel)[None, :] * SEL_BLOCK
    ov = np.minimum(cs + CMP_LEN, ss + SEL_BLOCK) - np.maximum(cs, ss)
    return jnp.asarray(np.clip(ov, 0, None).astype(np.float32) / CMP_LEN)

def compress(t, pe, w1, w2):
    B, H, T, dk = t.shape
    ratio = CMP_LEN // CMP_STRIDE
    n_chunks = T // CMP_STRIDE
    n_cmp = n_chunks - ratio + 1
    chunks = t.reshape(B, H, n_chunks, CMP_STRIDE, dk)
    blocks = jnp.concatenate([chunks[:, :, r:r + n_cmp] for r in range(ratio)], axis=3)
    blocks = blocks + pe
    flat = blocks.reshape(B, H, n_cmp, CMP_LEN * dk)
    return jax.nn.gelu(flat @ w1) @ w2

def nsa_mixer(q, k_cmp, v_cmp, k_sel, v_sel, k_win, v_win, gates, pos,
              pe_k, w1_k, w2_k, pe_v, w1_v, w2_v, g_q, g_kc, g_ks, g_kw):
    B, T = q.shape[:2]
    dk = HEAD_DIM
    scale = dk ** -0.5
    ang = rope_angles(pos)
    q = q.reshape(B, T, NSA_KV_HEADS, NSA_GROUP, dk).transpose(0, 2, 3, 1, 4)
    q = apply_rope(rms_norm(q, g_q), ang[:, None, None])

    def heads(t):
        return t.reshape(B, T, NSA_KV_HEADS, dk).transpose(0, 2, 1, 3)

    n_cmp = (T - CMP_LEN) // CMP_STRIDE + 1
    cmp_end = jnp.arange(n_cmp) * CMP_STRIDE + CMP_LEN - 1
    ang_c = rope_angles(pos[:, cmp_end])
    kc = apply_rope(rms_norm(compress(heads(k_cmp), pe_k, w1_k, w2_k), g_kc), ang_c[:, None])
    vc = compress(heads(v_cmp), pe_v, w1_v, w2_v)
    n_sel = T // SEL_BLOCK
    top_n = min(SEL_TOPK, n_sel)
    ks_blocks = apply_rope(rms_norm(heads(k_sel), g_ks), ang[:, None]).reshape(B, NSA_KV_HEADS, n_sel, SEL_BLOCK, dk)
    vs_blocks = heads(v_sel).reshape(B, NSA_KV_HEADS, n_sel, SEL_BLOCK, dk)
    w_ov = overlap_matrix(n_cmp, n_sel)
    pad = ((0, 0), (0, 0), (WINDOW, 0), (0, 0))
    kw_pad = jnp.pad(apply_rope(rms_norm(heads(k_win), g_kw), ang[:, None]), pad)
    vw_pad = jnp.pad(heads(v_win), pad)
    gates = jax.nn.sigmoid(gates.reshape(B, T, NSA_KV_HEADS, NSA_GROUP, 3).transpose(0, 2, 3, 1, 4))

    bi = jnp.arange(B)[:, None, None, None]
    hi = jnp.arange(NSA_KV_HEADS)[None, :, None, None]
    jblk = jnp.arange(n_sel)

    def block_fn(i):
        s0 = i * Q_BLOCK
        tq = s0 + jnp.arange(Q_BLOCK)
        qb = lax.dynamic_slice_in_dim(q, s0, Q_BLOCK, axis=3)
        gb = lax.dynamic_slice_in_dim(gates, s0, Q_BLOCK, axis=3)
        m_c = cmp_end[None, :] <= tq[:, None]
        p_c = masked_softmax(jnp.einsum('bhgqd,bhnd->bhgqn', qb, kc) * scale, m_c)
        o_c = jnp.einsum('bhgqn,bhnd->bhgqd', p_c, vc)
        imp = jnp.einsum('bhgqn,nj->bhqj', p_c, w_ov)
        cur = tq // SEL_BLOCK
        valid = jblk[None, :] * SEL_BLOCK <= tq[:, None]
        forced = (jblk[None, :] == 0) | (jblk[None, :] == cur[:, None]) | (jblk[None, :] == cur[:, None] - 1)
        score = jnp.where(valid & forced, FORCE_SCORE, jnp.where(valid, imp, -1.0))
        _, idx = lax.top_k(score, top_n)
        ksb = ks_blocks[bi, hi, idx].reshape(B, NSA_KV_HEADS, Q_BLOCK, top_n * SEL_BLOCK, dk)
        vsb = vs_blocks[bi, hi, idx].reshape(B, NSA_KV_HEADS, Q_BLOCK, top_n * SEL_BLOCK, dk)
        kpos = (idx[..., None] * SEL_BLOCK + jnp.arange(SEL_BLOCK)).reshape(B, NSA_KV_HEADS, Q_BLOCK, -1)
        m_s = (kpos <= tq[:, None])[:, :, None]
        p_s = masked_softmax(jnp.einsum('bhgqd,bhqkd->bhgqk', qb, ksb) * scale, m_s)
        o_s = jnp.einsum('bhgqk,bhqkd->bhgqd', p_s, vsb)
        kwb = lax.dynamic_slice_in_dim(kw_pad, s0, Q_BLOCK + WINDOW, axis=2)
        vwb = lax.dynamic_slice_in_dim(vw_pad, s0, Q_BLOCK + WINDOW, axis=2)
        kpos_w = s0 - WINDOW + jnp.arange(Q_BLOCK + WINDOW)
        diff = tq[:, None] - kpos_w[None, :]
        m_w = (kpos_w[None, :] >= 0) & (diff >= 0) & (diff < WINDOW)
        p_w = masked_softmax(jnp.einsum('bhgqd,bhkd->bhgqk', qb, kwb) * scale, m_w)
        o_w = jnp.einsum('bhgqk,bhkd->bhgqd', p_w, vwb)
        o = gb[..., 0:1] * o_c + gb[..., 1:2] * o_s + gb[..., 2:3] * o_w
        return o.astype(q.dtype)

    out = lax.map(block_fn, jnp.arange(T // Q_BLOCK))
    return out.transpose(1, 0, 4, 2, 3, 5).reshape(B, T, NSA_HEADS * dk)

def stick_breaking(q, k, v):
    B, T = q.shape[:2]
    dk = HEAD_DIM
    scale = dk ** -0.5

    def heads(t):
        return t.reshape(B, T, SB_HEADS, dk).transpose(0, 2, 1, 3)

    q, k, v = heads(q), heads(k), heads(v)
    kpos = jnp.arange(T)

    def block_fn(i):
        s0 = i * Q_BLOCK
        tq = s0 + jnp.arange(Q_BLOCK)
        qb = lax.dynamic_slice_in_dim(q, s0, Q_BLOCK, axis=2)
        z = jnp.einsum('bhqd,bhkd->bhqk', qb, k).astype(jnp.float32) * scale
        mask = kpos[None, :] < tq[:, None]
        log_rem = jnp.where(mask, jax.nn.log_sigmoid(-z), 0.0)
        suffix = lax.cumsum(log_rem, axis=3, reverse=True) - log_rem
        a = jnp.where(mask, jnp.exp(jax.nn.log_sigmoid(z) + suffix), 0.0)
        return jnp.einsum('bhqk,bhkd->bhqd', a, v).astype(q.dtype)

    out = lax.map(block_fn, jnp.arange(T // Q_BLOCK))
    return out.transpose(1, 0, 3, 2, 4).reshape(B, T, SB_HEADS * dk)

def memory_cross_attention(h, mem_n, wq, wk, wv, wo, g_q, g_k):
    B, T = h.shape[:2]
    M = mem_n.shape[1]
    q = rms_norm((h @ wq).reshape(B, T, MEM_HEADS, HEAD_DIM), g_q)
    k = rms_norm((mem_n @ wk).reshape(B, M, MEM_HEADS, HEAD_DIM), g_k)
    v = (mem_n @ wv).reshape(B, M, MEM_HEADS, HEAD_DIM)
    s = jnp.einsum('bqhd,bkhd->bhqk', q, k).astype(jnp.float32) * HEAD_DIM ** -0.5
    p = jax.nn.softmax(s, axis=-1)
    o = jnp.einsum('bhqk,bkhd->bqhd', p, v).astype(h.dtype).reshape(B, T, MEM_HEADS * HEAD_DIM)
    return o @ wo

def second_inputs(seed: int = 0) -> dict:
    key = jax.random.key(seed)
    ks = iter(jax.random.split(key, 40))

    def dense(shape, fan_in):
        return jax.random.normal(next(ks), (DEPTH_2,) + shape, jnp.float32) * fan_in ** -0.5

    def gain(n):
        return 1.0 + 0.05 * jax.random.normal(next(ks), (DEPTH_2, n), jnp.float32)

    x = jax.random.normal(next(ks), (BATCH, SEQ, D_MODEL), jnp.float32)
    mem = jax.random.normal(next(ks), (BATCH, MEM_LEN, D_MODEL), jnp.float32)
    start = jax.random.randint(next(ks), (BATCH, 1), 0, 4096, dtype=jnp.int32)
    positions = (start + jnp.arange(SEQ, dtype=jnp.int32)[None, :]).astype(jnp.int32)
    return {
        "x": x, "mem": mem, "positions": positions,
        "ffn1_norm": gain(D_MODEL),
        "ffn1_wg": dense((D_MODEL, D_FF), D_MODEL),
        "ffn1_wu": dense((D_MODEL, D_FF), D_MODEL),
        "ffn1_wd": dense((D_FF, D_MODEL), D_FF),
        "mix_norm": gain(D_MODEL),
        "w_in": dense((D_MODEL, IN_COLS), D_MODEL),
        "nsa_q_norm": gain(HEAD_DIM),
        "nsa_kc_norm": gain(HEAD_DIM),
        "nsa_ks_norm": gain(HEAD_DIM),
        "nsa_kw_norm": gain(HEAD_DIM),
        "cmp_pos_k": 0.1 * jax.random.normal(next(ks), (DEPTH_2, CMP_LEN, HEAD_DIM), jnp.float32),
        "cmp_w1_k": dense((CMP_LEN * HEAD_DIM, CMP_HIDDEN), CMP_LEN * HEAD_DIM),
        "cmp_w2_k": dense((CMP_HIDDEN, HEAD_DIM), CMP_HIDDEN),
        "cmp_pos_v": 0.1 * jax.random.normal(next(ks), (DEPTH_2, CMP_LEN, HEAD_DIM), jnp.float32),
        "cmp_w1_v": dense((CMP_LEN * HEAD_DIM, CMP_HIDDEN), CMP_LEN * HEAD_DIM),
        "cmp_w2_v": dense((CMP_HIDDEN, HEAD_DIM), CMP_HIDDEN),
        "w_out": dense((MIX_WIDTH, D_MODEL), MIX_WIDTH),
        "mem_x_norm": gain(D_MODEL),
        "mem_kv_norm": gain(D_MODEL),
        "mem_wq": dense((D_MODEL, MEM_HEADS * HEAD_DIM), D_MODEL),
        "mem_wk": dense((D_MODEL, MEM_HEADS * HEAD_DIM), D_MODEL),
        "mem_wv": dense((D_MODEL, MEM_HEADS * HEAD_DIM), D_MODEL),
        "mem_q_norm": gain(HEAD_DIM),
        "mem_k_norm": gain(HEAD_DIM),
        "mem_wo": dense((MEM_HEADS * HEAD_DIM, D_MODEL), MEM_HEADS * HEAD_DIM),
        "ffn2_norm": gain(D_MODEL),
        "ffn2_wg": dense((D_MODEL, D_FF), D_MODEL),
        "ffn2_wu": dense((D_MODEL, D_FF), D_MODEL),
        "ffn2_wd": dense((D_FF, D_MODEL), D_FF),
    }

def second_block(x, mem, positions, ffn1_norm, ffn1_wg, ffn1_wu, ffn1_wd, mix_norm, w_in,
              nsa_q_norm, nsa_kc_norm, nsa_ks_norm, nsa_kw_norm,
              cmp_pos_k, cmp_w1_k, cmp_w2_k, cmp_pos_v, cmp_w1_v, cmp_w2_v, w_out,
              mem_x_norm, mem_kv_norm, mem_wq, mem_wk, mem_wv, mem_q_norm, mem_k_norm, mem_wo,
              ffn2_norm, ffn2_wg, ffn2_wu, ffn2_wd):
    split_at = [int(c) for c in np.cumsum(IN_SPLITS)[:-1]]
    for l in range(DEPTH_2):
        x = x + 0.5 * swiglu(rms_norm(x, ffn1_norm[l]), ffn1_wg[l], ffn1_wu[l], ffn1_wd[l])
        h = rms_norm(x, mix_norm[l])
        (q_n, kc, vc, ksl, vsl, kwn, vwn, gts, q_s, k_s, v_s) = jnp.split(h @ w_in[l], split_at, axis=-1)
        o_nsa = nsa_mixer(q_n, kc, vc, ksl, vsl, kwn, vwn, gts, positions,
                          cmp_pos_k[l], cmp_w1_k[l], cmp_w2_k[l], cmp_pos_v[l], cmp_w1_v[l], cmp_w2_v[l],
                          nsa_q_norm[l], nsa_kc_norm[l], nsa_ks_norm[l], nsa_kw_norm[l])
        o_sb = stick_breaking(q_s, k_s, v_s)
        x = x + jnp.concatenate([o_nsa, o_sb], axis=-1) @ w_out[l]
        x = x + memory_cross_attention(rms_norm(x, mem_x_norm[l]), rms_norm(mem, mem_kv_norm[l]),
                                       mem_wq[l], mem_wk[l], mem_wv[l], mem_wo[l],
                                       mem_q_norm[l], mem_k_norm[l])
        x = x + 0.5 * swiglu(rms_norm(x, ffn2_norm[l]), ffn2_wg[l], ffn2_wu[l], ffn2_wd[l])
    return x


def setup_inputs(seed=0):
    out = dict(first_inputs(seed))
    for name, value in second_inputs(seed + 1).items():
        if name != "x":
            out[name + "_2"] = value
    return out


def reference(
    x, meta_tokens, norm_gain, w_in, forget_bias, lambda_q1, lambda_k1, lambda_q2, lambda_k2,
    subln_gain, w_out, final_gain, mem_2, positions_2, ffn1_norm_2, ffn1_wg_2, ffn1_wu_2,
    ffn1_wd_2, mix_norm_2, w_in_2, nsa_q_norm_2, nsa_kc_norm_2, nsa_ks_norm_2, nsa_kw_norm_2,
    cmp_pos_k_2, cmp_w1_k_2, cmp_w2_k_2, cmp_pos_v_2, cmp_w1_v_2, cmp_w2_v_2, w_out_2,
    mem_x_norm_2, mem_kv_norm_2, mem_wq_2, mem_wk_2, mem_wv_2, mem_q_norm_2, mem_k_norm_2,
    mem_wo_2, ffn2_norm_2, ffn2_wg_2, ffn2_wu_2, ffn2_wd_2,
):
    x = first_block(
        x, meta_tokens, norm_gain, w_in, forget_bias, lambda_q1, lambda_k1, lambda_q2,
        lambda_k2, subln_gain, w_out, final_gain,
    )
    return second_block(
        x, mem_2, positions_2, ffn1_norm_2, ffn1_wg_2, ffn1_wu_2, ffn1_wd_2, mix_norm_2, w_in_2,
        nsa_q_norm_2, nsa_kc_norm_2, nsa_ks_norm_2, nsa_kw_norm_2, cmp_pos_k_2, cmp_w1_k_2,
        cmp_w2_k_2, cmp_pos_v_2, cmp_w1_v_2, cmp_w2_v_2, w_out_2, mem_x_norm_2, mem_kv_norm_2,
        mem_wq_2, mem_wk_2, mem_wv_2, mem_q_norm_2, mem_k_norm_2, mem_wo_2, ffn2_norm_2,
        ffn2_wg_2, ffn2_wu_2, ffn2_wd_2,
    )


_drawn_inputs = setup_inputs


def setup_inputs(seed=0):
    import zlib

    import numpy as np

    out = dict(_drawn_inputs(seed))
    spreads = {}
    factors = {'forget_bias': 3.593,
     'subln_gain': 5.716,
     'nsa_q_norm_2': 8.0,
     'nsa_kc_norm_2': 8.0,
     'nsa_ks_norm_2': 8.0,
     'nsa_kw_norm_2': 8.0,
     'cmp_pos_k_2': 8.0,
     'cmp_pos_v_2': 3.254,
     'mem_x_norm_2': 8.0,
     'mem_kv_norm_2': 8.0,
     'mem_q_norm_2': 8.0,
     'mem_k_norm_2': 8.0,
     'ffn2_norm_2': 3.24}
    for name, (base, spread) in spreads.items():
        noise = np.random.default_rng([zlib.crc32(name.encode()), seed]).standard_normal(out[name].shape)
        drawn = base * np.exp(spread * noise) if base else spread * noise
        out[name] = __import__('jax').numpy.asarray(drawn.astype(out[name].dtype))
    for name, factor in factors.items():
        out[name] = (out[name] * factor).astype(out[name].dtype)
    return out
```

```python
import math
from contextlib import ExitStack

import numpy as np

import concourse.bass as bass
from concourse import mybir

F32 = mybir.dt.float32
F32R = mybir.dt.float32r
I32 = mybir.dt.int32
ALU = mybir.AluOpType
ACT = mybir.ActivationFunctionType
AX = mybir.AxisListType

D = 1024
T = 512
M = 16
L = M + T
KT = 8
FT = 22
NEG = -1e30
CW = 1120
LN_EXP = "natural_log_exp_and_others"



def chunk_sizes():
    ffn = [1024] * (2 * FT) + [1024, 1024, 768] * 8
    s = []
    for _ in range(2):
        s += [1024] * 8 + [1024] * 4 + [1024] * 8 + [1024] * 2 + [1056] * 2 + [1024] * 8
        s += [1024] * 8
    s += ffn
    s += [1024] * 14 + [1120] * 2 + [1024] * 4
    s += [1024] * 10
    s += [1024] * 8
    s += [1024] * 6 + [1024] * 2
    s += ffn
    return s


CONST = {}
_n = 0
for _name, _w in [("ident", 128), ("mean", 128), ("blk", 128), ("rot", 128), ("causal", 128),
                  ("chunk", 128), ("freq", 1), ("cos", L), ("sin", L),
                  ("strictT", 128), ("tri", 128), ("negone", 128), ("cmpadd", 128), ("cmp01", 128)]:
    CONST[_name] = (_n, _n + _w)
    _n += _w
NCONST = _n
NC1 = CONST["strictT"][0]

PARAM = {}
_n = 0
for _name, _w in [("g_norm0", 8), ("g_norm1", 8), ("g_final", 8), ("g_ffn1", 8), ("g_mix", 8),
                  ("g_memx", 8), ("g_memkv", 8), ("g_ffn2", 8), ("g_sub0", 1), ("g_sub1", 1),
                  ("g_q", 1), ("g_kc", 1), ("g_ks", 1), ("g_kw", 1), ("g_mq", 1), ("g_mk", 1),
                  ("fb0", 8), ("fb1", 8), ("lam0", 2), ("lam1", 2), ("pe_k", 16), ("pe_v", 16),
                  ("w2k", 256), ("w2v", 128)]:
    PARAM[_name] = (_n, _n + _w)
    _n += _w
NPARAM = _n


class Queue:

    def __init__(self, sem):
        self.sem, self.n, self.items = sem, 0, []

    def last(self):
        return (self.sem, self.n) if self.n else None

    def __call__(self, fn, *waits, alone=True, signal=True):
        w = list(waits)
        if alone:
            w.append(self.last())
        if signal:
            self.n += 1
        self.items.append((w, fn, signal))
        return (self.sem, self.n)

    def emit(self, eng):
        seen = {}
        for waits, fn, signal in self.items:
            need = {}
            flat = list(waits)
            while flat:
                t = flat.pop()
                if t is None:
                    continue
                if isinstance(t, list):
                    flat += t
                    continue
                s, v = t
                if seen.get(s, 0) < v:
                    need[s] = max(need.get(s, 0), v)
            for s, v in need.items():
                eng.wait_ge(s, v)
                seen[s] = v
            r = fn(eng)
            if signal:
                r.then_inc(self.sem, 1)


class Ring:

    def __init__(self, bufs):
        self.bufs, self.k, self.rel, self.held = bufs, -1, [[] for _ in bufs], [False] * len(bufs)

    def take(self):
        for _ in self.bufs:
            self.k = (self.k + 1) % len(self.bufs)
            if not self.held[self.k]:
                break
        assert not self.held[self.k]
        self.held[self.k] = True
        return self.k, self.bufs[self.k], list(self.rel[self.k])

    def free(self, k, *toks):
        self.rel[k] = list(toks)
        self.held[k] = False


def program(nc, wstream, xT, memT, pos, const, param, out):
    sizes = chunk_sizes()
    offs = [0]
    for s in sizes:
        offs.append(offs[-1] + 128 * s)

    ctx = ExitStack()
    with ctx:
        def sem(name):
            return ctx.enter_context(nc.semaphore(name))

        def sb(name, shape, dt=F32, at=None):
            return (at or ctx).enter_context(nc.sbuf_tensor(name, shape, dt))

        pe = Queue(sem("s_pe"))
        dve = Queue(sem("s_dve"))
        act = Queue(sem("s_act"))
        pool = Queue(sem("s_pool"))
        sync = Queue(sem("s_sync"))

        h = sb("h", [128, KT, L])
        xh = sb("xh", [128, KT, L], F32R)
        xl = sb("xl", [128, KT, L], F32R)
        NRAW, NW = 2, 2
        raw = [sb(f"raw{i}", [128, CW]) for i in range(NRAW)]
        wh = [sb(f"wh{i}", [128, CW], F32R) for i in range(NW)]
        wl = [sb(f"wl{i}", [128, CW], F32R) for i in range(NW)]
        cst = sb("cst", [128, NC1])
        cst2 = [None]
        par = sb("par", [128, NPARAM])
        small = sb("small", [128, 256])
        PS = [ctx.enter_context(nc.psum_tensor(f"ps{i}", [128, 1024], F32)) for i in range(4)]
        psum = Ring(PS)

        def C(name, a=None, b=None):
            lo, hi = CONST[name]
            if lo >= NC1:
                return cst2[0][:, lo - NC1:hi - NC1] if a is None else cst2[0][:, lo - NC1 + a:lo - NC1 + b]
            return cst[:, lo:hi] if a is None else cst[:, lo + a:lo + b]

        def P_(name, a=None, b=None):
            lo, hi = PARAM[name]
            return par[:, lo:hi] if a is None else par[:, lo + a:lo + b]

        def load(name, dst, src, *waits):
            s = sem(name)
            sync(lambda e: e.dma_start(dst, src).then_inc(s, 16), *waits, alone=False, signal=False)
            return (s, 16)

        t_par = load("d_par", par[:, :], param)
        t_x = load("d_x", h[:, :, :], xT)
        t_cst = load("d_cst", cst[:, :], const[:, 0:NC1])

        rawsem = [sem(f"d_raw{i}") for i in range(NRAW)]
        rawfree = [[] for _ in range(NRAW)]
        wfree = [[] for _ in range(NW)]
        loaded, parts = {}, {}
        at = {"load": 0, "split": 0, "use": 0}

        def load_chunk():
            c = at["load"]
            if c >= len(sizes):
                return
            at["load"] += 1
            r = c % NRAW
            src = wstream[offs[c]:offs[c + 1]].rearrange("(p n) -> p n", p=128)
            sync(lambda e: e.dma_start(raw[r][:, 0:sizes[c]], src).then_inc(rawsem[r], 16),
                 rawfree[r], alone=False, signal=False)
            loaded[c] = (rawsem[r], 16 * (c // NRAW + 1))

        def split_chunk():
            c = at["split"]
            if c >= len(sizes):
                return
            at["split"] += 1
            while at["load"] <= c:
                load_chunk()
            r, w, n = c % NRAW, c % NW, sizes[c]
            a = act(lambda e: e.activation(wh[w][:, 0:n], raw[r][:, 0:n], ACT.Copy),
                    loaded[c], wfree[w], alone=False)
            b = pool(lambda e: e.tensor_tensor(wl[w][:, 0:n], raw[r][:, 0:n],
                                               wh[w][:, 0:n].bitcast(F32), ALU.subtract),
                     a, wfree[w], alone=False)
            rawfree[r] = [a, b]
            parts[c] = (w, a, b)
            while at["load"] < min(len(sizes), c + 1 + NRAW):
                load_chunk()

        def chunk():
            c = at["use"]
            at["use"] += 1
            while at["split"] <= c:
                split_chunk()
            w, a, b = parts[c]
            return c, wh[w], wl[w], [a, b]

        def chunk_done(c, tok):
            wfree[c % NW] = [tok]
            split_chunk()

        def mm(out_, lhsT, rhs, start, stop, *waits, signal=False, onto=False):
            return pe(lambda e: e.matmul(out_, lhsT, rhs, start=start, stop=stop, skip_group_check=onto), *waits,
                      alone=False, signal=signal)

        def mm3(out_, ws, xs, start, stop, *waits, signal=False):
            mm(out_, ws[0], xs[0], start, False, *waits)
            mm(out_, ws[0], xs[1], False, False)
            return mm(out_, ws[1], xs[0], False, stop, signal=signal)

        def tr(out_, in_, *waits, signal=False):
            k = in_.shape[0]
            return pe(lambda e: e.transpose(out_, in_, C("ident")[0:k, 0:k]), *waits,
                      alone=False, signal=signal)

        def copy_act(dst, src, *waits, scale=1.0, func=ACT.Copy, alone=True, **kw):
            return act(lambda e: e.activation(dst, src, func, scale=scale, **kw), *waits, alone=alone)

        def tt(q, dst, a, b, op, *waits, alone=True):
            return q(lambda e: e.tensor_tensor(dst, a, b, op), *waits, alone=alone)

        def stt(dst, a, s, b, op0, op1, *waits, alone=True):
            return dve(lambda e: e.scalar_tensor_tensor(dst, a, s, b, op0, op1), *waits, alone=alone)

        def ts(dst, a, s1, s2, op0, op1=ALU.bypass, *waits, q=None, alone=True):
            return (q or dve)(lambda e: e.tensor_scalar(dst, a, s1, s2, op0, op1), *waits, alone=alone)

        def vcopy(dst, src, *waits, alone=True):
            return dve(lambda e: e.tensor_copy(dst, src), *waits, alone=alone)

        def fill(dst, v, *waits, q=None, alone=True):
            return (q or dve)(lambda e: e.memset(dst, v), *waits, alone=alone)

        def reduce(dst, src, op, *waits, alone=True, **kw):
            return dve(lambda e: e.tensor_reduce(dst, src, AX.X, op, **kw), *waits, alone=alone)

        def recip(dst, src, *waits, alone=True):
            return dve(lambda e: e.reciprocal(dst, src), *waits, alone=alone)

        def scan(dst, ones, src, *waits):
            return dve(lambda e: e.tensor_tensor_scan(dst, ones, src, 0.0, ALU.mult, ALU.subtract), *waits)

        def table(name):
            return act(lambda e: e.preload_act_table_set(name), signal=False)

        fence = [None]

        def phase():
            fence[0] = [pe.last(), dve.last(), act.last(), pool.last()]
            return fence[0]

        z = []
        for p in PS:
            z.append(fill(p[:, :], 0.0, alone=False))
        for k in range(4):
            psum.free(k, z[k])
        table(LN_EXP)

        scratch = sb("scratch", [128, 4, L])
        s_free = [[] for _ in range(4)]
        rst = sb("rst", [128, L])
        rst_free = [None]

        def rstd_of(src, c0, n, waits, halves):
            acc, sq = scratch[:, 2, 0:n], scratch[:, 0:2, 0:n]
            t_acc = None
            free = [None, None]
            for k in range(KT):
                dst = acc if k == 0 else sq[:, k % 2, :]
                t = copy_act(dst, src[:, k, c0:c0 + n], waits, s_free[2] if k == 0 else [free[k % 2], s_free[k % 2]],
                             func=ACT.Square, alone=False)
                if k:
                    t = tt(dve, acc, acc, dst, ALU.add, t, t_acc)
                    free[k % 2] = t
                t_acc = t
            k, ps, w = psum.take()
            o = ps[:, :].rearrange("p (a b) -> p a b", a=2)[:, 0:halves, 0:n // halves]
            for i in range(halves):
                t = mm(o[:, i, :], C("mean"), acc[:, i * (n // halves):(i + 1) * (n // halves)],
                       True, True, w, t_acc, t_cst, signal=True)
            s_free[0] = [free[0]]
            s_free[1] = [free[1]]
            s_free[2] = [t]
            r = rst[:, 0:n]
            t = copy_act(r.rearrange("p (a b) -> p a b", a=halves), o, t, rst_free[0], func=ACT.Ln, bias=1e-6)
            psum.free(k, t)
            return r, copy_act(r, r, t, func=ACT.Exp, scale=-0.5)

        tmpn = sb("tmpn", [128, 2, L])
        tmp_free = [None, None]

        def split(dst_h, dst_l, src, *waits):
            a = copy_act(dst_h, src, *waits, alone=False)
            b = tt(pool, dst_l, src, dst_h.bitcast(F32), ALU.subtract, a, *waits, alone=False)
            return a, b

        def norm(gain, src, c0, n, halves, dst_h, dst_l, *waits):
            r, t_r = rstd_of(src, c0, n, list(waits), halves)
            toks = []
            t = None
            for k in range(KT):
                u = tmpn[:, k % 2, 0:n]
                t = stt(u, src[:, k, c0:c0 + n], P_(gain, k, k + 1), r, ALU.mult, ALU.mult,
                        t_r, tmp_free[k % 2], t_par, *waits, alone=False)
                a, b = split(dst_h[:, k, c0:c0 + n], dst_l[:, k, c0:c0 + n], u, t, *waits)
                tmp_free[k % 2] = [a, b]
                toks.append([a, b])
            rst_free[0] = t
            return toks

        def tile_feature(wt, xt, x_toks, n, c0, tw, nk=KT, cols=None):
            k_, ps, w = psum.take()
            halves = 2 if n > 512 else 1
            m = n // halves
            o = ps[:, :].rearrange("p (a b) -> p a b", a=2)[:, 0:halves, 0:m]
            tok = None
            for i in range(halves):
                for k in range(nk):
                    a, b = c0 + i * m, c0 + (i + 1) * m
                    tok = mm3(o[:, i, :], (wt(0, k), wt(1, k)), (xt[0][:, k, a:b], xt[1][:, k, a:b]),
                              k == 0, k == nk - 1, w, tw, x_toks[k], signal=(k == nk - 1))
            return k_, o, tok

        def feature(x_toks, n, c0, evac, xt=None):
            c, hh, ll, tw = chunk()

            def wt(part, k):
                return (hh, ll)[part][:, 128 * k:128 * k + 128]
            k_, o, tok = tile_feature(wt, xt or (xh, xl), x_toks, n, c0, tw)
            chunk_done(c, tok)
            evac(k_, o, tok)

        def token_tiles(x_toks, starts, ncols, evac, xt=None):
            xt = xt or (xh, xl)
            slots = [psum.take() for _ in range((len(starts) + 1) // 2)]
            toks = []
            for half in range(2):
                c, hh, ll, tw = chunk()
                for i, a in enumerate(starts):
                    k_, ps, w = slots[i // 2]
                    o = ps[:, 512 * (i % 2):512 * (i % 2) + ncols]
                    for kk in range(4):
                        k = 4 * half + kk
                        tok = mm3(o, (xt[0][:, k, a:a + 128], xt[1][:, k, a:a + 128]),
                                  (hh[:, ncols * kk:ncols * (kk + 1)], ll[:, ncols * kk:ncols * (kk + 1)]),
                                  k == 0, k == KT - 1, w, tw, x_toks[k], signal=(kk == 3))
                    toks.append(tok)
                chunk_done(c, tok)
            for i in range(len(starts)):
                k_, ps, w = slots[i // 2]
                t = evac(i, ps[:, 512 * (i % 2):512 * (i % 2) + ncols], toks[len(starts) + i])
                if i % 2:
                    psum.free(k_, prev, t)
                elif i == len(starts) - 1:
                    psum.free(k_, t)
                prev = t

        xb = sb("xb", [128, 2, L])
        xb_free = [None, None]
        xb_k = [0]
        t1b = scratch

        def rope(src, t_src, n, cos, sin, dsts, *waits):
            i = xb_k[0]
            k_, ps, w = psum.take()
            halves = 2 if n > 512 else 1
            m = n // halves
            o = ps[:, :].rearrange("p (a b) -> p a b", a=2)[:, 0:halves, 0:m]
            for j in range(halves):
                t = mm(o[:, j, :], C("rot"), src[:, j * m:(j + 1) * m], True, True, w, t_src, signal=True)
            a = tt(dve, t1b[:, 0, 0:n], src, cos, ALU.mult, t_src, *waits)
            v = t1b[:, 1, 0:n]
            b = tt(dve, v.rearrange("p (a b) -> p a b", a=halves), o,
                   sin.rearrange("p (a b) -> p a b", a=halves), ALU.mult, t)
            psum.free(k_, b)
            for (p0, p1), dst in dsts:
                c = tt(dve, dst, t1b[p0:p1, 0, 0:n], t1b[p0:p1, 1, 0:n], ALU.add)
            return a, t, c

        def three(ap, n, halves):
            return ap.rearrange("p (a b) -> p a b", a=halves)

        NP, NT = 4, 2
        Pfree = [[] for _ in range(NP)]
        Pk = [0]
        nm = sb("nm", [128, 8])
        nmk = [0]
        nm_free = [None] * 8
        rs = sb("rs", [128, 2, 8])
        rr = sb("rr", [128, 2, 8])
        osb, fin = tmpn, xb
        fin_free, osb_free = xb_free, tmp_free
        flip = [0]
        bufs = {}

        def attention_buffers(name, scope, start):
            bufs["P"] = sb("Pb" + name, [128, NP, L], at=scope)
            bufs["T"] = Ring([sb(f"PT{name}{i}", [128, 640], at=scope) for i in range(NT)])
            for k in range(NP):
                Pfree[k] = list(start)
            for k in range(NT):
                bufs["T"].free(k, *start)

        def scores(q_lhsT, k_rhs, nkeys, meta, extra, mask, t_in):
            k_, ps, w = psum.take()
            o0 = 112 if meta else 0
            n = nkeys
            first = min(n, 512 - o0)
            spans = [(0, first)] + ([(first, n)] if n > first else [])
            for a, b in spans:
                o = ps[:, o0 + a:o0 + b]
                lastpart = b == n
                terms = [(q_lhsT, k_rhs(a, b), o)]
                if extra is not None:
                    terms.append((extra[0], extra[1](a, b), o))
                if mask is not None and lastpart:
                    mw = mask.shape[1]
                    terms.append((C("ident"), mask, ps[:, o0 + n - mw:o0 + n]))
                for i, (l_, r_, o_) in enumerate(terms):
                    t = mm(o_, l_, r_, i == 0, i == len(terms) - 1, w, t_in, t_cst,
                           signal=(lastpart and i == len(terms) - 1))
            return k_, ps[:, o0:o0 + n], t

        def softmax_exp(k_, S, t, rs_ap):
            c = nmk[0]
            nmk[0] = (c + 1) % 8
            m = reduce(nm[:, c:c + 1], S, ALU.max, t, nm_free[c], alone=False, negate=True)
            p = Pk[0]
            Pk[0] = (p + 1) % NP
            n = S.shape[1]
            a = copy_act(bufs["P"][:, p, 0:n], S, m, Pfree[p], func=ACT.Exp, bias=nm[:, c:c + 1], accum_out=rs_ap,
                         alone=False)
            nm_free[c] = a
            psum.free(k_, a)
            return p, a

        def flipP(p, t, cols, nq=128, k=None):
            k_, ps, w = psum.take()
            for j, (a, b) in enumerate(cols):
                t2 = tr(ps[0:b - a, 128 * j:128 * j + nq], bufs["P"][0:nq, p, a:b], w, t, t_cst,
                        signal=(j == len(cols) - 1))
            Pfree[p] = [t2]
            i, buf, w2 = bufs["T"].take()
            n = 128 * len(cols)
            q = dve if i % 2 else act
            if q is dve:
                t3 = vcopy(buf[:, 0:n], ps[:, 0:n], t2, w2, alone=False)
            else:
                t3 = copy_act(buf[:, 0:n], ps[:, 0:n], t2, w2, alone=False)
            psum.free(k_, t3)
            return i, buf, t3

        def finish_tile(o_ap, t_o, nq, scale_bc, square_w, ntile, dst_t0, col0, gate, gain, *waits):
            f = flip[0]
            flip[0] ^= 1
            w_ = 128 * ntile
            d = osb[0:nq, f, 0:w_]
            if scale_bc is not None:
                nh, hd = scale_bc
                t = tt(dve, d.rearrange("p (a b) -> p a b", a=nh[1]), o_ap.rearrange("p (a b) -> p a b", a=nh[1]),
                       hd, ALU.mult, t_o, osb_free[f])
            elif square_w:
                t = vcopy(d, o_ap, t_o, osb_free[f])
            else:
                d, t = o_ap, t_o
            k_, ps, w = psum.take()
            for j in range(ntile):
                t2 = tr(ps[:, 128 * j:128 * j + nq], d[:, 128 * j:128 * j + 128], w, t, signal=(j == ntile - 1))
            osb_free[f] = [t2] if d is not o_ap else osb_free[f]
            src = ps[:, 0:w_].rearrange("p (a b) -> p a b", a=ntile)[:, :, 0:nq]
            g = fin[:, f, 0:ntile * nq].rearrange("p (a b) -> p a b", a=ntile)
            if gate is None:
                t3 = vcopy(g, src, t2, fin_free[f])
            elif gain is None:
                t3 = tt(dve, g, src, gate, ALU.mult, t2, fin_free[f], *waits)
            else:
                for j in range(ntile):
                    t3 = stt(g[:, j, :], src[:, j, :], gain, gate[:, j, :], ALU.mult, ALU.mult, t2, fin_free[f], *waits,
                             alone=(j == 0))
            psum.free(k_, t3)
            a, b = split(xh[:, dst_t0:dst_t0 + ntile, col0:col0 + nq], xl[:, dst_t0:dst_t0 + ntile, col0:col0 + nq],
                         g, t3, *waits)
            fin_free[f] = [a, b]
            return [a, b], t

        lam_init = [0.8 - 0.6 * math.exp(-0.3 * l) for l in range(2)]
        neglam = [None, None]
        t_lam = None
        fill(small[:, 0:64], 0.0)
        t_small = dve.last()
        for l in range(2):
            b = 8 * l
            tt(dve, small[0:64, b:b + 1], P_(f"lam{l}", 0, 1)[0:64], P_(f"lam{l}", 1, 2)[0:64], ALU.mult, t_par)
            t = tt(dve, small[64:128, b + 1:b + 2], P_(f"lam{l}", 0, 1)[64:128], P_(f"lam{l}", 1, 2)[64:128], ALU.mult)
            k_, ps, w = psum.take()
            t = mm(ps[:, 0:2], C("mean"), small[:, b:b + 2], True, True, w, t, t_cst, signal=True)
            t = copy_act(small[:, b + 2:b + 4], ps[:, 0:2], t, scale=1024.0, func=ACT.Exp)
            psum.free(k_, t)
            t = tt(dve, small[:, b + 4:b + 5], small[:, b + 3:b + 4], small[:, b + 2:b + 3], ALU.subtract, t)
            t_lam = ts(small[:, b + 5:b + 6], small[:, b + 4:b + 5], -lam_init[l], None, ALU.add)
            ts(small[:, b + 6:b + 7], P_(f"g_sub{l}"), 1.0 - lam_init[l], None, ALU.mult)
            neglam[l] = small[:, b + 5:b + 6]
        gsub = [small[:, 6:7], small[:, 14:15]]
        gq8, gmq8 = small[:, 16:17], small[:, 17:18]
        ts(gq8, P_("g_q"), 0.125, None, ALU.mult)
        t_prep = ts(gmq8, P_("g_mq"), 0.125, None, ALU.mult)

        one = ExitStack()
        attention_buffers("1", one, [])
        QA = sb("QA", [128, 8, L], at=one)
        QB = sb("QB", [128, 8, L], at=one)
        KA = sb("KA", [128, 4, L], at=one)
        KB = sb("KB", [128, 4, L], at=one)
        VA = sb("VA", [128, 5, T], at=one)
        VB = sb("VB", [128, 5, T], at=one)
        G = sb("G", [128, 8, L], at=one)
        NCm = sb("NCm", [128, L], at=one)
        LF = sb("LF", [128, 3, 40], at=one)
        onesr = bufs["P"][0:8, 0, :]
        fill(QA[:, :, :], 0.0)
        fill(QB[:, :, :], 0.0)
        fill(NCm[:, :], 0.0)
        fill(LF[:, :, :], 0.0)
        t_b1 = dve.last()

        def q_dsts(Q, tile, cols):
            return [((0, 64), Q[0:64, 2 * tile, cols[0]:cols[1]]), ((64, 128), Q[64:128, 2 * tile + 1, cols[0]:cols[1]])]

        starts = [0] + [M + 128 * i for i in range(4)]

        def evac_copy(dst, src, k_, tok, *waits, scale=1.0, q=None):
            t = copy_act(dst, src, tok, *waits, scale=scale, alone=False) if q is None else \
                vcopy(dst, src, tok, *waits, alone=False)
            psum.free(k_, t)
            return t

        for l in range(2):
            full = l == 0
            n_q, c_q = (L, 0) if full else (T, M)
            ph = phase()
            x_toks = norm(f"g_norm{l}", h, 0, L, 2, xh, xl, t_x, ph)
            halves_q = 2 if full else 1

            def roped(dsts, cos_cols, n, scale):
                def evac(k_, o, tok):
                    i = xb_k[0]
                    xb_k[0] ^= 1
                    x_ = xb[:, i, 0:n]
                    hv = 2 if n > 512 else 1
                    t = copy_act(three(x_, n, hv), o, tok, xb_free[i], scale=scale, alone=False)
                    psum.free(k_, t)
                    a, b, c = rope(x_, t, n, C("cos", *cos_cols), C("sin", *cos_cols), dsts, ph, t_cst)
                    xb_free[i] = [a, b]
                return evac

            cols = (c_q, c_q + n_q)
            for c in range(4):
                feature(x_toks, n_q, c_q, roped(q_dsts(QA, c, cols), cols, n_q, 0.125))
            for c in range(4):
                feature(x_toks, L, 0, roped([((0, 128), KA[:, c, :])], (0, L), L, 1.0))

            def v_evac(V, c):
                def evac(i, ps, tok):
                    rows = 16 if i == 0 else 128
                    dst, src = V[0:rows, i, 256 * c:256 * c + 256], ps[0:rows, 0:256]
                    if i % 2:
                        return copy_act(dst, src, tok, ph, alone=False)
                    return vcopy(dst, src, tok, ph, alone=False)
                return evac
            for c in range(2):
                token_tiles(x_toks, starts, 256, v_evac(VA, c))

            def fq_evac(c):
                def evac(k_, o, tok):
                    for j, ((p0, p1), dst) in enumerate(q_dsts(QB, c, cols)):
                        t = copy_act(three(dst, n_q, halves_q), o[p0:p1, :, :], tok, ph, t_b1, scale=0.125, alone=False)
                    psum.free(k_, t)
                return evac

            def fk_evac(c):
                def evac(k_, o, tok):
                    evac_copy(three(KB[:, c, :], L, 2), o, k_, tok, ph, q=dve)
                return evac
            for c in range(4):
                feature(x_toks, n_q, c_q, fq_evac(c))
            for c in range(4):
                feature(x_toks, L, 0, fk_evac(c))
            token_tiles(x_toks, starts, 256, v_evac(VB, 0))

            def last_v(i, ps, tok):
                rows = 16 if i == 0 else 128
                t = vcopy(VB[0:rows, i, 256:512], ps[0:rows, 0:256], tok, ph, alone=False)
                t2 = tt(dve, LF[0:rows, 0, 8 * i:8 * i + 8], ps[0:rows, 256:264], P_(f"fb{l}")[0:rows], ALU.add,
                        tok, ph, t_par)
                return [t, t2]
            token_tiles(x_toks, starts, 264, last_v)
            z_, a_, b_ = LF[:, 0, :], LF[:, 1, :], LF[:, 2, :]
            t = stt(a_, z_, -1.0, z_, ALU.mult, ALU.max)
            t = copy_act(a_, a_, t, func=ACT.Exp, scale=-1.0)
            t = copy_act(a_, a_, t, func=ACT.Ln, bias=1.0)
            t = stt(b_, z_, 0.0, a_, ALU.min, ALU.subtract, t)
            k_, ps, w = psum.take()
            tr(ps[0:8, 112:128], LF[0:16, 2, 0:8], w, t, t_cst)
            for i in range(4):
                t = tr(ps[0:8, 128 * (i + 1):128 * (i + 2)], LF[:, 2, 8 * i + 8:8 * i + 16], signal=(i == 3))
            fill(onesr, 1.0, Pfree[0])
            t_nc = scan(NCm[0:8, :], onesr, ps[0:8, 112:640], t)
            psum.free(k_, t_nc)
            Pfree[0] = [t_nc]

            def gate_evac(c):
                def evac(k_, o, tok):
                    t = copy_act(three(G[:, c, cols[0]:cols[1]], n_q, halves_q), o, tok, ph,
                                 func=ACT.Silu, alone=False)
                    psum.free(k_, t)
                return evac
            for c in range(8):
                feature(x_toks, n_q, c_q, gate_evac(c))
            table(LN_EXP)
            att = phase()
            ao = []

            for kind in ("diff", "fox"):
                Q, K, V = (QA, KA, VA) if kind == "diff" else (QB, KB, VB)
                nh, hd, t0 = (4, 128, 0) if kind == "diff" else (8, 64, 4)
                tiles = ([-1] if full else []) + [0, 1, 2, 3]
                for i in tiles:
                    par_ = (i + 1) % 2
                    nq = 16 if i < 0 else 128
                    c0 = 0 if i < 0 else M + 128 * i
                    ok, ops, ow = psum.take()
                    O = ops[0:nq, 0:512]
                    if i < 0:
                        sk, sps, sw = psum.take()
                        for m in range(8):
                            o = sps[0:16, 16 * m:16 * m + 16]
                            if kind == "diff":
                                t = mm(o, Q[:, m, 0:16], K[:, m // 2, 0:16], True, True, sw, att, signal=m == 7)
                            else:
                                mm(o, Q[:, m, 0:16], K[:, m // 2, 0:16], True, False, sw, att)
                                mm(o, C("ident", m, m + 1).to_broadcast([128, 16]), NCm[:, 0:16], False, False)
                                t = mm(o, C("ident", 0, 16), C("causal", 0, 16), False, True, signal=m == 7)
                        S3 = sps[0:16, 0:128].rearrange("p (a b) -> p a b", a=8)
                        p = Pk[0]
                        Pk[0] = (p + 1) % NP
                        Pv = bufs["P"][0:16, p, 0:128]
                        P3 = Pv.rearrange("p (a b) -> p a b", a=8)
                        mx = small[0:16, 32:40]
                        t = reduce(mx, S3, ALU.max, t)
                        t = tt(dve, P3, S3, mx.unsqueeze(2).to_broadcast([16, 8, 16]), ALU.subtract, t, Pfree[p])
                        psum.free(sk, t)
                        t = copy_act(Pv, Pv, t, func=ACT.Exp)
                        t = reduce(mx, P3, ALU.add, t)
                        t = recip(mx, mx)
                        t = tt(dve, P3, P3, mx.unsqueeze(2).to_broadcast([16, 8, 16]), ALU.mult)
                        if kind == "diff":
                            P4 = Pv.rearrange("p (a m b) -> p a m b", a=4, m=2)
                            t = stt(P4[:, :, 0, :], P4[:, :, 1, :], neglam[l][0:16], P4[:, :, 0, :], ALU.mult, ALU.add, t_lam)
                        tk, tps, tw = psum.take()
                        for hh in range(nh):
                            a = 16 * (2 * hh if kind == "diff" else hh)
                            t2 = tr(tps[0:16, 16 * hh:16 * hh + 16], bufs["P"][0:16, p, a:a + 16], tw, t, signal=hh == nh - 1)
                        Pfree[p] = [t2]
                        pi, buf, w2 = bufs["T"].take()
                        t3 = vcopy(buf[0:16, 0:16 * nh], tps[0:16, 0:16 * nh], t2, w2)
                        psum.free(tk, t3)
                        for hh in range(nh):
                            t_pv = mm(ops[0:16, hd * hh:hd * hh + hd], buf[0:16, 16 * hh:16 * hh + 16],
                                      V[0:16, 0, hd * hh:hd * hh + hd], True, True, ow, t3, signal=True)
                        bufs["T"].free(pi, t_pv)
                        r_ap = None
                    else:
                        n = M + 128 * (i + 1)
                        blocks = [(0, M)] + [(M + 128 * j, M + 128 * j + 128) for j in range(i + 1)]
                        maps = 8

                        def score(m):
                            ex = None
                            if kind == "fox":
                                ex = (C("ident", m, m + 1).to_broadcast([128, 128]), lambda a, b: NCm[:, a:b])
                            return scores(Q[:, m, c0:c0 + 128], lambda a, b: K[:, m // 2, a:b], n, True, ex,
                                          C("causal") if kind == "fox" else C("chunk", 64, 128), [att, t_nc])

                        def head_out(hh, p, t):
                            pi, buf, t3 = flipP(p, t, blocks)
                            tv = None
                            for j, (a, b) in enumerate(blocks):
                                tv = mm(ops[:, hd * hh:hd * hh + hd], buf[0:b - a, 128 * j:128 * j + 128],
                                        V[0:b - a, j, hd * hh:hd * hh + hd], j == 0, j == len(blocks) - 1,
                                        ow, t3, signal=(j == len(blocks) - 1))
                            bufs["T"].free(pi, tv)
                            return tv

                        pend = [score(0), score(1)]
                        waiting = []
                        pair = []
                        for m in range(8):
                            k_, S, t = pend.pop(0)
                            p, t = softmax_exp(k_, S, t, rs[:, par_, m:m + 1])
                            if m + 2 < 8 and kind == "fox":
                                pass
                            pair.append((p, t))
                            if kind == "diff":
                                if m % 2:
                                    (p0, ta), (p1, tb) = pair
                                    pair = []
                                    q0, q1 = rr[:, par_, m - 1:m], rr[:, par_, m:m + 1]
                                    t = recip(rr[:, par_, m - 1:m + 1], rs[:, par_, m - 1:m + 1], ta, tb)
                                    t = tt(dve, q1, q1, neglam[l], ALU.mult, t_lam)
                                    t = ts(bufs["P"][:, p1, 0:n], bufs["P"][:, p1, 0:n], q1, None, ALU.mult)
                                    t = stt(bufs["P"][:, p0, 0:n], bufs["P"][:, p0, 0:n], q0, bufs["P"][:, p1, 0:n], ALU.mult, ALU.add)
                                    Pfree[p1] = [t]
                                    waiting.append((m // 2, p0, t))
                            else:
                                waiting.append((m, p, t))
                                pair = []
                            if m + 2 < 8:
                                pend.append(score(m + 2))
                            if len(waiting) > 1 or (kind == "diff" and m % 2 and len(waiting) > 1):
                                t_pv = head_out(*waiting.pop(0))
                        while waiting:
                            t_pv = head_out(*waiting.pop(0))
                    if kind == "diff":
                        f = flip[0]
                        sq = osb[0:nq, f, 0:512]
                        ms = small[0:nq, 48:52]
                        t = copy_act(sq, O, t_pv, osb_free[f], func=ACT.Square)
                        t = reduce(ms, sq.rearrange("p (a b) -> p a b", a=4), ALU.add, t)
                        t = copy_act(ms, ms, t, func=ACT.Ln, scale=1.0 / 128, bias=1e-5)
                        t = copy_act(ms, ms, t, func=ACT.Exp, scale=-0.5)
                        toks, t_used = finish_tile(O, t, nq, ((0, 4), ms.unsqueeze(2).to_broadcast([nq, 4, 128])), None,
                                                   4, 0, c0, G[:, 0:4, c0:c0 + nq], gsub[l], att)
                    elif i < 0:
                        toks, t_used = finish_tile(O, t_pv, nq, None, True, 4, 4, c0,
                                                   G[:, 4:8, c0:c0 + nq], None, att)
                    else:
                        t = recip(rr[:, par_, 0:8], rs[:, par_, 0:8], t_pv)
                        toks, t_used = finish_tile(O, t_pv, nq,
                                                   ((0, 8), rr[:, par_, 0:8].unsqueeze(2).to_broadcast([128, 8, 64])),
                                                   None, 4, 4, c0, G[:, 4:8, c0:c0 + nq], None, att)
                    psum.free(ok, t_used)
                    ao.append(toks)

            def res_evac(c, scale=None):
                def evac(k_, o, tok):
                    hv = o.shape[1]
                    dst = three(h[:, c, cols[0]:cols[1]], n_q, hv)
                    t = tt(dve, dst, dst, o, ALU.add, tok, alone=False)
                    psum.free(k_, t)
                return evac
            for c in range(8):
                feature([ao] * KT, n_q, c_q, res_evac(c))
        one.close()

        ph = phase()
        r, t_r = rstd_of(h, M, T, [ph], 1)
        for k in range(KT):
            t = stt(h[:, k, M:L], h[:, k, M:L], P_("g_final", k, k + 1), r, ALU.mult, ALU.mult, t_r, alone=False)
        rst_free[0] = t

        def ffn(gain, ph):
            st = ExitStack()
            aH = sb(gain + "aH", [128, FT, T], F32R, at=st)
            aL = sb(gain + "aL", [128, FT, T], F32R, at=st)
            x_toks = norm(gain, h, M, T, 1, xh, xl, ph)
            act_toks = []
            for f in range(FT):
                k_, ps, w = psum.take()
                for s in range(2):
                    c, hh, ll, tw = chunk()
                    for k in range(KT):
                        a = 128 * k
                        t = mm3(ps[:, 512 * s:512 * s + 512], (hh[:, a:a + 128], ll[:, a:a + 128]),
                                (xh[:, k, M:L], xl[:, k, M:L]), k == 0, k == KT - 1, w, tw, x_toks[k],
                                signal=(k == KT - 1))
                    chunk_done(c, t)
                    if s == 0:
                        tg = t
                i = f % 2
                a = copy_act(xb[:, i, 0:T], ps[:, 0:512], tg, xb_free[i], func=ACT.Silu, alone=False)
                b = tt(dve, tmpn[:, i, 0:T], xb[:, i, 0:T], ps[:, 512:1024], ALU.mult, a, t, tmp_free[i], alone=False)
                psum.free(k_, b)
                xb_free[i] = b
                p, q = split(aH[:, f, :], aL[:, f, :], tmpn[:, i, 0:T], b, ph)
                tmp_free[i] = [p, q]
                act_toks.append([p, q])
            for m in range(KT):
                k_, ps, w = psum.take()
                for f0, nf in ((0, 8), (8, 8), (16, 6)):
                    c, hh, ll, tw = chunk()
                    for kk in range(nf):
                        f = f0 + kk
                        t = mm3(ps[:, 0:512], (hh[:, 128 * kk:128 * kk + 128], ll[:, 128 * kk:128 * kk + 128]),
                                (aH[:, f, :], aL[:, f, :]), f == 0, f == FT - 1, w, tw, act_toks[f], signal=(kk == nf - 1))
                    chunk_done(c, t)
                t = stt(h[:, m, M:L], ps[:, 0:512], 0.5, h[:, m, M:L], ALU.mult, ALU.add, t, alone=False)
                psum.free(k_, t)
            st.close()

        ffn("g_ffn1", phase())

        two = ExitStack()
        cst2[0] = sb("cst2", [128, NCONST - NC1], at=two)
        QS = sb("QS", [128, 8, T], at=two)
        KS = sb("KS", [128, 4, T], at=two)
        VSB = sb("VSB", [128, 4, 4, 4, 64], at=two)
        nsa = ExitStack()
        QN = sb("QN", [128, 8, T], at=nsa)
        KSW = sb("KSW", [128, 2, T], at=nsa)
        VSW = sb("VSW", [128, 4, 256], at=nsa)
        Gt = sb("Gt", [128, 4, 24], at=nsa)
        cs = sb("cs", [128, 2, T], at=nsa)
        KC = sb("KC", [128, 32], at=nsa)
        VC = sb("VC", [128, 8, 64], at=nsa)
        OA = sb("OA", [128, 2, 512], at=nsa)
        cmp_ = ExitStack()
        X2 = sb("X2", [128, 2, T], at=cmp_)
        YH = sb("YH", [128, 2, 66, 8], F32R, at=cmp_)
        YL = sb("YL", [128, 2, 66, 8], F32R, at=cmp_)
        hid = sb("hid", [128, 2, 2, 64], at=cmp_)
        posi = sb("posi", [128, T], I32, at=cmp_)
        ph = phase()
        t_c2 = load("d_cst2", cst2[0][:, :], const[:, NC1:NCONST], ph)
        t_pos = load("d_pos", posi[:, :], pos.partition_broadcast(128), ph)
        ang, kk_, mm_ = scratch[:, 0, 0:T], scratch[:, 1, 0:T], scratch[:, 2, 0:T]
        t = vcopy(ang, posi[:, :], t_pos, ph)
        ts(ang, ang, C("freq"), None, ALU.mult, ALU.bypass)
        two_pi = 2.0 * math.pi
        MAGIC = 12582912.0

        def pieces(v, unit):
            res, rest = [], v
            for j in range(3):
                step = 2.0 ** (math.floor(math.log2(abs(v))) - 7 - 8 * j)
                q = math.floor(rest / step) * step
                if q:
                    res.append(q)
                rest -= q
            res.append(float(np.float32(rest)))
            return res

        for unit in (4096.0, 1.0):
            ts(kk_, ang, float(np.float32(1.0 / (two_pi * unit))), MAGIC, ALU.mult, ALU.add)
            ts(kk_, kk_, -MAGIC, None, ALU.add, ALU.bypass)
            for v in pieces(two_pi * unit, unit):
                stt(ang, kk_, -v, ang, ALU.mult, ALU.add)
        t = ts(ang, ang, math.pi, -math.pi, ALU.min, ALU.max)
        t1 = copy_act(cs[:, 1, :], ang, t, ph, func=ACT.Sin)
        t = stt(mm_, ang, -1.0, ang, ALU.mult, ALU.max)
        t = ts(mm_, mm_, -1.0, math.pi / 2, ALU.mult, ALU.add)
        t_cs = copy_act(cs[:, 0, :], mm_, t, ph, func=ACT.Sin)
        table(LN_EXP)
        cos2, sin2 = cs[:, 0, :], cs[:, 1, :]
        for k in range(3):
            s_free[k] = [t_cs, t]
        fill(QS[:, :, :], 0.0, ph)
        fill(QN[:, :, :], 0.0, ph)
        fill(VSB[:, :, :, :, :], 0.0)
        fill(VC[:, :, :], 0.0)
        t_z = dve.last()
        x_toks = norm("g_mix", h, M, T, 1, xh, xl, ph)

        def head_norm(src, sq_src, t_src, n, gain, dst, *waits):
            s = scratch[:, 3, 0:n]
            t = copy_act(s, src, t_src, s_free[3], func=ACT.Square)
            k_, ps, w = psum.take()
            t = mm(ps[:, 0:n], C("blk"), s, True, True, w, t, signal=True)
            t = copy_act(s, ps[:, 0:n], t, func=ACT.Ln, bias=1e-6)
            psum.free(k_, t)
            t = copy_act(s, s, t, func=ACT.Exp, scale=-0.5)
            t = stt(dst, src, gain, s, ALU.mult, ALU.mult, t, *waits)
            s_free[3] = [t]
            return t

        def normed_roped(gain, dsts, n=T, do_rope=True):
            def evac(k_, o, tok):
                i = xb_k[0]
                xb_k[0] ^= 1
                x_ = xb[:, i, 0:n]
                t = copy_act(x_, o[:, 0, :] if len(o.shape) == 3 else o, tok, xb_free[i], alone=False)
                psum.free(k_, t)
                if do_rope:
                    t = head_norm(x_, None, t, n, gain, x_)
                    a, b, c = rope(x_, t, n, cos2, sin2, dsts, ph, t_cs)
                    xb_free[i] = [a, b]
                else:
                    t = head_norm(x_, None, t, n, gain, x_)
                    for (p0, p1), dst in dsts:
                        t = vcopy(dst, xb[p0:p1, i, 0:n], ph)
                    xb_free[i] = [t]
            return evac

        for c in range(4):
            feature(x_toks, T, M, normed_roped(gq8, q_dsts(QN, c, (0, T))))
        for c in range(2):
            feature(x_toks, T, M, normed_roped(P_("g_ks") if c == 0 else P_("g_kw"), [((0, 128), KSW[:, c, :])]))

        def qs_evac(c):
            def evac(k_, o, tok):
                for (p0, p1), dst in q_dsts(QS, c, (0, T)):
                    t = copy_act(dst, o[p0:p1, 0, :], tok, ph, t_z, scale=0.125, alone=False)
                psum.free(k_, t)
            return evac

        def ks_evac(c):
            def evac(k_, o, tok):
                evac_copy(KS[:, c, :], o[:, 0, :], k_, tok, ph, q=dve)
            return evac
        for c in range(4):
            feature(x_toks, T, M, qs_evac(c))
        for c in range(4):
            feature(x_toks, T, M, ks_evac(c))
        starts2 = [M + 128 * i for i in range(4)]

        def vsw_evac(i, ps, tok):
            t = copy_act(VSW[:, i, :], ps[:, 0:256], tok, ph, alone=False)
            t2 = copy_act(Gt[:, i, :], ps[:, 256:280], tok, ph, func=ACT.Exp, scale=-1.0, alone=False)
            return [t, t2]
        token_tiles(x_toks, starts2, 280, vsw_evac)
        ts(Gt[:, :, :], Gt[:, :, :], 1.0, None, ALU.add, ALU.bypass, act.last())
        t_gt = recip(Gt[:, :, :], Gt[:, :, :])

        def vsb_evac(c):
            def evac(i, ps, tok):
                src = ps[:, 0:256].rearrange("p (a b d) -> p a b d", a=2, b=2)
                dst = VSB[:, i, 2 * c:2 * c + 2, 0:4:3, :]
                return vcopy(dst, src, tok, t_z, alone=False)
            return evac
        for c in range(2):
            token_tiles(x_toks, starts2, 256, vsb_evac(c))

        zz = fill(YH[:, :, 64:66, :].bitcast(F32), 0.0, ph, q=pool)
        zz = fill(YL[:, :, 64:66, :].bitcast(F32), 0.0, q=pool)
        x2_free, y_free = None, None
        for s in range(2):
            got = []
            feature(x_toks, T, M, lambda k_, o, tok: got.append((k_, o[:, 0, :], tok)))
            k_, src, tok = got[0]
            w = [tok, ph, x2_free]
            copy_act(X2[0:64, 0, :], src[0:64, :], *w)
            b = copy_act(X2[0:64, 1, :], src[64:128, :], *w)
            vcopy(X2[64:128, 0, 0:T - 1], src[0:64, 1:T], b, *w)
            d = vcopy(X2[64:128, 1, 0:T - 1], src[64:128, 1:T], b, *w)
            psum.free(k_, b, d)
            pe_ = P_("pe_k" if s == 0 else "pe_v")
            xin = X2[:, :, :].rearrange("p h (n j) -> p (h n) j", j=16)[:, :, 0:16:2]
            for v in range(2):
                u = tmpn[:, v, 0:512]
                t = tt(dve, u.rearrange("p (n j) -> p n j", j=8), xin,
                       pe_[:, 8 * v:8 * v + 8].unsqueeze(1).to_broadcast([128, 64, 8]), ALU.add, b, d, tmp_free[v])
                a, b_ = split(YH[:, v, 0:64, :].rearrange("p n j -> p (n j)"),
                              YL[:, v, 0:64, :].rearrange("p n j -> p (n j)"), u, t, y_free, ph)
                tmp_free[v] = [a, b_]
            x2_free = t
            ty = [a, b_, zz]
            k_, ps, w = psum.take()
            for v in range(2):
                for j0 in (0, 4):
                    c, hh, ll, tw = chunk()
                    for mt in range(2):
                        for jj in range(4):
                            j = j0 + jj
                            a0 = 256 * jj + 128 * mt
                            t = mm3(ps[:, 512 * mt:512 * mt + 64], (hh[:, a0:a0 + 128], ll[:, a0:a0 + 128]),
                                    (YH[:, v, v:v + 64, j], YL[:, v, v:v + 64, j]),
                                    v == 0 and j == 0, v == 1 and j == 7, w, tw, ty, signal=(jj == 3))
                    chunk_done(c, t)
            y_free = t
            t = copy_act(hid[:, s, :, :], ps[:, :].rearrange("p (a b) -> p a b", a=2)[:, :, 0:64], t, ph,
                         func=ACT.Gelu_apprx_tanh)
            psum.free(k_, t)
            t_hid = t
        table(LN_EXP)
        k_, ps, w = psum.take()
        for mt in range(2):
            t = mm(ps[:, 0:64], P_("w2k", 128 * mt, 128 * mt + 128), hid[:, 0, mt, :], mt == 0, mt == 1, w, t_hid,
                   signal=(mt == 1))
        i = xb_k[0]
        x_ = xb[:, i, 0:64]
        t = copy_act(x_, ps[:, 0:64], t, xb_free[i])
        psum.free(k_, t)
        t = head_norm(x_, None, t, 64, P_("g_kc"), x_)
        ce = small[:, 64:192].rearrange("p (c h n) -> p c h n", c=2, h=2)
        fill(small[:, 64:192], 0.0)
        for c in range(2):
            for hh in range(2):
                vcopy(ce[:, c, hh, 0:31],
                                                        cs[:, c, :].rearrange("p (n j) -> p n j", j=16)[:, 1:32, 15], t_cs)
        t = dve.last()
        a, b, c = rope(x_, t, 64, small[:, 64:128], small[:, 128:192],
                       [((0, 64), xb[0:64, i, 64:128]), ((64, 128), xb[64:128, i, 64:128])])
        vcopy(KC[0:64, :], xb[0:64, i, 64:96])
        t_kc = vcopy(KC[64:128, :], xb[64:128, i, 96:128])
        xb_free[i] = [t_kc, a, b]
        k_, ps, w = psum.take()
        for g in range(2):
            for mt in range(2):
                t = mm(ps[0:32, 64 * g:64 * g + 64], hid[:, 1, mt, 32 * g:32 * g + 32], P_("w2v", 64 * mt, 64 * mt + 64),
                       mt == 0, mt == 1, w, t_hid, signal=True)
        for m in range(8):
            r0, g = 32 * (m % 4), m % 2
            t_vc = vcopy(VC[r0:r0 + 32, m, :], ps[0:32, 64 * g:64 * g + 64], t, t_z)
        psum.free(k_, t_vc)
        cmp_.close()
        att = phase()
        attention_buffers("2", nsa, att)
        ao = []

        def nsa_tile(i):
            oa = OA[:, i % 2, :]
            c0 = 128 * i
            n = 128 * (i + 1)
            blocks = [(128 * j, 128 * j + 128) for j in range(i + 1)]
            oafree = oa_free[i % 2]
            t_oa = None
            for br in range(2):
                ok, ops, ow = psum.take()
                par_ = br

                def score(m):
                    return scores(QN[:, m, c0:c0 + 128], lambda a, b: KSW[:, br, a:b], n, False, None,
                                  C("causal"), [att])

                def head_out(m, p, t):
                    pi, buf, t3 = flipP(p, t, blocks)
                    g = m % 2
                    for j in range(i + 1):
                        tv = mm(ops[:, 64 * m:64 * m + 64], buf[:, 128 * j:128 * j + 128],
                                VSW[:, j, 128 * br + 64 * g:128 * br + 64 * g + 64], j == 0, j == i, ow, t3, signal=(j == i))
                    bufs["T"].free(pi, tv)
                    return tv
                pend = [score(0), score(1)]
                waiting = []
                for m in range(8):
                    k_, S, t = pend.pop(0)
                    p, t = softmax_exp(k_, S, t, rs[:, par_, m:m + 1])
                    waiting.append((m, p, t))
                    if m + 2 < 8:
                        pend.append(score(m + 2))
                    if len(waiting) > 1:
                        t_pv = head_out(*waiting.pop(0))
                while waiting:
                    t_pv = head_out(*waiting.pop(0))
                ts(rs[:, par_, 0:8], rs[:, par_, 0:8], 1e-30, None, ALU.max, ALU.bypass, act.last())
                recip(rr[:, par_, 0:8], rs[:, par_, 0:8])
                tt(dve, rr[:, par_, 0:8], rr[:, par_, 0:8], Gt[:, i, 8 * (br + 1):8 * (br + 1) + 8], ALU.mult)
                bc = rr[:, par_, 0:8].unsqueeze(2).to_broadcast([128, 8, 64])
                O3 = ops[:, 0:512].rearrange("p (a b) -> p a b", a=8)
                if br == 0:
                    t = tt(dve, oa.rearrange("p (a b) -> p a b", a=8), O3, bc, ALU.mult, t_pv, oafree)
                else:
                    f2 = fin[:, flip[0], 0:512]
                    t = tt(dve, f2.rearrange("p (a b) -> p a b", a=8), O3, bc, ALU.mult, t_pv, fin_free[flip[0]])
                    psum.free(ok, t)
                    t = tt(dve, oa, oa, f2, ALU.add)
                psum.free(ok, t)
            sk, sps, sw = psum.take()
            for m in range(8):
                o = sps[:, 32 * m:32 * m + 32]
                mm(o, QN[:, m, c0:c0 + 128], KC[:, :], True, False, sw, att, t_c2)
                t = mm(o, C("ident"), C("cmpadd", 32 * i, 32 * i + 32), False, True, signal=(m == 7))
            S3 = sps[:, 0:256].rearrange("p (a b) -> p a b", a=8)
            p = Pk[0]
            Pk[0] = (p + 1) % NP
            Pv = bufs["P"][:, p, 0:256]
            P3 = Pv.rearrange("p (a b) -> p a b", a=8)
            mx = small[:, 32:40]
            reduce(mx, S3, ALU.max, t)
            t = tt(dve, P3, S3, mx.unsqueeze(2).to_broadcast([128, 8, 32]), ALU.subtract, Pfree[p])
            psum.free(sk, t)
            t = copy_act(Pv, Pv, t, func=ACT.Exp)
            tt(dve, P3, P3, C("cmp01", 32 * i, 32 * i + 32).unsqueeze(1).to_broadcast([128, 8, 32]), ALU.mult, t)
            reduce(mx, P3, ALU.add)
            ts(mx, mx, 1e-30, None, ALU.max)
            recip(mx, mx)
            tt(dve, mx, mx, Gt[:, i, 0:8], ALU.mult)
            t = tt(dve, P3, P3, mx.unsqueeze(2).to_broadcast([128, 8, 32]), ALU.mult)
            pi, buf, t3 = flipP(p, t, [(0, 128), (128, 256)])
            ok, ops, ow = psum.take()
            for m in range(8):
                tv = mm(ops[:, 64 * m:64 * m + 64], buf[:, 128 * (m // 4):128 * (m // 4) + 128], VC[:, m, :],
                        True, True, ow, t3, signal=(m == 7))
            bufs["T"].free(pi, tv)
            t = tt(dve, oa, oa, ops[:, 0:512], ALU.add, tv)
            psum.free(ok, t)
            toks, t_used = finish_tile(oa, t, 128, None, None, 4, 0, M + c0, None, None, att)
            oa_free[i % 2] = osb_free[(flip[0] + 1) % 2]
            ao.append(toks)

        oa_free = [None, None]
        for i in range(4):
            nsa_tile(i)

        nsa.close()
        att = phase()
        SPb = sb("SPb", [128, 2, 4, T], at=two)
        Ab = sb("Ab", [128, 2, 4, T], at=two)
        RT = sb("RT", [128, 2, T], at=two)
        sp_free = [[], []]
        rt_free = [None, None]
        af = [[], []]
        opair = None
        for hd_ in range(8):
            u = hd_ % 2
            tile_ = hd_ // 2
            if u == 0:
                opair = psum.take()
            ok, ops, ow = opair
            t_sum = None
            prev = None
            for j in (3, 2, 1, 0):
                q0 = 128 * j
                n = T - q0
                k_, ps, w = psum.take()
                o = ps[:, 0:n]
                mm(o, KS[:, tile_, q0:q0 + 128], QS[:, hd_, q0:T], True, False, w, att)
                t = mm(ps[:, 0:128], C("ident"), C("strictT"), False, True, t_c2, signal=True)
                e_ = Ab[:, u, j, 0:n]
                t = copy_act(e_, o, t, af[u], func=ACT.Abs, alone=False)
                t = copy_act(e_, e_, t, func=ACT.Exp, scale=-1.0)
                t = copy_act(e_, e_, t, func=ACT.Ln, bias=1.0)
                sp = SPb[:, u, j, 0:n]
                t = stt(sp, o, 0.0, e_, ALU.max, ALU.add, t, sp_free[u])
                t2 = mm(o, C("tri"), sp, False, True, t, signal=(j == 3), onto=True)
                if j < 3:
                    t2 = mm(ps[:, 128:n], C("negone"), RT[:, u, q0 + 128:T], False, True, t_sum, signal=True,
                            onto=True)
                    sp_prev_use = t2
                t3 = copy_act(e_, o, t2, func=ACT.Exp)
                psum.free(k_, t3)
                if j == 3:
                    t_sum = vcopy(RT[:, u, 384:512], sp, rt_free[u])
                elif j:
                    vcopy(RT[:, u, q0:q0 + 128], sp[:, 0:128], t2)
                    t_sum = tt(dve, RT[:, u, q0 + 128:T], RT[:, u, q0 + 128:T], sp[:, 128:n], ALU.add, t2)
                rt_free[u] = t2
                pv = (j, t3)
                if prev is not None:
                    pass
                prev = pv
                tails = t3
            sp_free[u] = [t2, dve.last()]
            for j in range(4):
                q0 = 128 * j
                vt = VSB[:, j, tile_, 0:2, :] if u == 0 else VSB[:, j, tile_, 2:4, :]
                t = mm(ops[:, q0:T], vt.rearrange("p a b -> p (a b)"), Ab[:, u, j, 0:T - q0],
                       u == 0 and j == 0, u == 1 and j == 3, ow, tails, signal=(j == 3))
            af[u] = [t]
            if u:
                src = ops[:, 0:512]
                f = flip[0]
                flip[0] ^= 1
                t = copy_act(fin[:, f, 0:512], src, t, fin_free[f])
                psum.free(ok, t)
                a, b = split(xh[:, 4 + tile_, M:L], xl[:, 4 + tile_, M:L], fin[:, f, 0:512], t, att)
                fin_free[f] = [a, b]
                ao.append([a, b])

        def res2(c):
            def evac(k_, o, tok):
                dst = h[:, c, M:L]
                t = tt(dve, dst, dst, o[:, 0, :], ALU.add, tok, alone=False)
                psum.free(k_, t)
            return evac
        for c in range(8):
            feature([ao] * KT, T, M, res2(c))
        two.close()

        mem = ExitStack()
        hm = sb("hm", [128, KT, 256], at=mem)
        mh = sb("mh", [128, KT, 256], F32R, at=mem)
        ml = sb("ml", [128, KT, 256], F32R, at=mem)
        KM = sb("KM", [128, 2, 256], at=mem)
        VM = sb("VM", [128, 2, 256], at=mem)
        QM = sb("QM", [128, 4, T], at=mem)
        ph = phase()
        attention_buffers("3", mem, ph)
        fill(QM[:, :, :], 0.0, ph)
        t_mem = load("d_mem", hm[:, :, :], memT, ph)
        x_toks = norm("g_memx", h, M, T, 1, xh, xl, ph)
        m_toks = norm("g_memkv", hm, 0, 256, 1, mh, ml, t_mem, ph)
        for c in range(2):
            feature(x_toks, T, M, normed_roped(gmq8, q_dsts(QM, c, (0, T)), do_rope=False))
        for c in range(2):
            feature(m_toks, 256, 0, normed_roped(P_("g_mk"), [((0, 128), KM[:, c, :])], n=256, do_rope=False),
                    xt=(mh, ml))

        def vm_evac(i, ps, tok):
            return copy_act(VM[:, i, :], ps[:, 0:256], tok, ph, alone=False)
        token_tiles(m_toks, [0, 128], 256, vm_evac, xt=(mh, ml))
        att = phase()
        ao = []
        for i in range(4):
            c0 = 128 * i
            ok, ops, ow = psum.take()
            par_ = i % 2

            def score(m):
                return scores(QM[:, m, c0:c0 + 128], lambda a, b: KM[:, m // 2, a:b], 256, False, None, None, [att])

            def head_out(m, p, t):
                pi, buf, t3 = flipP(p, t, [(0, 128), (128, 256)])
                for j in range(2):
                    tv = mm(ops[:, 64 * m:64 * m + 64], buf[:, 128 * j:128 * j + 128], VM[:, j, 64 * m:64 * m + 64],
                            j == 0, j == 1, ow, t3, signal=(j == 1))
                bufs["T"].free(pi, tv)
                return tv
            pend = [score(0), score(1)]
            waiting = []
            for m in range(4):
                k_, S, t = pend.pop(0)
                p, t = softmax_exp(k_, S, t, rs[:, par_, m:m + 1])
                waiting.append((m, p, t))
                if m + 2 < 4:
                    pend.append(score(m + 2))
                if len(waiting) > 1:
                    t_pv = head_out(*waiting.pop(0))
            while waiting:
                t_pv = head_out(*waiting.pop(0))
            t = recip(rr[:, par_, 0:4], rs[:, par_, 0:4], act.last())
            toks, t_used = finish_tile(ops[:, 0:256], t_pv, 128,
                                       ((0, 4), rr[:, par_, 0:4].unsqueeze(2).to_broadcast([128, 4, 64])),
                                       None, 2, 0, M + c0, None, None, att)
            psum.free(ok, t_used)
            ao.append(toks)
        for half in range(2):
            c, hh, ll, tw = chunk()
            for mm_i in range(4):
                m = 4 * half + mm_i

                def wt(part, k, m=mm_i, hh=hh, ll=ll):
                    return (hh, ll)[part][:, 512 * k + 128 * m:512 * k + 128 * m + 128]
                k_, o, tok = tile_feature(wt, (xh, xl), [ao] * 2, T, M, tw, nk=2)
                t = tt(dve, h[:, m, M:L], h[:, m, M:L], o[:, 0, :], ALU.add, tok, alone=False)
                psum.free(k_, t)
            chunk_done(c, tok)
        mem.close()

        ffn("g_ffn2", phase())
        s_out = sem("d_out")
        sync(lambda e: e.dma_start(out, h[:, :, M:L]).then_inc(s_out, 16), dve.last(), alone=False, signal=False)
        sync(lambda e: e.wait_ge(s_out, 16), alone=False, signal=False)
        assert at["use"] == len(sizes)

        block = ctx.enter_context(nc.Block())

        @block.sync
        def _(e):
            sync.emit(e)

        @block.scalar
        def _(e):
            act.emit(e)

        @block.vector
        def _(e):
            dve.emit(e)

        @block.gpsimd
        def _(e):
            pool.emit(e)

        @block.tensor
        def _(e):
            pe.emit(e)


def constants():
    c = np.zeros((128, NCONST), np.float32)

    def put(name, v):
        c[:, CONST[name][0]:CONST[name][1]] = v
    i = np.arange(128)
    put("ident", np.eye(128))
    put("mean", 1.0 / D)
    put("blk", (i[:, None] // 64 == i[None, :] // 64) / 64.0)
    rot = np.zeros((128, 128))
    for b in (0, 64):
        for d in range(8):
            rot[b + d + 8, b + d] = -1.0
            rot[b + d, b + d + 8] = 1.0
    put("rot", rot)
    put("causal", np.where(i[None, :] > i[:, None], NEG, 0.0))
    put("strictT", np.where(i[:, None] >= i[None, :], NEG, 0.0))
    put("chunk", np.where((i[None, :] >= 64) & (i[:, None] < 64), NEG, 0.0))
    put("tri", np.where(i[:, None] >= i[None, :], -1.0, 0.0))
    put("negone", -1.0)
    n = np.arange(32)
    q = i[:, None, None] + 128 * np.arange(4)[None, :, None]
    seen = (16 * n[None, None, :] + 31 <= q) & (n[None, None, :] < 31)
    put("cmpadd", np.where(seen, 0.0, NEG).reshape(128, 128))
    put("cmp01", np.where(seen, 1.0, 0.0).reshape(128, 128))
    d = i % 64
    theta = np.float32(500000.0)
    f8 = theta ** (-np.arange(0, 16, 2, dtype=np.float32) / np.float32(16))
    put("freq", np.where(d < 16, f8[d % 8], 0.0)[:, None])
    inv = (np.float32(1.0) / (theta ** (np.arange(0, 16, 2, dtype=np.float32) / np.float32(16)))).astype(np.float32)
    ang = np.where(d < 16, inv[d % 8], 0.0).astype(np.float32)[:, None] * np.arange(L, dtype=np.float32)[None, :]
    put("cos", np.cos(ang.astype(np.float64)))
    put("sin", np.sin(ang.astype(np.float64)))
    return c


def rows(w):
    return w.reshape(w.shape[0] // 128, 128, w.shape[1]).transpose(1, 0, 2)


def by_cols(w, width=128):
    r = rows(w)
    return [r[:, :, a:a + width].reshape(-1) for a in range(0, w.shape[1], width)]


def by_halves(w):
    r = rows(w)
    return [r[:, 0:4].reshape(-1), r[:, 4:8].reshape(-1)]


def pieces_of(w, sizes):
    at, out = 0, []
    for n in sizes:
        out.append(w[:, at:at + n])
        at += n
    return out


def weights(a):
    out = []
    for l in range(2):
        dq, dk, dv, dg, fq, fk, fv, ff, fg = pieces_of(a["w_in"][l], (512,) * 7 + (8, 512))
        out += by_cols(dq) + by_cols(dk)
        out += by_halves(dv[:, 0:256]) + by_halves(dv[:, 256:512])
        out += by_cols(fq) + by_cols(fk)
        out += by_halves(fv[:, 0:256]) + by_halves(np.concatenate([fv[:, 256:512], ff], axis=1))
        out += by_cols(dg) + by_cols(fg)
        out += by_cols(a["w_out"][l])

    def ffn(wg, wu, wd):
        r = []
        for g, u in zip(by_cols(wg), by_cols(wu)):
            r += [g, u]
        d = rows(wd)
        for m in range(8):
            for f0, f1 in ((0, 8), (8, 16), (16, 22)):
                r.append(d[:, f0:f1, 128 * m:128 * m + 128].reshape(-1))
        return r
    out += ffn(a["ffn1_wg_2"][0], a["ffn1_wu_2"][0], a["ffn1_wd_2"][0])
    q, kc, vc, ks, vs, kw, vw, gt, qs, kk, vv = pieces_of(a["w_in_2"][0], (512,) + (128,) * 6 + (24, 512, 512, 512))
    heads = [m // 2 + 4 * (m % 2) for m in range(8)]
    out += by_cols(q.reshape(D, 8, 64)[:, heads].reshape(D, 512))
    out += by_cols(ks) + by_cols(kw) + by_cols(qs) + by_cols(kk)
    gt = gt.reshape(D, 8, 3)[:, heads].transpose(0, 2, 1).reshape(D, 24)
    out += by_halves(np.concatenate([vs, vw, gt], axis=1))
    out += by_halves(vv[:, 0:256]) + by_halves(vv[:, 256:512])
    for w, name in ((kc, "cmp_w1_k_2"), (vc, "cmp_w1_v_2")):
        out += by_cols(w)
        r = rows(a[name][0])
        out += [r[:, j:j + 4].reshape(-1) for j in range(0, 16, 4)]
    wo = a["w_out_2"][0]
    out += by_cols(np.concatenate([wo[0:512].reshape(8, 64, D)[heads].reshape(512, D), wo[512:]], axis=0))
    out += by_cols(a["mem_wq_2"][0]) + by_cols(a["mem_wk_2"][0]) + by_halves(a["mem_wv_2"][0])
    out += by_cols(a["mem_wo_2"][0], 512)
    out += ffn(a["ffn2_wg_2"][0], a["ffn2_wu_2"][0], a["ffn2_wd_2"][0])
    return np.concatenate(out)


def params(a):
    parts = {}

    def col(g):
        return g.reshape(8, 128).T
    parts["g_norm0"], parts["g_norm1"] = col(a["norm_gain"][0]), col(a["norm_gain"][1])
    parts["g_final"] = col(a["final_gain"])
    for n, k in (("g_ffn1", "ffn1_norm_2"), ("g_mix", "mix_norm_2"), ("g_memx", "mem_x_norm_2"),
                 ("g_memkv", "mem_kv_norm_2"), ("g_ffn2", "ffn2_norm_2")):
        parts[n] = col(a[k][0])
    for l in range(2):
        parts[f"g_sub{l}"] = a["subln_gain"][l][:, None]
        parts[f"fb{l}"] = np.broadcast_to(a["forget_bias"][l][None, :], (128, 8))
        parts[f"lam{l}"] = np.stack([np.concatenate([a["lambda_q1"][l], a["lambda_q2"][l]]),
                                     np.concatenate([a["lambda_k1"][l], a["lambda_k2"][l]])], axis=1)
    for n, k in (("g_q", "nsa_q_norm_2"), ("g_kc", "nsa_kc_norm_2"), ("g_ks", "nsa_ks_norm_2"),
                 ("g_kw", "nsa_kw_norm_2"), ("g_mq", "mem_q_norm_2"), ("g_mk", "mem_k_norm_2")):
        parts[n] = np.concatenate([a[k][0], a[k][0]])[:, None]
    for n, k in (("pe_k", "cmp_pos_k_2"), ("pe_v", "cmp_pos_v_2")):
        parts[n] = a[k][0].reshape(16, 128).T
    w2 = rows(a["cmp_w2_k_2"][0])
    parts["w2k"] = np.concatenate([w2, w2], axis=2).reshape(128, 256)
    parts["w2v"] = rows(a["cmp_w2_v_2"][0]).reshape(128, 128)
    return np.concatenate([parts[n] for n in PARAM], axis=1)


def kernel(**inputs):
    import concourse.bacc as bacc
    from concourse.bass_utils import run_bass_kernel_spmd as run

    a = {k: np.asarray(v) for k, v in inputs.items()}
    hT = np.concatenate([a["meta_tokens"], a["x"][0]], axis=0).T
    arrays = {
        "wstream": weights(a),
        "xT": rows(hT),
        "memT": rows(a["mem_2"][0].T),
        "pos": a["positions_2"].reshape(T),
        "const": constants(),
        "param": params(a),
    }
    arrays = {k: np.ascontiguousarray(v) for k, v in arrays.items()}
    nc = bacc.Bacc("TRN2", target_bir_lowering=False, num_devices=1)
    args = [nc.dram_tensor(k, v.shape, mybir.dt.from_np(v.dtype), kind="ExternalInput").ap() for k, v in arrays.items()]
    args.append(nc.dram_tensor("out", (128, KT, T), F32, kind="ExternalOutput").ap())
    program(nc, *args)
    r = run(nc, [arrays], core_ids=[0])
    got = r.results[0]["out"]
    return got.transpose(2, 1, 0).reshape(1, T, D)
```

```python
import math
from contextlib import ExitStack

import numpy as np

import concourse.bass as bass
from concourse import mybir

F32 = mybir.dt.float32
F32R = mybir.dt.float32r
I32 = mybir.dt.int32
ALU = mybir.AluOpType
ACT = mybir.ActivationFunctionType
AX = mybir.AxisListType

D = 1024
T = 512
M = 16
L = M + T
KT = 8
FT = 22
NEG = -(2.0 ** 100)
CW = 1056
LN_EXP = "natural_log_exp_and_others"



def chunk_sizes():
    ffn = [1024] * (2 * FT) + [1024, 1024, 768] * 8
    s = []
    for _ in range(2):
        s += [1024] * 8 + [1024] * 4 + [1024] * 8 + [1024] * 2 + [1056] * 2 + [1024] * 8
        s += [1024] * 8
    s += ffn
    s += [1024] * 14 + [1056] * 6
    s += [1024] * 10
    s += [1024] * 8
    s += [1024] * 6 + [1024] * 2
    s += ffn
    return s


CONST = {}
_n = 0
for _name, _w in [("ident", 128), ("causal", 128), ("chunk", 64),
                  ("mean", 128), ("blk", 128), ("rot", 128), ("freq", 1), ("cos", L), ("sin", L),
                  ("strictT", 128), ("tri", 128), ("negone", 128), ("cmpadd", 128), ("cmp01", 128)]:
    CONST[_name] = (_n, _n + _w)
    _n += _w
NCONST = _n
NC0 = CONST["mean"][0]
NC1 = CONST["strictT"][0]

PARAM = {}
_n = 0
for _name, _w in [("g_norm0", 8), ("g_norm1", 8), ("g_final", 8), ("g_ffn1", 8), ("g_mix", 8),
                  ("g_memx", 8), ("g_memkv", 8), ("g_ffn2", 8), ("g_sub0", 1), ("g_sub1", 1),
                  ("g_q", 1), ("g_kc", 1), ("g_ks", 1), ("g_kw", 1), ("g_mq", 1), ("g_mk", 1),
                  ("fb0", 8), ("fb1", 8), ("lam0", 2), ("lam1", 2), ("pe_k", 16), ("pe_v", 16),
                  ("w2k", 256), ("w2v", 128)]:
    PARAM[_name] = (_n, _n + _w)
    _n += _w
NPARAM = _n


class Queue:

    def __init__(self, sem):
        self.sem, self.n, self.items = sem, 0, []

    def last(self):
        return (self.sem, self.n) if self.n else None

    def __call__(self, fn, *waits, alone=True, signal=True):
        w = list(waits)
        if alone:
            w.append(self.last())
        if signal:
            self.n += 1
        self.items.append((w, fn, signal))
        return (self.sem, self.n)

    def emit(self, eng):
        seen = {}
        for waits, fn, signal in self.items:
            need = {}
            flat = list(waits)
            while flat:
                t = flat.pop()
                if t is None:
                    continue
                if isinstance(t, list):
                    flat += t
                    continue
                s, v = t
                if seen.get(s, 0) < v:
                    need[s] = max(need.get(s, 0), v)
            for s, v in need.items():
                eng.wait_ge(s, v)
                seen[s] = v
            r = fn(eng)
            if signal:
                r.then_inc(self.sem, 1)


class Ring:

    def __init__(self, count):
        self.rel = [[] for _ in range(count)]
        self.held = [False] * count
        self.age = list(range(count))
        self.now = count

    def take(self, n=1):
        spans = [k for k in range(len(self.rel) - n + 1) if not any(self.held[k:k + n])]
        k = min(spans, key=lambda k: max(self.age[k:k + n]))
        for i in range(k, k + n):
            self.held[i] = True
        return k, [t for r in self.rel[k:k + n] for t in r]

    def free(self, k, n, *toks):
        for i in range(k, k + n):
            self.rel[i], self.held[i], self.age[i] = list(toks), False, self.now
        self.now += 1


def program(nc, wstream, xT, memT, pos, const, param, out):
    sizes = chunk_sizes()
    offs = [0]
    for s in sizes:
        offs.append(offs[-1] + 128 * s)

    ctx = ExitStack()
    with ctx:
        def sem(name):
            return ctx.enter_context(nc.semaphore(name))

        def sb(name, shape, dt=F32, at=None):
            return (at or ctx).enter_context(nc.sbuf_tensor(name, shape, dt))

        pe = Queue(sem("s_pe"))
        dve = Queue(sem("s_dve"))
        act = Queue(sem("s_act"))
        pool = Queue(sem("s_pool"))
        sync = Queue(sem("s_sync"))

        h = sb("h", [128, KT, L])
        xh = sb("xh", [128, KT, L], F32R)
        xl = sb("xl", [128, KT, L], F32R)
        NRAW, NW = 2, 2
        raw = [sb(f"raw{i}", [128, CW]) for i in range(NRAW)]
        wh = [sb(f"wh{i}", [128, CW], F32R) for i in range(NW)]
        wl = [sb(f"wl{i}", [128, CW], F32R) for i in range(NW)]
        cst = sb("cst", [128, NC1 - NC0])
        identR = sb("identR", [128, 128], F32R)
        maskR = sb("maskR", [128, 192], F32R)
        ident = identR[:, :].bitcast(F32)
        causalR, chunkR = maskR[:, 0:128], maskR[:, 128:192]
        xb = sb("xb", [128, 2, L])
        cst2 = [None]
        par = sb("par", [128, NPARAM])
        small = sb("small", [128, 256])
        PS = ctx.enter_context(nc.psum_tensor("ps", [128, 8 * 512], F32))
        banks = Ring(8)
        span = {}

        class psum:

            @staticmethod
            def take(n=2):
                k, w = banks.take(n)
                span[k] = n
                return k, PS[:, 512 * k:512 * (k + n)], w

            @staticmethod
            def free(k, *toks):
                banks.free(k, span[k], *toks)

        def C(name, a=None, b=None):
            lo, hi = CONST[name]
            if lo >= NC1:
                return cst2[0][:, lo - NC1:hi - NC1] if a is None else cst2[0][:, lo - NC1 + a:lo - NC1 + b]
            return cst[:, lo - NC0:hi - NC0] if a is None else cst[:, lo - NC0 + a:lo - NC0 + b]

        def P_(name, a=None, b=None):
            lo, hi = PARAM[name]
            return par[:, lo:hi] if a is None else par[:, lo + a:lo + b]

        def load(name, dst, src, *waits):
            s = sem(name)
            sync(lambda e: e.dma_start(dst, src).then_inc(s, 16), *waits, alone=False, signal=False)
            return (s, 16)

        t_par = load("d_par", par[:, :], param)
        t_x = load("d_x", h[:, :, :], xT)
        t_mats = load("d_mats", xb[:, 0, 0:NC0], const[:, 0:NC0])
        t_cst = load("d_cst", cst[:, :], const[:, NC0:NC1])

        rawsem = [sem(f"d_raw{i}") for i in range(NRAW)]
        rawfree = [[] for _ in range(NRAW)]
        wfree = [[] for _ in range(NW)]
        loaded, parts = {}, {}
        at = {"load": 0, "split": 0, "use": 0}

        def load_chunk():
            c = at["load"]
            if c >= len(sizes):
                return
            at["load"] += 1
            r = c % NRAW
            src = wstream[offs[c]:offs[c + 1]].rearrange("(p n) -> p n", p=128)
            sync(lambda e: e.dma_start(raw[r][:, 0:sizes[c]], src).then_inc(rawsem[r], 16),
                 rawfree[r], alone=False, signal=False)
            loaded[c] = (rawsem[r], 16 * (c // NRAW + 1))

        def split_chunk():
            c = at["split"]
            if c >= len(sizes):
                return
            at["split"] += 1
            while at["load"] <= c:
                load_chunk()
            r, w, n = c % NRAW, c % NW, sizes[c]
            a = act(lambda e: e.activation(wh[w][:, 0:n], raw[r][:, 0:n], ACT.Copy),
                    loaded[c], wfree[w], alone=False)
            b = pool(lambda e: e.tensor_tensor(wl[w][:, 0:n], raw[r][:, 0:n],
                                               wh[w][:, 0:n].bitcast(F32), ALU.subtract),
                     a, wfree[w], alone=False)
            rawfree[r] = [a, b]
            parts[c] = (w, a, b)
            while at["load"] < min(len(sizes), c + 1 + NRAW):
                load_chunk()

        def chunk():
            c = at["use"]
            at["use"] += 1
            while at["split"] <= c:
                split_chunk()
            w, a, b = parts[c]
            return c, wh[w], wl[w], [a, b]

        def chunk_done(c, tok):
            wfree[c % NW] = [tok]
            split_chunk()

        def mm(out_, lhsT, rhs, start, stop, *waits, signal=False, onto=False):
            return pe(lambda e: e.matmul(out_, lhsT, rhs, start=start, stop=stop, skip_group_check=onto), *waits,
                      alone=False, signal=signal)

        def mm3(out_, ws, xs, start, stop, *waits, signal=False):
            mm(out_, ws[0], xs[0], start, False, *waits)
            mm(out_, ws[0], xs[1], False, False)
            return mm(out_, ws[1], xs[0], False, stop, signal=signal)

        def tr(out_, in_, *waits, signal=False):
            k = in_.shape[0]
            return pe(lambda e: e.transpose(out_, in_, ident[0:k, 0:k]), *waits,
                      alone=False, signal=signal)

        def copy_act(dst, src, *waits, scale=1.0, func=ACT.Copy, alone=True, **kw):
            return act(lambda e: e.activation(dst, src, func, scale=scale, **kw), *waits, alone=alone)

        def tt(q, dst, a, b, op, *waits, alone=True):
            return q(lambda e: e.tensor_tensor(dst, a, b, op), *waits, alone=alone)

        def stt(dst, a, s, b, op0, op1, *waits, alone=True):
            return dve(lambda e: e.scalar_tensor_tensor(dst, a, s, b, op0, op1), *waits, alone=alone)

        def ts(dst, a, s1, s2, op0, op1=ALU.bypass, *waits, q=None, alone=True):
            return (q or dve)(lambda e: e.tensor_scalar(dst, a, s1, s2, op0, op1), *waits, alone=alone)

        def vcopy(dst, src, *waits, alone=True):
            return dve(lambda e: e.tensor_copy(dst, src), *waits, alone=alone)

        def fill(dst, v, *waits, q=None, alone=True):
            return (q or dve)(lambda e: e.memset(dst, v), *waits, alone=alone)

        def reduce(dst, src, op, *waits, alone=True, **kw):
            return dve(lambda e: e.tensor_reduce(dst, src, AX.X, op, **kw), *waits, alone=alone)

        def recip(dst, src, *waits, alone=True):
            return dve(lambda e: e.reciprocal(dst, src), *waits, alone=alone)

        def scan(dst, ones, src, *waits):
            return dve(lambda e: e.tensor_tensor_scan(dst, ones, src, 0.0, ALU.mult, ALU.subtract), *waits)

        def table(name):
            return act(lambda e: e.preload_act_table_set(name), signal=False)

        fence = [None]

        def phase():
            fence[0] = [pe.last(), dve.last(), act.last(), pool.last()]
            return fence[0]

        for k in range(8):
            span[k] = 1
            psum.free(k, fill(PS[:, 512 * k:512 * k + 512], 0.0, alone=False))
        table(LN_EXP)
        copy_act(identR[:, :], xb[:, 0, 0:128], t_mats)
        t_ident = copy_act(maskR[:, :], xb[:, 0, 128:320])

        scratch = sb("scratch", [128, 4, L])
        s_free = [[] for _ in range(4)]
        rst = sb("rst", [128, L])
        rst_free = [None]

        def rstd_of(src, c0, n, waits, halves):
            acc, sq = scratch[:, 2, 0:n], scratch[:, 0:2, 0:n]
            t_acc = None
            free = [None, None]
            for k in range(KT):
                dst = acc if k == 0 else sq[:, k % 2, :]
                t = copy_act(dst, src[:, k, c0:c0 + n], waits, s_free[2] if k == 0 else [free[k % 2], s_free[k % 2]],
                             func=ACT.Square, alone=False)
                if k:
                    t = tt(dve, acc, acc, dst, ALU.add, t, t_acc)
                    free[k % 2] = t
                t_acc = t
            k, ps, w = psum.take()
            o = ps[:, :].rearrange("p (a b) -> p a b", a=2)[:, 0:halves, 0:n // halves]
            for i in range(halves):
                t = mm(o[:, i, :], C("mean"), acc[:, i * (n // halves):(i + 1) * (n // halves)],
                       True, True, w, t_acc, t_cst, signal=True)
            s_free[0] = [free[0]]
            s_free[1] = [free[1]]
            s_free[2] = [t]
            r = rst[:, 0:n]
            t = copy_act(r.rearrange("p (a b) -> p a b", a=halves), o, t, rst_free[0], func=ACT.Ln, bias=1e-6)
            psum.free(k, t)
            return r, copy_act(r, r, t, func=ACT.Exp, scale=-0.5)

        tmpn = sb("tmpn", [128, 2, L])
        tmp_free = [None, None]

        def split(dst_h, dst_l, src, *waits):
            a = copy_act(dst_h, src, *waits, alone=False)
            b = tt(pool, dst_l, src, dst_h.bitcast(F32), ALU.subtract, a, *waits, alone=False)
            return a, b

        def norm(gain, src, c0, n, halves, dst_h, dst_l, *waits):
            r, t_r = rstd_of(src, c0, n, list(waits), halves)
            toks = []
            t = None
            for k in range(KT):
                u = tmpn[:, k % 2, 0:n]
                t = stt(u, src[:, k, c0:c0 + n], P_(gain, k, k + 1), r, ALU.mult, ALU.mult,
                        t_r, tmp_free[k % 2], t_par, *waits, alone=False)
                a, b = split(dst_h[:, k, c0:c0 + n], dst_l[:, k, c0:c0 + n], u, t, *waits)
                tmp_free[k % 2] = [a, b]
                toks.append([a, b])
            rst_free[0] = t
            return toks

        def tile_feature(wt, xt, x_toks, n, c0, tw, nk=KT, cols=None):
            k_, ps, w = psum.take()
            halves = 2 if n > 512 else 1
            m = n // halves
            o = ps[:, :].rearrange("p (a b) -> p a b", a=2)[:, 0:halves, 0:m]
            tok = None
            for i in range(halves):
                for k in range(nk):
                    a, b = c0 + i * m, c0 + (i + 1) * m
                    tok = mm3(o[:, i, :], (wt(0, k), wt(1, k)), (xt[0][:, k, a:b], xt[1][:, k, a:b]),
                              k == 0, k == nk - 1, w, tw, x_toks[k], signal=(k == nk - 1))
            return k_, o, tok

        def feature(x_toks, n, c0, evac, xt=None):
            c, hh, ll, tw = chunk()

            def wt(part, k):
                return (hh, ll)[part][:, 128 * k:128 * k + 128]
            k_, o, tok = tile_feature(wt, xt or (xh, xl), x_toks, n, c0, tw)
            chunk_done(c, tok)
            evac(k_, o, tok)

        def token_tiles(x_toks, starts, ncols, evac, xt=None):
            xt = xt or (xh, xl)
            slots = [psum.take() for _ in range((len(starts) + 1) // 2)]
            toks = []
            for half in range(2):
                c, hh, ll, tw = chunk()
                for i, a in enumerate(starts):
                    k_, ps, w = slots[i // 2]
                    o = ps[:, 512 * (i % 2):512 * (i % 2) + ncols]
                    for kk in range(4):
                        k = 4 * half + kk
                        tok = mm3(o, (xt[0][:, k, a:a + 128], xt[1][:, k, a:a + 128]),
                                  (hh[:, ncols * kk:ncols * (kk + 1)], ll[:, ncols * kk:ncols * (kk + 1)]),
                                  k == 0, k == KT - 1, w, tw, x_toks[k], signal=(kk == 3))
                    toks.append(tok)
                chunk_done(c, tok)
            for i in range(len(starts)):
                k_, ps, w = slots[i // 2]
                t = evac(i, ps[:, 512 * (i % 2):512 * (i % 2) + ncols], toks[len(starts) + i])
                if i % 2:
                    psum.free(k_, prev, t)
                elif i == len(starts) - 1:
                    psum.free(k_, t)
                prev = t

        xb_free = [t_ident, None]
        xb_k = [0]
        t1b = scratch

        def rope(src, t_src, n, cos, sin, dsts, *waits):
            i = xb_k[0]
            k_, ps, w = psum.take()
            halves = 2 if n > 512 else 1
            m = n // halves
            o = ps[:, :].rearrange("p (a b) -> p a b", a=2)[:, 0:halves, 0:m]
            for j in range(halves):
                t = mm(o[:, j, :], C("rot"), src[:, j * m:(j + 1) * m], True, True, w, t_src, signal=True)
            a = tt(dve, t1b[:, 0, 0:n], src, cos, ALU.mult, t_src, *waits)
            v = t1b[:, 1, 0:n]
            b = tt(dve, v.rearrange("p (a b) -> p a b", a=halves), o,
                   sin.rearrange("p (a b) -> p a b", a=halves), ALU.mult, t)
            psum.free(k_, b)
            for (p0, p1), dst in dsts:
                c = tt(dve, dst, t1b[p0:p1, 0, 0:n], t1b[p0:p1, 1, 0:n], ALU.add)
            return a, t, c

        def three(ap, n, halves):
            return ap.rearrange("p (a b) -> p a b", a=halves)

        NP, NT = 4, 2
        Pfree = [[] for _ in range(NP)]
        Pk = [0]
        nm = sb("nm", [128, 8])
        nmk = [0]
        nm_free = [None] * 8
        rs = sb("rs", [128, 2, 8])
        rr = sb("rr", [128, 2, 8])
        osb, fin = tmpn, xb
        fin_free, osb_free = xb_free, tmp_free
        flip = [0]
        bufs = {}

        def attention_buffers(name, scope, start):
            bufs["P"] = sb("Pb" + name, [128, NP, L], at=scope)
            bufs["T"] = [sb(f"PT{name}{i}", [128, 640], at=scope) for i in range(NT)]
            bufs["Tr"] = Ring(NT)
            for k in range(NP):
                Pfree[k] = list(start)
            for k in range(NT):
                bufs["Tr"].free(k, 1, *start)

        def scores(q_lhsT, k_rhs, nkeys, meta, extra, mask, t_in):
            o0 = 112 if meta else 0
            n = nkeys
            k_, ps, w = psum.take(2 if o0 + n > 512 else 1)
            first = min(n, 512 - o0)
            spans = [(0, first)] + ([(first, n)] if n > first else [])
            for a, b in spans:
                o = ps[:, o0 + a:o0 + b]
                lastpart = b == n
                terms = [(q_lhsT, k_rhs(a, b), o)]
                if extra is not None:
                    terms += [(extra[0], r, o) for r in extra[1](a, b)]
                if mask is not None and lastpart:
                    mw = mask.shape[1]
                    terms.append((identR[:, :], mask, ps[:, o0 + n - mw:o0 + n]))
                for i, (l_, r_, o_) in enumerate(terms):
                    t = mm(o_, l_, r_, i == 0, i == len(terms) - 1, w, t_in, t_cst, t_ident,
                           signal=(lastpart and i == len(terms) - 1))
            return k_, ps[:, o0:o0 + n], t

        def row_max(k_, S, t):
            c = nmk[0]
            nmk[0] = (c + 1) % 8
            return c, reduce(nm[:, c:c + 1], S, ALU.max, t, nm_free[c], alone=False, negate=True)

        def row_exp(k_, S, c, t_max, rs_ap, *waits):
            p = Pk[0]
            Pk[0] = (p + 1) % NP
            a = copy_act(bufs["P"][:, p, 0:S.shape[1]], S, t_max, Pfree[p], *waits, func=ACT.Exp,
                         bias=nm[:, c:c + 1], accum_out=rs_ap, alone=False)
            nm_free[c] = a
            psum.free(k_, a)
            return p, a

        def flip_pe(p, t, cols, src=None):
            k_, ps, w = psum.take((len(cols) + 3) // 4)
            src = bufs["P"][:, p, :] if src is None else src
            for j, (a, b) in enumerate(cols):
                t2 = tr(ps[0:b - a, 128 * j:128 * j + 128], src[:, a:b], w, t, t_ident, signal=(j == len(cols) - 1))
            if p is not None:
                Pfree[p] = [t2]
            return k_, ps, t2, 128 * len(cols)

        def flip_copy(k_, ps, t2, n, q):
            i, w2 = bufs["Tr"].take()
            buf = bufs["T"][i]
            if q is dve:
                t3 = vcopy(buf[:, 0:n], ps[:, 0:n], t2, w2, alone=False)
            else:
                t3 = copy_act(buf[:, 0:n], ps[:, 0:n], t2, w2, alone=False)
            psum.free(k_, t3)
            return i, buf, t3

        def flip_free(i, tok):
            bufs["Tr"].free(i, 1, tok)

        def attention(units):
            nxt, S, mx = 0, {}, {}
            flips, pvs, later = [], [], []
            s = 0

            def more(s):
                nonlocal nxt
                while nxt < len(units) and nxt <= s + units[nxt]["ahead"]:
                    S[nxt] = units[nxt]["score"]()
                    nxt += 1
            more(-1)
            if 0 in S:
                mx[0] = row_max(*S[0])
            while s < len(units) or flips or pvs or later:
                got = None
                if s < len(units):
                    if s not in S:
                        more(s)
                        mx[s] = row_max(*S[s])
                    k_, S_, _ = S.pop(s)
                    c, t = mx.pop(s)
                    got = row_exp(k_, S_, c, t, units[s]["sum"], *units[s]["sum_waits"]())
                fl = [(f, flip_pe(f["p"], f["t"], f["blocks"])) for f in flips]
                more(s)
                for job, (i, buf, t3) in pvs:
                    tok = job["pv"](buf, t3)
                    flip_free(i, tok)
                    if job["end"] is not None:
                        later.append(job["end"](tok))
                if s + 1 in S:
                    mx[s + 1] = row_max(*S[s + 1])
                flips = []
                if s < len(units) and "start" in units[s]:
                    later.append(units[s]["start"]())
                if got is not None:
                    job = units[s]["job"](*got)
                    if job is not None:
                        flips.append(job)
                pvs = [(f, flip_copy(*r, dve if s % 2 else act)) for f, r in fl]
                later = [g for g in later if next(g, False)]
                s += 1

        def finish_tile(o_ap, t_o, nq, heads, scale_bc, copy, ntile, dst_t0, col0, gate, gain, toks, used, *waits):
            f = flip[0]
            flip[0] ^= 1
            w_ = 128 * ntile
            d = osb[0:nq, f, 0:w_]
            if scale_bc is not None:
                t = tt(dve, d.rearrange("p (a b) -> p a b", a=heads), o_ap.rearrange("p (a b) -> p a b", a=heads),
                       scale_bc, ALU.mult, t_o, osb_free[f])
            elif copy:
                t = vcopy(d, o_ap, t_o, osb_free[f])
            else:
                d, t = o_ap, t_o
            used(t)
            yield True
            k_, ps, w = psum.take(1)
            for j in range(ntile):
                t2 = tr(ps[:, 128 * j:128 * j + nq], d[:, 128 * j:128 * j + 128], w, t, signal=(j == ntile - 1))
            if d is not o_ap:
                osb_free[f] = [t2]
            else:
                oa_free[0] = t2
            src = ps[:, 0:w_].rearrange("p (a b) -> p a b", a=ntile)[:, :, 0:nq]
            g = fin[:, f, 0:ntile * nq].rearrange("p (a b) -> p a b", a=ntile)
            if gate is None:
                t3 = vcopy(g, src, t2, fin_free[f])
            elif gain is None:
                t3 = tt(dve, g, src, gate, ALU.mult, t2, fin_free[f], *waits)
            else:
                for j in range(ntile):
                    t3 = stt(g[:, j, :], src[:, j, :], gain, gate[:, j, :], ALU.mult, ALU.mult, t2, fin_free[f], *waits,
                             alone=(j == 0))
            psum.free(k_, t3)
            a, b = split(xh[:, dst_t0:dst_t0 + ntile, col0:col0 + nq], xl[:, dst_t0:dst_t0 + ntile, col0:col0 + nq],
                         g, t3, *waits)
            fin_free[f] = [a, b]
            toks += [a, b]

        rs_free = [None, None]
        oa_free = [None]

        def drain(gen):
            for _ in gen:
                pass

        lam_init = [0.8 - 0.6 * math.exp(-0.3 * l) for l in range(2)]
        neglam = [None, None]
        t_lam = None
        fill(small[:, 0:64], 0.0)
        t_small = dve.last()
        for l in range(2):
            b = 8 * l
            tt(dve, small[0:64, b:b + 1], P_(f"lam{l}", 0, 1)[0:64], P_(f"lam{l}", 1, 2)[0:64], ALU.mult, t_par)
            t = tt(dve, small[64:128, b + 1:b + 2], P_(f"lam{l}", 0, 1)[64:128], P_(f"lam{l}", 1, 2)[64:128], ALU.mult)
            k_, ps, w = psum.take()
            t = mm(ps[:, 0:2], C("mean"), small[:, b:b + 2], True, True, w, t, t_cst, signal=True)
            t = copy_act(small[:, b + 2:b + 4], ps[:, 0:2], t, scale=1024.0, func=ACT.Exp)
            psum.free(k_, t)
            t = tt(dve, small[:, b + 4:b + 5], small[:, b + 3:b + 4], small[:, b + 2:b + 3], ALU.subtract, t)
            t_lam = ts(small[:, b + 5:b + 6], small[:, b + 4:b + 5], -lam_init[l], None, ALU.add)
            ts(small[:, b + 6:b + 7], P_(f"g_sub{l}"), 1.0 - lam_init[l], None, ALU.mult)
            neglam[l] = small[:, b + 5:b + 6]
        gsub = [small[:, 6:7], small[:, 14:15]]
        gq8, gmq8 = small[:, 16:17], small[:, 17:18]
        ts(gq8, P_("g_q"), 0.125, None, ALU.mult)
        t_prep = ts(gmq8, P_("g_mq"), 0.125, None, ALU.mult)

        one = ExitStack()
        attention_buffers("1", one, [])
        QA = sb("QA", [128, 8, L], at=one)
        QB = sb("QB", [128, 8, L], at=one)
        KA = sb("KA", [128, 4, L], at=one)
        KB = sb("KB", [128, 4, L], at=one)
        VA = sb("VA", [128, 5, T], at=one)
        VB = sb("VB", [128, 5, T], at=one)
        G = sb("G", [128, 8, L], at=one)
        NCh = sb("NCh", [128, L], F32R, at=one)
        NCl = sb("NCl", [128, L], F32R, at=one)
        LF = sb("LF", [128, 3, 40], at=one)
        onesr = bufs["P"][0:8, 0, :]
        fill(QA[:, :, :], 0.0)
        fill(QB[:, :, :], 0.0)
        fill(NCh[:, :].bitcast(F32), 0.0)
        fill(NCl[:, :].bitcast(F32), 0.0)
        fill(LF[:, :, :], 0.0)
        t_b1 = dve.last()

        def q_dsts(Q, tile, cols):
            return [((0, 64), Q[0:64, 2 * tile, cols[0]:cols[1]]), ((64, 128), Q[64:128, 2 * tile + 1, cols[0]:cols[1]])]

        starts = [0] + [M + 128 * i for i in range(4)]

        def evac_copy(dst, src, k_, tok, *waits, scale=1.0, q=None):
            t = copy_act(dst, src, tok, *waits, scale=scale, alone=False) if q is None else \
                vcopy(dst, src, tok, *waits, alone=False)
            psum.free(k_, t)
            return t

        for l in range(2):
            full = l == 0
            n_q, c_q = (L, 0) if full else (T, M)
            ph = phase()
            x_toks = norm(f"g_norm{l}", h, 0, L, 2, xh, xl, t_x, ph)
            halves_q = 2 if full else 1

            def roped(dsts, cos_cols, n, scale):
                def evac(k_, o, tok):
                    i = xb_k[0]
                    xb_k[0] ^= 1
                    x_ = xb[:, i, 0:n]
                    hv = 2 if n > 512 else 1
                    t = copy_act(three(x_, n, hv), o, tok, xb_free[i], scale=scale, alone=False)
                    psum.free(k_, t)
                    a, b, c = rope(x_, t, n, C("cos", *cos_cols), C("sin", *cos_cols), dsts, ph, t_cst)
                    xb_free[i] = [a, b]
                return evac

            cols = (c_q, c_q + n_q)
            for c in range(4):
                feature(x_toks, n_q, c_q, roped(q_dsts(QA, c, cols), cols, n_q, 0.125))
            for c in range(4):
                feature(x_toks, L, 0, roped([((0, 128), KA[:, c, :])], (0, L), L, 1.0))

            def v_evac(V, c):
                def evac(i, ps, tok):
                    rows = 16 if i == 0 else 128
                    dst, src = V[0:rows, i, 256 * c:256 * c + 256], ps[0:rows, 0:256]
                    if i % 2:
                        return copy_act(dst, src, tok, ph, alone=False)
                    return vcopy(dst, src, tok, ph, alone=False)
                return evac
            for c in range(2):
                token_tiles(x_toks, starts, 256, v_evac(VA, c))

            def fq_evac(c):
                def evac(k_, o, tok):
                    for j, ((p0, p1), dst) in enumerate(q_dsts(QB, c, cols)):
                        t = copy_act(three(dst, n_q, halves_q), o[p0:p1, :, :], tok, ph, t_b1, scale=0.125, alone=False)
                    psum.free(k_, t)
                return evac

            def fk_evac(c):
                def evac(k_, o, tok):
                    evac_copy(three(KB[:, c, :], L, 2), o, k_, tok, ph, q=dve)
                return evac
            for c in range(4):
                feature(x_toks, n_q, c_q, fq_evac(c))
            for c in range(4):
                feature(x_toks, L, 0, fk_evac(c))
            token_tiles(x_toks, starts, 256, v_evac(VB, 0))

            def last_v(i, ps, tok):
                rows = 16 if i == 0 else 128
                t = vcopy(VB[0:rows, i, 256:512], ps[0:rows, 0:256], tok, ph, alone=False)
                t2 = tt(dve, LF[0:rows, 0, 8 * i:8 * i + 8], ps[0:rows, 256:264], P_(f"fb{l}")[0:rows], ALU.add,
                        tok, ph, t_par)
                return [t, t2]
            token_tiles(x_toks, starts, 264, last_v)
            z_, a_, b_ = LF[:, 0, :], LF[:, 1, :], LF[:, 2, :]
            t = stt(a_, z_, -1.0, z_, ALU.mult, ALU.max)
            t = copy_act(a_, a_, t, func=ACT.Exp, scale=-1.0)
            t = copy_act(a_, a_, t, func=ACT.Ln, bias=1.0)
            t = stt(b_, z_, 0.0, a_, ALU.min, ALU.subtract, t)
            k_, ps, w = psum.take()
            tr(ps[0:8, 112:128], LF[0:16, 2, 0:8], w, t, t_ident)
            for i in range(4):
                t = tr(ps[0:8, 128 * (i + 1):128 * (i + 2)], LF[:, 2, 8 * i + 8:8 * i + 16], signal=(i == 3))
            fill(onesr, 1.0, Pfree[0])
            ncm = bufs["P"][0:8, 1, :]
            t = scan(ncm, onesr, ps[0:8, 112:640], t, Pfree[1])
            psum.free(k_, t)
            Pfree[0] = [t]
            t_nc = list(split(NCh[0:8, :], NCl[0:8, :], ncm, t, ph, t_b1))
            Pfree[1] = t_nc

            def gate_evac(c):
                def evac(k_, o, tok):
                    t = copy_act(three(G[:, c, cols[0]:cols[1]], n_q, halves_q), o, tok, ph,
                                 func=ACT.Silu, alone=False)
                    psum.free(k_, t)
                return evac
            for c in range(8):
                feature(x_toks, n_q, c_q, gate_evac(c))
            table(LN_EXP)
            att = phase()
            ao_toks = []
            units = []
            n_units = 0

            def head_end(l, kind, i, ok, O, nq, c0, par_, t_pv, att):
                def used(t):
                    psum.free(ok, t)
                gate = G[:, 0:4, c0:c0 + nq] if kind == "diff" else G[:, 4:8, c0:c0 + nq]
                if kind == "diff":
                    f = flip[0]
                    sq = osb[0:nq, f, 0:512]
                    ms = small[0:nq, 48:52]
                    t = copy_act(sq, O, t_pv, osb_free[f], func=ACT.Square, alone=False)
                    yield True
                    t = reduce(ms, sq.rearrange("p (a b) -> p a b", a=4), ALU.add, t, alone=False)
                    t = copy_act(ms, ms, t, func=ACT.Ln, scale=1.0 / 128, bias=1e-5, alone=False)
                    t = copy_act(ms, ms, t, func=ACT.Exp, scale=-0.5, alone=False)
                    yield True
                    g = finish_tile(O, t, nq, 4, ms.unsqueeze(2).to_broadcast([nq, 4, 128]), False, 4, 0, c0, gate,
                                    gsub[l], ao_toks, used, att)
                elif i < 0:
                    g = finish_tile(O, t_pv, nq, 8, None, True, 4, 4, c0, gate, None, ao_toks, used, att)
                else:
                    recip(rr[:, par_, 0:8], rs[:, par_, 0:8], t_pv, alone=False)
                    rs_free[par_] = dve.last()
                    g = finish_tile(O, t_pv, nq, 8, rr[:, par_, 0:8].unsqueeze(2).to_broadcast([128, 8, 64]), False,
                                    4, 4, c0, gate, None, ao_toks, used, att)
                yield from g

            outs = {}
            pair = []

            def unit(l, kind, i, m, index, Q, K, V, c0, att, t_nc):
                par_ = (i + 1) % 2
                n = M + 128 * (i + 1)
                blocks = [(0, M)] + [(M + 128 * j, M + 128 * j + 128) for j in range(i + 1)]
                nh, hd = (4, 128) if kind == "diff" else (8, 64)

                def score():
                    ex = None
                    if kind == "fox":
                        ex = (identR[:, m:m + 1].to_broadcast([128, 128]), lambda a, b: (NCh[:, a:b], NCl[:, a:b]))
                    return scores(Q[:, m, c0:c0 + 128], lambda a, b: K[:, m // 2, a:b], n, True, ex,
                                  causalR if kind == "fox" else chunkR, [att, t_nc])

                def pv_of(hh):
                    def pv(buf, t3):
                        if hh == 0:
                            outs[(kind, i)] = psum.take(1)
                        ok, ops, ow = outs[(kind, i)]
                        for j, (a, b) in enumerate(blocks):
                            tv = mm(ops[:, hd * hh:hd * hh + hd], buf[0:b - a, 128 * j:128 * j + 128],
                                    V[0:b - a, j, hd * hh:hd * hh + hd], j == 0, j == len(blocks) - 1,
                                    ow, t3, signal=(j == len(blocks) - 1))
                        return tv
                    return pv

                def end(tok):
                    ok, ops, ow = outs[(kind, i)]
                    return head_end(l, kind, i, ok, ops[:, 0:512], 128, c0, par_, tok, att)

                def job(p, t):
                    if kind == "fox":
                        return dict(p=p, t=t, blocks=blocks, pv=pv_of(m), end=end if m == 7 else None)
                    pair.append((p, t))
                    if m % 2 == 0:
                        return None
                    (p0, ta), (p1, tb) = pair
                    del pair[:]
                    q0, q1 = rr[:, par_, m - 1:m], rr[:, par_, m:m + 1]
                    P = bufs["P"]
                    t = recip(rr[:, par_, m - 1:m + 1], rs[:, par_, m - 1:m + 1], ta, tb)
                    rs_free[par_] = t
                    t = tt(dve, q1, q1, neglam[l], ALU.mult, t_lam)
                    t = ts(P[:, p1, 0:n], P[:, p1, 0:n], q1, None, ALU.mult)
                    t = stt(P[:, p0, 0:n], P[:, p0, 0:n], q0, P[:, p1, 0:n], ALU.mult, ALU.add)
                    Pfree[p1] = [t]
                    return dict(p=p0, t=t, blocks=blocks, pv=pv_of(m // 2), end=end if m == 7 else None)
                return dict(ahead=1 if i == 3 else 2, score=score, sum=rs[:, par_, m:m + 1],
                            sum_waits=lambda: [rs_free[par_]], job=job)

            for kind in ("diff", "fox"):
                Q, K, V = (QA, KA, VA) if kind == "diff" else (QB, KB, VB)
                nh, hd, t0 = (4, 128, 0) if kind == "diff" else (8, 64, 4)
                tiles = ([-1] if full else []) + [0, 1, 2, 3]
                for i in tiles:
                    par_ = (i + 1) % 2
                    nq = 16 if i < 0 else 128
                    c0 = 0 if i < 0 else M + 128 * i
                    if i < 0:
                        ok, ops, ow = psum.take(1)
                        O = ops[0:16, 0:512]
                        sk, sps, sw = psum.take(1)
                        for m in range(8):
                            o = sps[0:16, 16 * m:16 * m + 16]
                            if kind == "diff":
                                t = mm(o, Q[:, m, 0:16], K[:, m // 2, 0:16], True, True, sw, att, signal=m == 7)
                            else:
                                mm(o, Q[:, m, 0:16], K[:, m // 2, 0:16], True, False, sw, att)
                                for part in (NCh, NCl):
                                    mm(o, ident[:, m:m + 1].to_broadcast([128, 16]), part[:, 0:16].bitcast(F32),
                                       False, False, t_nc)
                                t = mm(o, ident[:, 0:16], causalR[:, 0:16].bitcast(F32), False, True, signal=m == 7)
                        S3 = sps[0:16, 0:128].rearrange("p (a b) -> p a b", a=8)
                        p = Pk[0]
                        Pk[0] = (p + 1) % NP
                        Pv = bufs["P"][0:16, p, 0:128]
                        P3 = Pv.rearrange("p (a b) -> p a b", a=8)
                        mx = small[0:16, 32:40]
                        t = reduce(mx, S3, ALU.max, t)
                        t = tt(dve, P3, S3, mx.unsqueeze(2).to_broadcast([16, 8, 16]), ALU.subtract, t, Pfree[p])
                        psum.free(sk, t)
                        t = copy_act(Pv, Pv, t, func=ACT.Exp)
                        t = reduce(mx, P3, ALU.add, t)
                        t = recip(mx, mx)
                        t = tt(dve, P3, P3, mx.unsqueeze(2).to_broadcast([16, 8, 16]), ALU.mult)
                        if kind == "diff":
                            P4 = Pv.rearrange("p (a m b) -> p a m b", a=4, m=2)
                            t = stt(P4[:, :, 0, :], P4[:, :, 1, :], neglam[l][0:16], P4[:, :, 0, :], ALU.mult, ALU.add,
                                    t_lam)
                        tk, tps, tw = psum.take(1)
                        for hh in range(nh):
                            a = 16 * (2 * hh if kind == "diff" else hh)
                            t2 = tr(tps[0:16, 16 * hh:16 * hh + 16], bufs["P"][0:16, p, a:a + 16], tw, t,
                                    signal=hh == nh - 1)
                        Pfree[p] = [t2]
                        pi, w2 = bufs["Tr"].take()
                        buf = bufs["T"][pi]
                        t3 = vcopy(buf[0:16, 0:16 * nh], tps[0:16, 0:16 * nh], t2, w2)
                        psum.free(tk, t3)
                        for hh in range(nh):
                            t_pv = mm(ops[0:16, hd * hh:hd * hh + hd], buf[0:16, 16 * hh:16 * hh + 16],
                                      V[0:16, 0, hd * hh:hd * hh + hd], True, True, ow, t3, signal=True)
                        flip_free(pi, t_pv)
                        drain(head_end(l, kind, i, ok, O, 16, c0, None, t_pv, att))
                        continue
                    units += [unit(l, kind, i, m, n_units + m, Q, K, V, c0, att, t_nc) for m in range(8)]
                    n_units += 8
            attention(units)
            ao = list(ao_toks)

            def res_evac(c, scale=None):
                def evac(k_, o, tok):
                    hv = o.shape[1]
                    dst = three(h[:, c, cols[0]:cols[1]], n_q, hv)
                    t = tt(dve, dst, dst, o, ALU.add, tok, alone=False)
                    psum.free(k_, t)
                return evac
            for c in range(8):
                feature([ao] * KT, n_q, c_q, res_evac(c))
        one.close()

        ph = phase()
        r, t_r = rstd_of(h, M, T, [ph], 1)
        for k in range(KT):
            t = stt(h[:, k, M:L], h[:, k, M:L], P_("g_final", k, k + 1), r, ALU.mult, ALU.mult, t_r, alone=False)
        rst_free[0] = t

        def ffn(gain, ph):
            st = ExitStack()
            aH = sb(gain + "aH", [128, FT, T], F32R, at=st)
            aL = sb(gain + "aL", [128, FT, T], F32R, at=st)
            x_toks = norm(gain, h, M, T, 1, xh, xl, ph)
            act_toks = []
            for f in range(FT):
                k_, ps, w = psum.take()
                for s in range(2):
                    c, hh, ll, tw = chunk()
                    for k in range(KT):
                        a = 128 * k
                        t = mm3(ps[:, 512 * s:512 * s + 512], (hh[:, a:a + 128], ll[:, a:a + 128]),
                                (xh[:, k, M:L], xl[:, k, M:L]), k == 0, k == KT - 1, w, tw, x_toks[k],
                                signal=(k == KT - 1))
                    chunk_done(c, t)
                    if s == 0:
                        tg = t
                i = f % 2
                a = copy_act(xb[:, i, 0:T], ps[:, 0:512], tg, xb_free[i], func=ACT.Silu, alone=False)
                b = tt(dve, tmpn[:, i, 0:T], xb[:, i, 0:T], ps[:, 512:1024], ALU.mult, a, t, tmp_free[i], alone=False)
                psum.free(k_, b)
                xb_free[i] = b
                p, q = split(aH[:, f, :], aL[:, f, :], tmpn[:, i, 0:T], b, ph)
                tmp_free[i] = [p, q]
                act_toks.append([p, q])
            for m in range(KT):
                k_, ps, w = psum.take()
                for f0, nf in ((0, 8), (8, 8), (16, 6)):
                    c, hh, ll, tw = chunk()
                    for kk in range(nf):
                        f = f0 + kk
                        t = mm3(ps[:, 0:512], (hh[:, 128 * kk:128 * kk + 128], ll[:, 128 * kk:128 * kk + 128]),
                                (aH[:, f, :], aL[:, f, :]), f == 0, f == FT - 1, w, tw, act_toks[f], signal=(kk == nf - 1))
                    chunk_done(c, t)
                t = stt(h[:, m, M:L], ps[:, 0:512], 0.5, h[:, m, M:L], ALU.mult, ALU.add, t, alone=False)
                psum.free(k_, t)
            st.close()

        ffn("g_ffn1", phase())

        two = ExitStack()
        cst2[0] = sb("cst2", [128, NCONST - NC1], at=two)
        QS = sb("QS", [128, 8, T], at=two)
        KS = sb("KS", [128, 4, T], at=two)
        VSB = sb("VSB", [128, 4, 4, 4, 64], at=two)
        nsa = ExitStack()
        QN = sb("QN", [128, 8, T], at=nsa)
        KSW = sb("KSW", [128, 2, T], at=nsa)
        VSW = sb("VSW", [128, 4, 256], at=nsa)
        Gt = sb("Gt", [128, 4, 24], at=nsa)
        cs = sb("cs", [128, 2, T], at=nsa)
        KC = sb("KC", [128, 32], at=nsa)
        VC = sb("VC", [128, 8, 64], at=nsa)
        OA = sb("OA", [128, 2, 512], at=nsa)
        cmp_ = ExitStack()
        X2 = sb("X2", [128, 2, T], at=cmp_)
        YH = sb("YH", [128, 2, 66, 8], F32R, at=cmp_)
        YL = sb("YL", [128, 2, 66, 8], F32R, at=cmp_)
        hid = sb("hid", [128, 2, 2, 64], at=cmp_)
        posi = sb("posi", [128, T], I32, at=cmp_)
        ph = phase()
        t_c2 = load("d_cst2", cst2[0][:, :], const[:, NC1:NCONST], ph)
        t_pos = load("d_pos", posi[:, :], pos.partition_broadcast(128), ph)
        ang, kk_, mm_ = scratch[:, 0, 0:T], scratch[:, 1, 0:T], scratch[:, 2, 0:T]
        t = vcopy(ang, posi[:, :], t_pos, ph)
        ts(ang, ang, C("freq"), None, ALU.mult, ALU.bypass)
        two_pi = 2.0 * math.pi
        MAGIC = 12582912.0

        def pieces(v, unit):
            res, rest = [], v
            for j in range(3):
                step = 2.0 ** (math.floor(math.log2(abs(v))) - 7 - 8 * j)
                q = math.floor(rest / step) * step
                if q:
                    res.append(q)
                rest -= q
            res.append(float(np.float32(rest)))
            return res

        for unit in (4096.0, 1.0):
            ts(kk_, ang, float(np.float32(1.0 / (two_pi * unit))), MAGIC, ALU.mult, ALU.add)
            ts(kk_, kk_, -MAGIC, None, ALU.add, ALU.bypass)
            for v in pieces(two_pi * unit, unit):
                stt(ang, kk_, -v, ang, ALU.mult, ALU.add)
        t = ts(ang, ang, math.pi, -math.pi, ALU.min, ALU.max)
        t1 = copy_act(cs[:, 1, :], ang, t, ph, func=ACT.Sin)
        t = stt(mm_, ang, -1.0, ang, ALU.mult, ALU.max)
        t = ts(mm_, mm_, -1.0, math.pi / 2, ALU.mult, ALU.add)
        t_cs = copy_act(cs[:, 0, :], mm_, t, ph, func=ACT.Sin)
        table(LN_EXP)
        cos2, sin2 = cs[:, 0, :], cs[:, 1, :]
        for k in range(3):
            s_free[k] = [t_cs, t]
        fill(QS[:, :, :], 0.0, ph)
        fill(QN[:, :, :], 0.0, ph)
        fill(VSB[:, :, :, :, :], 0.0)
        fill(VC[:, :, :], 0.0)
        t_z = dve.last()
        x_toks = norm("g_mix", h, M, T, 1, xh, xl, ph)

        def head_norm(src, sq_src, t_src, n, gain, dst, *waits):
            s = scratch[:, 3, 0:n]
            t = copy_act(s, src, t_src, s_free[3], func=ACT.Square)
            k_, ps, w = psum.take()
            t = mm(ps[:, 0:n], C("blk"), s, True, True, w, t, signal=True)
            t = copy_act(s, ps[:, 0:n], t, func=ACT.Ln, bias=1e-6)
            psum.free(k_, t)
            t = copy_act(s, s, t, func=ACT.Exp, scale=-0.5)
            t = stt(dst, src, gain, s, ALU.mult, ALU.mult, t, *waits)
            s_free[3] = [t]
            return t

        def normed_roped(gain, dsts, n=T, do_rope=True):
            def evac(k_, o, tok):
                i = xb_k[0]
                xb_k[0] ^= 1
                x_ = xb[:, i, 0:n]
                t = copy_act(x_, o[:, 0, :] if len(o.shape) == 3 else o, tok, xb_free[i], alone=False)
                psum.free(k_, t)
                if do_rope:
                    t = head_norm(x_, None, t, n, gain, x_)
                    a, b, c = rope(x_, t, n, cos2, sin2, dsts, ph, t_cs)
                    xb_free[i] = [a, b]
                else:
                    t = head_norm(x_, None, t, n, gain, x_)
                    for (p0, p1), dst in dsts:
                        t = vcopy(dst, xb[p0:p1, i, 0:n], ph)
                    xb_free[i] = [t]
            return evac

        for c in range(4):
            feature(x_toks, T, M, normed_roped(gq8, q_dsts(QN, c, (0, T))))
        for c in range(2):
            feature(x_toks, T, M, normed_roped(P_("g_ks") if c == 0 else P_("g_kw"), [((0, 128), KSW[:, c, :])]))

        def qs_evac(c):
            def evac(k_, o, tok):
                for (p0, p1), dst in q_dsts(QS, c, (0, T)):
                    t = copy_act(dst, o[p0:p1, 0, :], tok, ph, t_z, scale=0.125, alone=False)
                psum.free(k_, t)
            return evac

        def ks_evac(c):
            def evac(k_, o, tok):
                evac_copy(KS[:, c, :], o[:, 0, :], k_, tok, ph, q=dve)
            return evac
        for c in range(4):
            feature(x_toks, T, M, qs_evac(c))
        for c in range(4):
            feature(x_toks, T, M, ks_evac(c))
        starts2 = [M + 128 * i for i in range(4)]

        def vsw_evac(i, ps, tok):
            t = copy_act(VSW[:, i, :], ps[:, 0:256], tok, ph, alone=False)
            return [t, gate_exp(0, i, ps, tok)]

        def gate_exp(br, i, ps, tok):
            return copy_act(Gt[:, i, 8 * br:8 * br + 8], ps[:, 256:264], tok, ph, func=ACT.Exp, scale=-1.0, alone=False)
        token_tiles(x_toks, starts2, 264, vsw_evac)

        def vsb_evac(c):
            def evac(i, ps, tok):
                src = ps[:, 0:256].rearrange("p (a b d) -> p a b d", a=2, b=2)
                dst = VSB[:, i, 2 * c:2 * c + 2, 0:4:3, :]
                t = vcopy(dst, src, tok, t_z, alone=False)
                return [t, gate_exp(c + 1, i, ps, t)]
            return evac
        for c in range(2):
            token_tiles(x_toks, starts2, 264, vsb_evac(c))
        ts(Gt[:, :, :], Gt[:, :, :], 1.0, None, ALU.add, ALU.bypass, act.last())
        t_gt = recip(Gt[:, :, :], Gt[:, :, :])

        zz = fill(YH[:, :, 64:66, :].bitcast(F32), 0.0, ph, q=pool)
        zz = fill(YL[:, :, 64:66, :].bitcast(F32), 0.0, q=pool)
        x2_free, y_free = None, None
        for s in range(2):
            got = []
            feature(x_toks, T, M, lambda k_, o, tok: got.append((k_, o[:, 0, :], tok)))
            k_, src, tok = got[0]
            w = [tok, ph, x2_free]
            copy_act(X2[0:64, 0, :], src[0:64, :], *w)
            b = copy_act(X2[0:64, 1, :], src[64:128, :], *w)
            vcopy(X2[64:128, 0, 0:T - 1], src[0:64, 1:T], b, *w)
            d = vcopy(X2[64:128, 1, 0:T - 1], src[64:128, 1:T], b, *w)
            psum.free(k_, b, d)
            pe_ = P_("pe_k" if s == 0 else "pe_v")
            xin = X2[:, :, :].rearrange("p h (n j) -> p (h n) j", j=16)[:, :, 0:16:2]
            for v in range(2):
                u = tmpn[:, v, 0:512]
                t = tt(dve, u.rearrange("p (n j) -> p n j", j=8), xin,
                       pe_[:, 8 * v:8 * v + 8].unsqueeze(1).to_broadcast([128, 64, 8]), ALU.add, b, d, tmp_free[v])
                a, b_ = split(YH[:, v, 0:64, :].rearrange("p n j -> p (n j)"),
                              YL[:, v, 0:64, :].rearrange("p n j -> p (n j)"), u, t, y_free, ph)
                tmp_free[v] = [a, b_]
            x2_free = t
            ty = [a, b_, zz]
            k_, ps, w = psum.take()
            for v in range(2):
                for j0 in (0, 4):
                    c, hh, ll, tw = chunk()
                    for mt in range(2):
                        for jj in range(4):
                            j = j0 + jj
                            a0 = 256 * jj + 128 * mt
                            t = mm3(ps[:, 512 * mt:512 * mt + 64], (hh[:, a0:a0 + 128], ll[:, a0:a0 + 128]),
                                    (YH[:, v, v:v + 64, j], YL[:, v, v:v + 64, j]),
                                    v == 0 and j == 0, v == 1 and j == 7, w, tw, ty, signal=(jj == 3))
                    chunk_done(c, t)
            y_free = t
            t = copy_act(hid[:, s, :, :], ps[:, :].rearrange("p (a b) -> p a b", a=2)[:, :, 0:64], t, ph,
                         func=ACT.Gelu_apprx_tanh)
            psum.free(k_, t)
            t_hid = t
        table(LN_EXP)
        k_, ps, w = psum.take()
        for mt in range(2):
            t = mm(ps[:, 0:64], P_("w2k", 128 * mt, 128 * mt + 128), hid[:, 0, mt, :], mt == 0, mt == 1, w, t_hid,
                   signal=(mt == 1))
        i = xb_k[0]
        x_ = xb[:, i, 0:64]
        t = copy_act(x_, ps[:, 0:64], t, xb_free[i])
        psum.free(k_, t)
        t = head_norm(x_, None, t, 64, P_("g_kc"), x_)
        ce = small[:, 64:192].rearrange("p (c h n) -> p c h n", c=2, h=2)
        fill(small[:, 64:192], 0.0)
        for c in range(2):
            for hh in range(2):
                vcopy(ce[:, c, hh, 0:31],
                                                        cs[:, c, :].rearrange("p (n j) -> p n j", j=16)[:, 1:32, 15], t_cs)
        t = dve.last()
        a, b, c = rope(x_, t, 64, small[:, 64:128], small[:, 128:192],
                       [((0, 64), xb[0:64, i, 64:128]), ((64, 128), xb[64:128, i, 64:128])])
        vcopy(KC[0:64, :], xb[0:64, i, 64:96])
        t_kc = vcopy(KC[64:128, :], xb[64:128, i, 96:128])
        xb_free[i] = [t_kc, a, b]
        k_, ps, w = psum.take()
        for g in range(2):
            for mt in range(2):
                t = mm(ps[0:32, 64 * g:64 * g + 64], hid[:, 1, mt, 32 * g:32 * g + 32], P_("w2v", 64 * mt, 64 * mt + 64),
                       mt == 0, mt == 1, w, t_hid, signal=True)
        for m in range(8):
            r0, g = 32 * (m % 4), m % 2
            t_vc = vcopy(VC[r0:r0 + 32, m, :], ps[0:32, 64 * g:64 * g + 64], t, t_z)
        psum.free(k_, t_vc)
        cmp_.close()
        att = phase()
        attention_buffers("2", nsa, att)
        ao = []

        def compressed(i):
            oa, c0 = OA[:, i % 2, :], 128 * i
            sk, sps, sw = psum.take(1)
            for m in range(8):
                o = sps[:, 32 * m:32 * m + 32]
                mm(o, QN[:, m, c0:c0 + 128], KC[:, :], True, False, sw, att, t_c2)
                t = mm(o, ident, C("cmpadd", 32 * i, 32 * i + 32), False, True, signal=(m == 7))
            yield True
            S3 = sps[:, 0:256].rearrange("p (a b) -> p a b", a=8)
            Pv = scratch[:, 0, 0:256]
            P3 = Pv.rearrange("p (a b) -> p a b", a=8)
            mx = small[:, 32:40]
            reduce(mx, S3, ALU.max, t)
            t = tt(dve, P3, S3, mx.unsqueeze(2).to_broadcast([128, 8, 32]), ALU.subtract, cfree[0])
            psum.free(sk, t)
            t = copy_act(Pv, Pv, t, func=ACT.Exp)
            yield True
            tt(dve, P3, P3, C("cmp01", 32 * i, 32 * i + 32).unsqueeze(1).to_broadcast([128, 8, 32]), ALU.mult, t)
            reduce(mx, P3, ALU.add)
            ts(mx, mx, 1e-30, None, ALU.max)
            recip(mx, mx)
            tt(dve, mx, mx, Gt[:, i, 0:8], ALU.mult)
            t = tt(dve, P3, P3, mx.unsqueeze(2).to_broadcast([128, 8, 32]), ALU.mult)
            yield True
            r = flip_pe(None, t, [(0, 128), (128, 256)], src=Pv)
            cfree[0] = r[2]
            buf = scratch[:, 1, 0:256]
            t3 = copy_act(buf, r[1][:, 0:256], r[2], cfree[1], alone=False)
            psum.free(r[0], t3)
            yield True
            ok, ops, ow = psum.take(1)
            for m in range(8):
                tv = mm(ops[:, 64 * m:64 * m + 64], buf[:, 128 * (m // 4):128 * (m // 4) + 128], VC[:, m, :],
                        True, True, ow, t3, signal=(m == 7))
            cfree[1] = tv
            yield True
            t = copy_act(oa, ops[:, 0:512], tv, oa_free[0])
            oa_tok[0] = t
            psum.free(ok, t)

        cfree = [None, None]
        oa_tok = [None]
        nsa_out = {}

        def nsa_unit(i, br, m):
            c0 = 128 * i
            n = 128 * (i + 1)
            blocks = [(128 * j, 128 * j + 128) for j in range(i + 1)]

            def score():
                return scores(QN[:, m, c0:c0 + 128], lambda a, b: KSW[:, br, a:b], n, False, None, causalR, [att])

            def pv(buf, t3):
                if m == 0:
                    nsa_out[(i, br)] = psum.take(1)
                ok, ops, ow = nsa_out[(i, br)]
                a = 128 * br + 64 * (m % 2)
                for j in range(i + 1):
                    tv = mm(ops[:, 64 * m:64 * m + 64], buf[:, 128 * j:128 * j + 128], VSW[:, j, a:a + 64],
                            j == 0, j == i, ow, t3, signal=(j == i))
                return tv

            def end(tok):
                ok, ops, ow = nsa_out[(i, br)]
                oa = OA[:, i % 2, :]
                r = rr[:, br, 0:8]
                rs_free[br] = ts(rs[:, br, 0:8], rs[:, br, 0:8], 1e-30, None, ALU.max, ALU.bypass, tok)
                rs_free[br] = recip(r, rs[:, br, 0:8])
                tt(dve, r, r, Gt[:, i, 8 * (br + 1):8 * (br + 1) + 8], ALU.mult)
                u = scratch[:, 2, 0:512]
                t = tt(dve, u.rearrange("p (a b) -> p a b", a=8), ops[:, 0:512].rearrange("p (a b) -> p a b", a=8),
                       r.unsqueeze(2).to_broadcast([128, 8, 64]), ALU.mult, tok)
                psum.free(ok, t)
                t = tt(dve, oa, oa, u, ALU.add, oa_tok[0])
                if br:
                    yield True
                    yield from finish_tile(oa, t, 128, 8, None, False, 4, 0, M + c0, None, None, ao, lambda t: None, att)

            def job(p, t):
                return dict(p=p, t=t, blocks=blocks, pv=pv, end=end if m == 7 else None)
            u = dict(ahead=2, score=score, sum=rs[:, br, m:m + 1], sum_waits=lambda: [rs_free[br]], job=job)
            if br == 0 and m == 0:
                u["start"] = lambda: compressed(i)
            return u

        attention([nsa_unit(i, br, m) for i in range(4) for br in range(2) for m in range(8)])

        nsa.close()
        att = phase()
        strictR = sb("strictR", [128, 128], F32R, at=two)[:, :]
        t_strict = copy_act(strictR, C("strictT"), att, t_c2)
        SPb = sb("SPb", [128, 2, 4, T], at=two)
        Ab = sb("Ab", [128, 2, 4, T], at=two)
        RT = sb("RT", [128, 2, T], at=two)
        sp_free = [[], []]
        rt_free = [None, None]
        af = [[], []]
        opair = {}
        st = {}

        def sb_scores(hd_, j):
            k_, ps, w = psum.take(1)
            q0 = 128 * j
            mm(ps[:, 0:T - q0], KS[:, hd_ // 2, q0:q0 + 128], QS[:, hd_, q0:T], True, False, w, att)
            t = mm(ps[:, 0:128], identR[:, :], strictR, False, True, t_strict, signal=True)
            st[(hd_, j)] = [k_, ps, t]

        def sb_softplus(hd_, j):
            k_, ps, t = st[(hd_, j)]
            u, n = hd_ % 2, T - 128 * j
            o, e_, sp = ps[:, 0:n], Ab[:, u, j, 0:n], SPb[:, u, j, 0:n]
            t = copy_act(e_, o, t, af[u], func=ACT.Abs, alone=False)
            t = copy_act(e_, e_, t, func=ACT.Exp, scale=-1.0, alone=False)
            t = copy_act(e_, e_, t, func=ACT.Ln, bias=1.0, alone=False)
            t = stt(sp, o, 0.0, e_, ALU.max, ALU.add, t, sp_free[u], alone=False)
            st[(hd_, j)].append(t)

        def sb_suffix(hd_, j):
            k_, ps, _, t_sp = st[(hd_, j)]
            u, q0 = hd_ % 2, 128 * j
            n = T - q0
            sp = SPb[:, u, j, 0:n]
            t2 = mm(ps[:, 0:n], C("tri"), sp, False, True, t_sp, signal=True, onto=True)
            if j < 3:
                t2 = mm(ps[:, 128:n], C("negone"), RT[:, u, q0 + 128:T], False, True, rt_tok[u], signal=True, onto=True)
            if j == 3:
                rt_tok[u] = vcopy(RT[:, u, 384:512], sp, rt_free[u], t_sp, alone=False)
            elif j:
                vcopy(RT[:, u, q0:q0 + 128], sp[:, 0:128], t2, alone=False)
                rt_tok[u] = tt(dve, RT[:, u, q0 + 128:T], RT[:, u, q0 + 128:T], sp[:, 128:n], ALU.add, t2, rt_tok[u],
                               alone=False)
            else:
                rt_free[u] = t2
                sp_free[u] = [t2, rt_tok[u]]
            st[(hd_, j)].append(t2)

        def sb_exp(hd_, j):
            k_, ps, _, _, t2 = st[(hd_, j)]
            u, n = hd_ % 2, T - 128 * j
            t3 = copy_act(Ab[:, u, j, 0:n], ps[:, 0:n], t2, func=ACT.Exp, alone=False)
            psum.free(k_, t3)
            st[(hd_, j)].append(t3)

        def sb_values(hd_):
            u, tile_ = hd_ % 2, hd_ // 2
            if u == 0:
                opair[tile_] = psum.take(1)
            ok, ops, ow = opair[tile_]
            for j in range(4):
                vt = VSB[:, j, tile_, 0:2, :] if u == 0 else VSB[:, j, tile_, 2:4, :]
                t = mm(ops[:, 128 * j:T], vt.rearrange("p a b -> p (a b)"), Ab[:, u, j, 0:T - 128 * j],
                       u == 0 and j == 0, u == 1 and j == 3, ow, st[(hd_, 0)][5], signal=(j == 3))
            af[u] = [t]
            if u:
                f = flip[0]
                flip[0] ^= 1
                t = copy_act(fin[:, f, 0:512], ops[:, 0:512], t, fin_free[f], alone=False)
                psum.free(ok, t)
                a, b = split(xh[:, 4 + tile_, M:L], xl[:, 4 + tile_, M:L], fin[:, f, 0:512], t, att)
                fin_free[f] = [a, b]
                ao.extend([a, b])

        rt_tok = [None, None]
        seq = [(a, j) for a in range(8) for j in (3, 2, 1, 0)]
        sb_scores(*seq[0])
        sb_scores(*seq[1])
        for k in range(len(seq) + 2):
            if k < len(seq):
                sb_softplus(*seq[k])
            if 1 <= k <= len(seq):
                sb_suffix(*seq[k - 1])
            if k + 2 < len(seq):
                sb_scores(*seq[k + 2])
            if 1 <= k <= len(seq):
                sb_exp(*seq[k - 1])
            if k >= 2 and seq[k - 2][1] == 0:
                sb_values(seq[k - 2][0])

        def res2(c):
            def evac(k_, o, tok):
                dst = h[:, c, M:L]
                t = tt(dve, dst, dst, o[:, 0, :], ALU.add, tok, alone=False)
                psum.free(k_, t)
            return evac
        for c in range(8):
            feature([ao] * KT, T, M, res2(c))
        two.close()

        mem = ExitStack()
        hm = sb("hm", [128, KT, 256], at=mem)
        mh = sb("mh", [128, KT, 256], F32R, at=mem)
        ml = sb("ml", [128, KT, 256], F32R, at=mem)
        KM = sb("KM", [128, 2, 256], at=mem)
        VM = sb("VM", [128, 2, 256], at=mem)
        QM = sb("QM", [128, 4, T], at=mem)
        ph = phase()
        attention_buffers("3", mem, ph)
        fill(QM[:, :, :], 0.0, ph)
        t_mem = load("d_mem", hm[:, :, :], memT, ph)
        x_toks = norm("g_memx", h, M, T, 1, xh, xl, ph)
        m_toks = norm("g_memkv", hm, 0, 256, 1, mh, ml, t_mem, ph)
        for c in range(2):
            feature(x_toks, T, M, normed_roped(gmq8, q_dsts(QM, c, (0, T)), do_rope=False))
        for c in range(2):
            feature(m_toks, 256, 0, normed_roped(P_("g_mk"), [((0, 128), KM[:, c, :])], n=256, do_rope=False),
                    xt=(mh, ml))

        def vm_evac(i, ps, tok):
            return copy_act(VM[:, i, :], ps[:, 0:256], tok, ph, alone=False)
        token_tiles(m_toks, [0, 128], 256, vm_evac, xt=(mh, ml))
        att = phase()
        ao = []
        mem_out = {}

        def mem_unit(i, m):
            c0 = 128 * i

            def score():
                return scores(QM[:, m, c0:c0 + 128], lambda a, b: KM[:, m // 2, a:b], 256, False, None, None, [att])

            def pv(buf, t3):
                if m == 0:
                    mem_out[i] = psum.take(1)
                ok, ops, ow = mem_out[i]
                for j in range(2):
                    tv = mm(ops[:, 64 * m:64 * m + 64], buf[:, 128 * j:128 * j + 128], VM[:, j, 64 * m:64 * m + 64],
                            j == 0, j == 1, ow, t3, signal=(j == 1))
                return tv

            def end(tok):
                ok, ops, ow = mem_out[i]
                r = rr[:, i % 2, 0:4]
                rs_free[i % 2] = recip(r, rs[:, i % 2, 0:4], tok)
                yield from finish_tile(ops[:, 0:256], tok, 128, 4, r.unsqueeze(2).to_broadcast([128, 4, 64]), False, 2, 0,
                                       M + c0, None, None, ao, lambda t: psum.free(ok, t), att)

            def job(p, t):
                return dict(p=p, t=t, blocks=[(0, 128), (128, 256)], pv=pv, end=end if m == 3 else None)
            return dict(ahead=2, score=score, sum=rs[:, i % 2, m:m + 1], sum_waits=lambda: [rs_free[i % 2]], job=job)

        attention([mem_unit(i, m) for i in range(4) for m in range(4)])
        for half in range(2):
            c, hh, ll, tw = chunk()
            for mm_i in range(4):
                m = 4 * half + mm_i

                def wt(part, k, m=mm_i, hh=hh, ll=ll):
                    return (hh, ll)[part][:, 512 * k + 128 * m:512 * k + 128 * m + 128]
                k_, o, tok = tile_feature(wt, (xh, xl), [ao] * 2, T, M, tw, nk=2)
                t = tt(dve, h[:, m, M:L], h[:, m, M:L], o[:, 0, :], ALU.add, tok, alone=False)
                psum.free(k_, t)
            chunk_done(c, tok)
        mem.close()

        ffn("g_ffn2", phase())
        s_out = sem("d_out")
        sync(lambda e: e.dma_start(out, h[:, :, M:L]).then_inc(s_out, 16), dve.last(), alone=False, signal=False)
        sync(lambda e: e.wait_ge(s_out, 16), alone=False, signal=False)
        assert at["use"] == len(sizes)

        block = ctx.enter_context(nc.Block())

        @block.sync
        def _(e):
            sync.emit(e)

        @block.scalar
        def _(e):
            act.emit(e)

        @block.vector
        def _(e):
            dve.emit(e)

        @block.gpsimd
        def _(e):
            pool.emit(e)

        @block.tensor
        def _(e):
            pe.emit(e)


def constants():
    c = np.zeros((128, NCONST), np.float32)

    def put(name, v):
        c[:, CONST[name][0]:CONST[name][1]] = v
    i = np.arange(128)
    put("ident", np.eye(128))
    put("mean", 1.0 / D)
    put("blk", (i[:, None] // 64 == i[None, :] // 64) / 64.0)
    rot = np.zeros((128, 128))
    for b in (0, 64):
        for d in range(8):
            rot[b + d + 8, b + d] = -1.0
            rot[b + d, b + d + 8] = 1.0
    put("rot", rot)
    put("causal", np.where(i[None, :] > i[:, None], NEG, 0.0))
    put("strictT", np.where(i[:, None] >= i[None, :], NEG, 0.0))
    put("chunk", np.where((i[None, 64:] >= 64) & (i[:, None] < 64), NEG, 0.0))
    put("tri", np.where(i[:, None] >= i[None, :], -1.0, 0.0))
    put("negone", -1.0)
    n = np.arange(32)
    q = i[:, None, None] + 128 * np.arange(4)[None, :, None]
    seen = (16 * n[None, None, :] + 31 <= q) & (n[None, None, :] < 31)
    put("cmpadd", np.where(seen, 0.0, NEG).reshape(128, 128))
    put("cmp01", np.where(seen, 1.0, 0.0).reshape(128, 128))
    d = i % 64
    theta = np.float32(500000.0)
    f8 = theta ** (-np.arange(0, 16, 2, dtype=np.float32) / np.float32(16))
    put("freq", np.where(d < 16, f8[d % 8], 0.0)[:, None])
    inv = (np.float32(1.0) / (theta ** (np.arange(0, 16, 2, dtype=np.float32) / np.float32(16)))).astype(np.float32)
    ang = np.where(d < 16, inv[d % 8], 0.0).astype(np.float32)[:, None] * np.arange(L, dtype=np.float32)[None, :]
    put("cos", np.cos(ang.astype(np.float64)))
    put("sin", np.sin(ang.astype(np.float64)))
    return c


def rows(w):
    return w.reshape(w.shape[0] // 128, 128, w.shape[1]).transpose(1, 0, 2)


def by_cols(w, width=128):
    r = rows(w)
    return [r[:, :, a:a + width].reshape(-1) for a in range(0, w.shape[1], width)]


def by_halves(w):
    r = rows(w)
    return [r[:, 0:4].reshape(-1), r[:, 4:8].reshape(-1)]


def pieces_of(w, sizes):
    at, out = 0, []
    for n in sizes:
        out.append(w[:, at:at + n])
        at += n
    return out


def weights(a):
    out = []
    for l in range(2):
        dq, dk, dv, dg, fq, fk, fv, ff, fg = pieces_of(a["w_in"][l], (512,) * 7 + (8, 512))
        out += by_cols(dq) + by_cols(dk)
        out += by_halves(dv[:, 0:256]) + by_halves(dv[:, 256:512])
        out += by_cols(fq) + by_cols(fk)
        out += by_halves(fv[:, 0:256]) + by_halves(np.concatenate([fv[:, 256:512], ff], axis=1))
        out += by_cols(dg) + by_cols(fg)
        out += by_cols(a["w_out"][l])

    def ffn(wg, wu, wd):
        r = []
        for g, u in zip(by_cols(wg), by_cols(wu)):
            r += [g, u]
        d = rows(wd)
        for m in range(8):
            for f0, f1 in ((0, 8), (8, 16), (16, 22)):
                r.append(d[:, f0:f1, 128 * m:128 * m + 128].reshape(-1))
        return r
    out += ffn(a["ffn1_wg_2"][0], a["ffn1_wu_2"][0], a["ffn1_wd_2"][0])
    q, kc, vc, ks, vs, kw, vw, gt, qs, kk, vv = pieces_of(a["w_in_2"][0], (512,) + (128,) * 6 + (24, 512, 512, 512))
    heads = [m // 2 + 4 * (m % 2) for m in range(8)]
    out += by_cols(q.reshape(D, 8, 64)[:, heads].reshape(D, 512))
    out += by_cols(ks) + by_cols(kw) + by_cols(qs) + by_cols(kk)
    gt = gt.reshape(D, 8, 3)[:, heads].transpose(0, 2, 1).reshape(D, 24)
    for c, v in enumerate(([vs, vw], [vv[:, 0:256]], [vv[:, 256:512]])):
        out += by_halves(np.concatenate(v + [gt[:, 8 * c:8 * c + 8]], axis=1))
    for w, name in ((kc, "cmp_w1_k_2"), (vc, "cmp_w1_v_2")):
        out += by_cols(w)
        r = rows(a[name][0])
        out += [r[:, j:j + 4].reshape(-1) for j in range(0, 16, 4)]
    wo = a["w_out_2"][0]
    out += by_cols(np.concatenate([wo[0:512].reshape(8, 64, D)[heads].reshape(512, D), wo[512:]], axis=0))
    out += by_cols(a["mem_wq_2"][0]) + by_cols(a["mem_wk_2"][0]) + by_halves(a["mem_wv_2"][0])
    out += by_cols(a["mem_wo_2"][0], 512)
    out += ffn(a["ffn2_wg_2"][0], a["ffn2_wu_2"][0], a["ffn2_wd_2"][0])
    return np.concatenate(out)


def params(a):
    parts = {}

    def col(g):
        return g.reshape(8, 128).T
    parts["g_norm0"], parts["g_norm1"] = col(a["norm_gain"][0]), col(a["norm_gain"][1])
    parts["g_final"] = col(a["final_gain"])
    for n, k in (("g_ffn1", "ffn1_norm_2"), ("g_mix", "mix_norm_2"), ("g_memx", "mem_x_norm_2"),
                 ("g_memkv", "mem_kv_norm_2"), ("g_ffn2", "ffn2_norm_2")):
        parts[n] = col(a[k][0])
    for l in range(2):
        parts[f"g_sub{l}"] = a["subln_gain"][l][:, None]
        parts[f"fb{l}"] = np.broadcast_to(a["forget_bias"][l][None, :], (128, 8))
        parts[f"lam{l}"] = np.stack([np.concatenate([a["lambda_q1"][l], a["lambda_q2"][l]]),
                                     np.concatenate([a["lambda_k1"][l], a["lambda_k2"][l]])], axis=1)
    for n, k in (("g_q", "nsa_q_norm_2"), ("g_kc", "nsa_kc_norm_2"), ("g_ks", "nsa_ks_norm_2"),
                 ("g_kw", "nsa_kw_norm_2"), ("g_mq", "mem_q_norm_2"), ("g_mk", "mem_k_norm_2")):
        parts[n] = np.concatenate([a[k][0], a[k][0]])[:, None]
    for n, k in (("pe_k", "cmp_pos_k_2"), ("pe_v", "cmp_pos_v_2")):
        parts[n] = a[k][0].reshape(16, 128).T
    w2 = rows(a["cmp_w2_k_2"][0])
    parts["w2k"] = np.concatenate([w2, w2], axis=2).reshape(128, 256)
    parts["w2v"] = rows(a["cmp_w2_v_2"][0]).reshape(128, 128)
    return np.concatenate([parts[n] for n in PARAM], axis=1)


def kernel(**inputs):
    import concourse.bacc as bacc
    from concourse.bass_utils import run_bass_kernel_spmd as run

    a = {k: np.asarray(v) for k, v in inputs.items()}
    hT = np.concatenate([a["meta_tokens"], a["x"][0]], axis=0).T
    arrays = {
        "wstream": weights(a),
        "xT": rows(hT),
        "memT": rows(a["mem_2"][0].T),
        "pos": a["positions_2"].reshape(T),
        "const": constants(),
        "param": params(a),
    }
    arrays = {k: np.ascontiguousarray(v) for k, v in arrays.items()}
    nc = bacc.Bacc("TRN2", target_bir_lowering=False, num_devices=1)
    args = [nc.dram_tensor(k, v.shape, mybir.dt.from_np(v.dtype), kind="ExternalInput").ap() for k, v in arrays.items()]
    args.append(nc.dram_tensor("out", (128, KT, T), F32, kind="ExternalOutput").ap())
    program(nc, *args)
    r = run(nc, [arrays], core_ids=[0])
    got = r.results[0]["out"]
    return got.transpose(2, 1, 0).reshape(1, T, D)
```

```python
import math
from contextlib import ExitStack

import numpy as np

import concourse.bass as bass
from concourse import mybir

F32 = mybir.dt.float32
F32R = mybir.dt.float32r
I32 = mybir.dt.int32
ALU = mybir.AluOpType
ACT = mybir.ActivationFunctionType
AX = mybir.AxisListType

D = 1024
T = 512
M = 16
L = M + T
KT = 8
FT = 22
NEG = -(2.0 ** 100)
CW = 1056
LN_EXP = "natural_log_exp_and_others"



def chunk_sizes():
    ffn = [1024] * (2 * FT) + [1024, 1024, 768] * 8
    s = []
    for _ in range(2):
        s += [1024] * 16 + [1024] * 6 + [1056] * 2 + [1024] * 8
        s += [1024] * 8
    s += ffn
    s += [1024] * 2 + [1024, -1024] * 8 + [1024] * 2 + [1056] * 6 + [1024] * 4
    s += [1024] * 8
    s += [1024] * 6 + [1024] * 2
    s += ffn
    return s


CONST = {}
_n = 0
for _name, _w in [("ident", 128), ("causal", 128), ("chunk", 64), ("pick", 8),
                  ("mean", 128), ("blk", 128), ("rot", 128), ("freq", 1), ("cos", L), ("sin", L),
                  ("strictT", 128), ("tri", 128), ("negone", 128), ("cmpadd", 128), ("cmp01", 128)]:
    CONST[_name] = (_n, _n + _w)
    _n += _w
NCONST = _n
NC0 = CONST["mean"][0]
NC1 = CONST["strictT"][0]

PARAM = {}
_n = 0
for _name, _w in [("g_norm0", 8), ("g_norm1", 8), ("g_final", 8), ("g_ffn1", 8), ("g_mix", 8),
                  ("g_memx", 8), ("g_memkv", 8), ("g_ffn2", 8), ("g_sub0", 1), ("g_sub1", 1),
                  ("g_q", 1), ("g_kc", 1), ("g_ks", 1), ("g_kw", 1), ("g_mq", 1), ("g_mk", 1),
                  ("fb0", 8), ("fb1", 8), ("lam0", 2), ("lam1", 2), ("pe_k", 16), ("pe_v", 16),
                  ("w2k", 256), ("w2v", 128)]:
    PARAM[_name] = (_n, _n + _w)
    _n += _w
NPARAM = _n


class Queue:

    def __init__(self, sem):
        self.sem, self.n, self.items = sem, 0, []

    def last(self):
        return (self.sem, self.n) if self.n else None

    def __call__(self, fn, *waits, alone=True, signal=True):
        w = list(waits)
        if alone:
            w.append(self.last())
        if signal:
            self.n += 1
        self.items.append((w, fn, signal))
        return (self.sem, self.n)

    def emit(self, eng):
        seen = {}
        for waits, fn, signal in self.items:
            need = {}
            flat = list(waits)
            while flat:
                t = flat.pop()
                if t is None:
                    continue
                if isinstance(t, list):
                    flat += t
                    continue
                s, v = t
                if seen.get(s, 0) < v:
                    need[s] = max(need.get(s, 0), v)
            for s, v in need.items():
                eng.wait_ge(s, v)
                seen[s] = v
            r = fn(eng)
            if signal:
                r.then_inc(self.sem, 1)


class Ring:

    def __init__(self, count):
        self.rel = [[] for _ in range(count)]
        self.held = [False] * count
        self.age = list(range(count))
        self.now = count

    def take(self, n=1):
        spans = [k for k in range(len(self.rel) - n + 1) if not any(self.held[k:k + n])]
        k = min(spans, key=lambda k: max(self.age[k:k + n]))
        for i in range(k, k + n):
            self.held[i] = True
        return k, [t for r in self.rel[k:k + n] for t in r]

    def free(self, k, n, *toks):
        for i in range(k, k + n):
            self.rel[i], self.held[i], self.age[i] = list(toks), False, self.now
        self.now += 1


def program(nc, wstream, xT, memT, pos, const, param, out):
    sizes = chunk_sizes()
    whole = [n < 0 for n in sizes]
    sizes = [abs(n) for n in sizes]
    offs = [0]
    for s in sizes:
        offs.append(offs[-1] + 128 * s)

    ctx = ExitStack()
    with ctx:
        def sem(name):
            return ctx.enter_context(nc.semaphore(name))

        def sb(name, shape, dt=F32, at=None):
            return (at or ctx).enter_context(nc.sbuf_tensor(name, shape, dt))

        pe = Queue(sem("s_pe"))
        dve = Queue(sem("s_dve"))
        act = Queue(sem("s_act"))
        pool = Queue(sem("s_pool"))
        sync = Queue(sem("s_sync"))

        h = sb("h", [128, KT, L])
        xh = sb("xh", [128, KT, L], F32R)
        xl = sb("xl", [128, KT, L], F32R)
        NRAW, NW = 2, 2
        raw = [sb(f"raw{i}", [128, CW]) for i in range(NRAW)]
        wh = [sb(f"wh{i}", [128, CW], F32R) for i in range(NW)]
        wl = [sb(f"wl{i}", [128, CW], F32R) for i in range(NW)]
        cst = sb("cst", [128, NC1 - NC0])
        identR = sb("identR", [128, 128], F32R)
        maskR = sb("maskR", [128, 200], F32R)
        ident = identR[:, :].bitcast(F32)
        causalR, chunkR, pickR = maskR[:, 0:128], maskR[:, 128:192], maskR[:, 192:200]
        xb = sb("xb", [128, 2, L])
        cst2 = [None]
        par = sb("par", [128, NPARAM])
        small = sb("small", [128, 256])
        PS = ctx.enter_context(nc.psum_tensor("ps", [128, 8 * 512], F32))
        banks = Ring(8)
        span = {}

        class psum:

            @staticmethod
            def take(n=2):
                k, w = banks.take(n)
                span[k] = n
                return k, PS[:, 512 * k:512 * (k + n)], w

            @staticmethod
            def free(k, *toks):
                banks.free(k, span[k], *toks)

        def C(name, a=None, b=None):
            lo, hi = CONST[name]
            if lo >= NC1:
                return cst2[0][:, lo - NC1:hi - NC1] if a is None else cst2[0][:, lo - NC1 + a:lo - NC1 + b]
            return cst[:, lo - NC0:hi - NC0] if a is None else cst[:, lo - NC0 + a:lo - NC0 + b]

        def P_(name, a=None, b=None):
            lo, hi = PARAM[name]
            return par[:, lo:hi] if a is None else par[:, lo + a:lo + b]

        def load(name, dst, src, *waits):
            s = sem(name)
            sync(lambda e: e.dma_start(dst, src).then_inc(s, 16), *waits, alone=False, signal=False)
            return (s, 16)

        t_mats = load("d_mats", xb[:, 0, 0:NC0], const[:, 0:NC0])
        t_x = [load(f"d_x{i}", h[:, 2 * i:2 * i + 2, :], xT[:, 2 * i:2 * i + 2, :]) for i in range(4)]

        rawsem = [sem(f"d_raw{i}") for i in range(NRAW)]
        rawfree = [[] for _ in range(NRAW)]
        wfree = [[] for _ in range(NW)]
        loaded, parts = {}, {}
        at = {"load": 0, "split": 0, "part": 0, "done": 0, "use": 0}
        rawheld = [False] * NRAW

        def load_chunk():
            c = at["load"]
            r = c % NRAW
            if c >= len(sizes) or rawheld[r]:
                return False
            at["load"] += 1
            src = wstream[offs[c]:offs[c + 1]].rearrange("(p n) -> p n", p=128)
            sync(lambda e: e.dma_start(raw[r][:, 0:sizes[c]], src).then_inc(rawsem[r], 16),
                 rawfree[r], alone=False, signal=False)
            loaded[c] = (rawsem[r], 16 * (c // NRAW + 1))
            rawheld[r] = True
            return True

        def load_ahead():
            while load_chunk():
                pass

        load_ahead()
        t_cst = load("d_cst", cst[:, :], const[:, NC0:NC1])
        t_par = load("d_par", par[:, :], param)

        def split_chunk():
            c = at["split"]
            while c < len(sizes) and whole[c]:
                c += 1
            load_ahead()
            if c not in loaded or at["part"] - at["done"] >= NW:
                return False
            at["split"] = c + 1
            r, w, n = c % NRAW, at["part"] % NW, sizes[c]
            at["part"] += 1
            a = act(lambda e: e.activation(wh[w][:, 0:n], raw[r][:, 0:n], ACT.Copy),
                    loaded[c], wfree[w], alone=False)
            b = pool(lambda e: e.tensor_tensor(wl[w][:, 0:n], raw[r][:, 0:n],
                                               wh[w][:, 0:n].bitcast(F32), ALU.subtract),
                     a, wfree[w], alone=False)
            rawfree[r] = [a, b]
            rawheld[r] = False
            parts[c] = (w, a, b)
            load_ahead()
            return True

        def chunk():
            c = at["use"]
            at["use"] += 1
            while split_chunk():
                pass
            w, a, b = parts[c]
            return c, wh[w], wl[w], [a, b]

        def chunk_done(c, tok):
            wfree[parts[c][0]] = [tok]
            at["done"] += 1
            split_chunk()

        def whole_chunk():
            c = at["use"]
            at["use"] += 1
            load_ahead()
            return c, raw[c % NRAW], loaded[c]

        def whole_done(c, tok):
            rawfree[c % NRAW] = [tok]
            rawheld[c % NRAW] = False
            load_ahead()

        def mm(out_, lhsT, rhs, start, stop, *waits, signal=False, onto=False):
            return pe(lambda e: e.matmul(out_, lhsT, rhs, start=start, stop=stop, skip_group_check=onto), *waits,
                      alone=False, signal=signal)

        def mm3(out_, ws, xs, start, stop, *waits, signal=False):
            mm(out_, ws[0], xs[0], start, False, *waits)
            mm(out_, ws[0], xs[1], False, False)
            return mm(out_, ws[1], xs[0], False, stop, signal=signal)

        def tr(out_, in_, *waits, signal=False):
            k = in_.shape[0]
            return pe(lambda e: e.transpose(out_, in_, ident[0:k, 0:k]), *waits,
                      alone=False, signal=signal)

        def copy_act(dst, src, *waits, scale=1.0, func=ACT.Copy, alone=True, **kw):
            return act(lambda e: e.activation(dst, src, func, scale=scale, **kw), *waits, alone=alone)

        def tt(q, dst, a, b, op, *waits, alone=True):
            return q(lambda e: e.tensor_tensor(dst, a, b, op), *waits, alone=alone)

        def stt(dst, a, s, b, op0, op1, *waits, alone=True):
            return dve(lambda e: e.scalar_tensor_tensor(dst, a, s, b, op0, op1), *waits, alone=alone)

        def ts(dst, a, s1, s2, op0, op1=ALU.bypass, *waits, q=None, alone=True):
            return (q or dve)(lambda e: e.tensor_scalar(dst, a, s1, s2, op0, op1), *waits, alone=alone)

        def vcopy(dst, src, *waits, alone=True):
            return dve(lambda e: e.tensor_copy(dst, src), *waits, alone=alone)

        def fill(dst, v, *waits, q=None, alone=True):
            return (q or dve)(lambda e: e.memset(dst, v), *waits, alone=alone)

        def reduce(dst, src, op, *waits, alone=True, **kw):
            return dve(lambda e: e.tensor_reduce(dst, src, AX.X, op, **kw), *waits, alone=alone)

        def recip(dst, src, *waits, alone=True):
            return dve(lambda e: e.reciprocal(dst, src), *waits, alone=alone)

        def scan(dst, ones, src, *waits):
            return dve(lambda e: e.tensor_tensor_scan(dst, ones, src, 0.0, ALU.mult, ALU.subtract), *waits)

        def table(name):
            return act(lambda e: e.preload_act_table_set(name), signal=False)

        fence = [None]

        def phase():
            fence[0] = [pe.last(), dve.last(), act.last(), pool.last()]
            return fence[0]

        for k in range(8):
            span[k] = 1
            psum.free(k, fill(PS[:, 512 * k:512 * k + 512], 0.0, alone=False))
        table(LN_EXP)
        copy_act(identR[:, :], xb[:, 0, 0:128], t_mats)
        t_ident = copy_act(maskR[:, :], xb[:, 0, 128:328])

        scratch = sb("scratch", [128, 4, L])
        s_free = [[] for _ in range(4)]
        rst = sb("rst", [128, L])
        rst_free = [None]

        sums = {}

        def square(k, src, *waits):
            n = src.shape[1]
            acc, sq = scratch[:, 2, 0:n], scratch[:, k % 2, 0:n]
            dst = acc if k == 0 else sq
            t = copy_act(dst, src, *waits, s_free[2] if k == 0 else s_free[k % 2], func=ACT.Square, alone=False)
            if 0 < k < KT - 1:
                t = tt(dve, acc, acc, sq, ALU.add, t, sums[k - 1], alone=False)
                s_free[k % 2] = [t]
            sums[k] = t

        gsums = {}

        def gained_square(k, src, *waits):
            acc = scratch[:, 3, 0:T]
            dst = xb[:, k % 2, 0:T] if k else acc
            t = copy_act(dst, src, *waits, xb_free[k % 2] if k else s_free[3], t_par, func=ACT.Square,
                         scale=P_("g_final", k, k + 1), alone=False)
            if k:
                t = tt(dve, acc, acc, dst, ALU.add, t, gsums[k - 1], alone=False)
                xb_free[k % 2] = t
            gsums[k] = t

        def rstd(n, halves, given=None):
            parts = [given] if given else [(scratch[:, 2, 0:n], sums[KT - 2], 2), (scratch[:, 1, 0:n], sums[KT - 1], 1)]
            k, ps, w = psum.take(halves)
            o = ps[:, :].rearrange("p (a b) -> p a b", a=halves)[:, :, 0:n // halves]
            m = n // halves
            for acc, t_acc, slot in parts:
                for i in range(halves):
                    t = mm(o[:, i, :], C("mean"), acc[:, i * m:(i + 1) * m],
                           slot != 1, slot != 2, w, t_acc, t_cst, signal=True)
                s_free[slot] = [t]
            r = rst[:, 0:n]
            t = copy_act(r.rearrange("p (a b) -> p a b", a=halves), o, t, rst_free[0], func=ACT.Ln, bias=1e-6,
                         alone=False)
            psum.free(k, t)
            return r, copy_act(r, r, t, func=ACT.Exp, scale=-0.5, alone=False)

        xb_free = [t_ident, None]
        tmpn = sb("tmpn", [128, 2, L])
        tmp_free = [None, None]

        def split(dst_h, dst_l, src, *waits):
            a = copy_act(dst_h, src, *waits, alone=False)
            b = tt(pool, dst_l, src, dst_h.bitcast(F32), ALU.subtract, a, *waits, alone=False)
            return a, b

        def norm(gain, src, c0, n, halves, dst_h, dst_l, *waits, sums=None, scale=None):
            r, t_r = scale or rstd(n, halves, sums)
            gains = P_(gain) if isinstance(gain, str) else gain
            toks = []
            late = []

            def low(q, k, dst, u, high, a, free, i):
                b = tt(q, dst, u, high, ALU.subtract, a, *waits, alone=False)
                free[i] = toks[k] = [a, b]
            for k in range(KT):
                buf, free = ((tmpn, tmp_free), (xb, xb_free))[k % 4 // 2]
                u, i = buf[:, k % 2, 0:n], k % 2
                t = stt(u, src[:, k, c0:c0 + n], gains[:, k:k + 1], r, ALU.mult, ALU.mult,
                        t_r, free[i], t_par, *waits, alone=False)
                while late:
                    low(*late.pop())
                dh, dl = dst_h[:, k, c0:c0 + n], dst_l[:, k, c0:c0 + n]
                a = copy_act(dh, u, t, *waits, alone=False)
                toks.append(None)
                args = (k, dl, u, dh.bitcast(F32), a, free, i)
                if k % 3 == 1:
                    late.append((dve,) + args)
                else:
                    low(pool, *args)
            while late:
                low(*late.pop())
            rst_free[0] = t
            return toks

        def tile_feature(wt, xt, x_toks, n, c0, tw, nk=KT, cols=None):
            halves = 2 if n > 512 else 1
            k_, ps, w = psum.take(halves)
            m = n // halves
            o = ps[:, :].rearrange("p (a b) -> p a b", a=halves)[:, :, 0:m]
            tok = None
            for i in range(halves):
                for k in range(nk):
                    a, b = c0 + i * m, c0 + (i + 1) * m
                    tok = mm3(o[:, i, :], (wt(0, k), wt(1, k)), (xt[0][:, k, a:b], xt[1][:, k, a:b]),
                              k == 0, k == nk - 1, w, tw, x_toks[k], signal=(k == nk - 1))
            return k_, o, tok

        def feature(x_toks, n, c0, evac, xt=None, steps=1):
            c, hh, ll, tw = chunk()

            def wt(part, k):
                return (hh, ll)[part][:, 128 * k:128 * k + 128]
            k_, o, tok = tile_feature(wt, xt or (xh, xl), x_toks, n, c0, tw)
            chunk_done(c, tok)
            for _ in range(steps):
                advance()
            more = evac(k_, o, tok)
            if more is not None:
                next(more)
                pending.append(more)

        pending = []

        def advance():
            pending[:] = [g for g in pending if next(g, None)]

        def token_tiles(x_toks, starts, ncols, evac, xt=None, between=None):
            xt = xt or (xh, xl)
            slots = [psum.take() for _ in range((len(starts) + 1) // 2)]
            toks = []
            for half in range(2):
                c, hh, ll, tw = chunk()
                for i, a in enumerate(starts):
                    k_, ps, w = slots[i // 2]
                    o = ps[:, 512 * (i % 2):512 * (i % 2) + ncols]
                    for kk in range(4):
                        k = 4 * half + kk
                        tok = mm3(o, (xt[0][:, k, a:a + 128], xt[1][:, k, a:a + 128]),
                                  (hh[:, ncols * kk:ncols * (kk + 1)], ll[:, ncols * kk:ncols * (kk + 1)]),
                                  k == 0, k == KT - 1, w, tw, x_toks[k], signal=(kk == 3))
                    toks.append(tok)
                chunk_done(c, tok)
                advance()
                if between is not None:
                    between()
            for i in range(len(starts)):
                k_, ps, w = slots[i // 2]
                t = evac(i, ps[:, 512 * (i % 2):512 * (i % 2) + ncols], toks[len(starts) + i])
                if i % 2:
                    psum.free(k_, prev, t)
                elif i == len(starts) - 1:
                    psum.free(k_, t)
                prev = t

        xb_k = [0]
        t1b = scratch

        def rope(src, t_src, n, cos, sin, dsts, *waits):
            i = xb_k[0]
            halves = 2 if n > 512 else 1
            k_, ps, w = psum.take(halves)
            m = n // halves
            o = ps[:, :].rearrange("p (a b) -> p a b", a=halves)[:, :, 0:m]
            for j in range(halves):
                t = mm(o[:, j, :], C("rot"), src[:, j * m:(j + 1) * m], True, True, w, t_src, signal=True)
            a = tt(dve, t1b[:, 0, 0:n], src, cos, ALU.mult, t_src, s_free[0], *waits)
            v = t1b[:, 1, 0:n]
            b = tt(dve, v.rearrange("p (a b) -> p a b", a=halves), o,
                   sin.rearrange("p (a b) -> p a b", a=halves), ALU.mult, t)
            psum.free(k_, b)
            for (p0, p1), dst in dsts:
                c = tt(dve, dst, t1b[p0:p1, 0, 0:n], t1b[p0:p1, 1, 0:n], ALU.add)
            return a, t, c

        def three(ap, n, halves):
            return ap.rearrange("p (a b) -> p a b", a=halves)

        NP, NT = 4, 2
        Pfree = [[] for _ in range(NP)]
        Pk = [0]
        nm = sb("nm", [128, 8])
        nmk = [0]
        nm_free = [None] * 8
        rs = sb("rs", [128, 2, 8])
        rr = sb("rr", [128, 2, 8])
        osb, fin = tmpn, xb
        fin_free, osb_free = xb_free, tmp_free
        flip = [0]
        bufs = {}

        def attention_buffers(name, scope, start):
            bufs["P"] = sb("Pb" + name, [128, NP, L], at=scope)
            bufs["T"] = [sb(f"PT{name}{i}", [128, 640], at=scope) for i in range(NT)]
            bufs["Tr"] = Ring(NT)
            for k in range(NP):
                Pfree[k] = list(start)
            for k in range(NT):
                bufs["Tr"].free(k, 1, *start)

        def scores(q_lhsT, k_rhs, nkeys, meta, extra, mask, t_in):
            o0 = 112 if meta else 0
            n = nkeys
            k_, ps, w = psum.take(2 if o0 + n > 512 else 1)
            first = min(n, 512 - o0)
            spans = [(0, first)] + ([(first, n)] if n > first else [])
            for a, b in spans:
                o = ps[:, o0 + a:o0 + b]
                lastpart = b == n
                terms = [(q_lhsT, r, o) for r in k_rhs(a, b)]
                if extra is not None:
                    terms += [(extra[0], r, o) for r in extra[1](a, b)]
                if mask is not None and lastpart:
                    mw = mask.shape[1]
                    terms.append((identR[:, :], mask, ps[:, o0 + n - mw:o0 + n]))
                for i, (l_, r_, o_) in enumerate(terms):
                    t = mm(o_, l_, r_, i == 0, i == len(terms) - 1, w, t_in, t_cst, t_ident,
                           signal=(lastpart and i == len(terms) - 1))
            return k_, ps[:, o0:o0 + n], t

        def row_max(k_, S, t):
            c = nmk[0]
            nmk[0] = (c + 1) % 8
            return c, reduce(nm[:, c:c + 1], S, ALU.max, t, nm_free[c], alone=False, negate=True)

        def row_exp(k_, S, c, t_max, rs_ap, *waits):
            p = Pk[0]
            Pk[0] = (p + 1) % NP
            a = copy_act(bufs["P"][:, p, 0:S.shape[1]], S, t_max, Pfree[p], *waits, func=ACT.Exp,
                         bias=nm[:, c:c + 1], accum_out=rs_ap, alone=False)
            nm_free[c] = a
            psum.free(k_, a)
            return p, a

        def flip_pe(p, t, cols, src=None):
            k_, ps, w = psum.take((len(cols) + 3) // 4)
            src = bufs["P"][:, p, :] if src is None else src
            for j, (a, b) in enumerate(cols):
                t2 = tr(ps[0:b - a, 128 * j:128 * j + 128], src[:, a:b], w, t, t_ident, signal=(j == len(cols) - 1))
            if p is not None:
                Pfree[p] = [t2]
            return k_, ps, t2, 128 * len(cols)

        def flip_copy(k_, ps, t2, n, q):
            i, w2 = bufs["Tr"].take()
            buf = bufs["T"][i]
            if q is dve:
                t3 = vcopy(buf[:, 0:n], ps[:, 0:n], t2, w2, alone=False)
            else:
                t3 = copy_act(buf[:, 0:n], ps[:, 0:n], t2, w2, alone=False)
            psum.free(k_, t3)
            return i, buf, t3

        def flip_free(i, tok):
            bufs["Tr"].free(i, 1, tok)

        def attention(units):
            nxt, S, mx, turn = 0, {}, {}, 0
            flips, pvs, later = [], [], []
            s = 0

            def more(s):
                nonlocal nxt
                while nxt < len(units) and nxt <= s + units[nxt]["ahead"]:
                    S[nxt] = units[nxt]["score"]()
                    nxt += 1
            more(-1)
            if 0 in S:
                mx[0] = row_max(*S[0])
            while s < len(units) or flips or pvs or later:
                got = None
                if s < len(units):
                    if s not in S:
                        more(s)
                        mx[s] = row_max(*S[s])
                    k_, S_, _ = S.pop(s)
                    c, t = mx.pop(s)
                    got = row_exp(k_, S_, c, t, units[s]["sum"], *units[s]["sum_waits"]())
                fl = [(f, flip_pe(f["p"], f["t"], f["blocks"])) for due, f in flips if due <= s]
                flips = [(due, f) for due, f in flips if due > s]
                more(s)
                for job, (i, buf, t3) in pvs:
                    tok = job["pv"](buf, t3)
                    flip_free(i, tok)
                    if job["end"] is not None:
                        later.append(job["end"](tok))
                if s + 1 in S:
                    mx[s + 1] = row_max(*S[s + 1])
                pvs = []
                for f, r in fl:
                    turn += 1
                    pvs.append((f, flip_copy(*r, dve if turn % f["every"] == 0 else act)))
                if s < len(units) and "start" in units[s]:
                    later.append(units[s]["start"]())
                if got is not None:
                    job = units[s]["job"](*got)
                    if job is not None:
                        flips.append((s + job.get("lag", 1), job))
                later = [g for g in later if next(g, False)]
                s += 1

        def finish_tile(o_ap, t_o, nq, heads, scale_bc, copy, ntile, dst_t0, col0, gate, gain, toks, used, *waits):
            f = flip[0]
            flip[0] ^= 1
            w_ = 128 * ntile
            d = osb[0:nq, f, 0:w_]
            if scale_bc is not None:
                t = tt(dve, d.rearrange("p (a b) -> p a b", a=heads), o_ap.rearrange("p (a b) -> p a b", a=heads),
                       scale_bc, ALU.mult, t_o, osb_free[f])
            elif copy:
                t = vcopy(d, o_ap, t_o, osb_free[f])
            else:
                d, t = o_ap, t_o
            used(t)
            yield True
            k_, ps, w = psum.take(1)
            for j in range(ntile):
                t2 = tr(ps[:, 128 * j:128 * j + nq], d[:, 128 * j:128 * j + 128], w, t, signal=(j == ntile - 1))
            if d is not o_ap:
                osb_free[f] = [t2]
            else:
                oa_free[0] = t2
            src = ps[:, 0:w_].rearrange("p (a b) -> p a b", a=ntile)[:, :, 0:nq]
            g = fin[:, f, 0:ntile * nq].rearrange("p (a b) -> p a b", a=ntile)
            if gate is None:
                t3 = vcopy(g, src, t2, fin_free[f])
            elif gain is None:
                t3 = tt(dve, g, src, gate, ALU.mult, t2, fin_free[f], *waits)
            else:
                for j in range(ntile):
                    t3 = stt(g[:, j, :], src[:, j, :], gain, gate[:, j, :], ALU.mult, ALU.mult, t2, fin_free[f], *waits,
                             alone=(j == 0))
            psum.free(k_, t3)
            yield True
            a, b = split(xh[:, dst_t0:dst_t0 + ntile, col0:col0 + nq], xl[:, dst_t0:dst_t0 + ntile, col0:col0 + nq],
                         g, t3, *waits)
            fin_free[f] = [a, b]
            toks += [a, b]

        rs_free = [None, None]
        oa_free = [None]

        def drain(gen):
            for _ in gen:
                pass

        lam_init = [0.8 - 0.6 * math.exp(-0.3 * l) for l in range(2)]
        neglam = [small[:, 8 * l + 5:8 * l + 6] for l in range(2)]
        gsub = [small[:, 8 * l + 6:8 * l + 7] for l in range(2)]
        fill(small[:, 0:64], 0.0)
        t_lam = [None]

        def lambdas():
            for l in range(2):
                b = 8 * l
                tt(dve, small[0:64, b:b + 1], P_(f"lam{l}", 0, 1)[0:64], P_(f"lam{l}", 1, 2)[0:64], ALU.mult, t_par)
                t = tt(dve, small[64:128, b + 1:b + 2], P_(f"lam{l}", 0, 1)[64:128], P_(f"lam{l}", 1, 2)[64:128],
                       ALU.mult)
                k_, ps, w = psum.take(1)
                t = mm(ps[:, 0:2], C("mean"), small[:, b:b + 2], True, True, w, t, t_cst, signal=True)
                t = copy_act(small[:, b + 2:b + 4], ps[:, 0:2], t, scale=1024.0, func=ACT.Exp)
                psum.free(k_, t)
                t = tt(dve, small[:, b + 4:b + 5], small[:, b + 3:b + 4], small[:, b + 2:b + 3], ALU.subtract, t)
                ts(neglam[l], small[:, b + 4:b + 5], -lam_init[l], None, ALU.add)
                ts(gsub[l], P_(f"g_sub{l}"), 1.0 - lam_init[l], None, ALU.mult)
            ts(gq8, P_("g_q"), 0.125, None, ALU.mult)
            t_lam[0] = ts(gmq8, P_("g_mq"), 0.125, None, ALU.mult)
        gq8, gmq8 = small[:, 16:17], small[:, 17:18]

        one = ExitStack()
        attention_buffers("1", one, [])
        QA = sb("QA", [128, 8, L], at=one)
        QB = sb("QB", [128, 8, L], at=one)
        KA = sb("KA", [128, 4, L], at=one)
        KB = sb("KB", [128, 4, L], at=one)
        VA = sb("VA", [128, 5, T], at=one)
        VB = sb("VB", [128, 5, T], at=one)
        G = sb("G", [128, 8, L], at=one)
        NCh = sb("NCh", [128, L], F32R, at=one)
        LF = sb("LF", [128, 3, 40], at=one)
        onesr = bufs["P"][0:8, 0, :]
        for k in range(8):
            a = 64 * (1 - k % 2)
            fill(QA[a:a + 64, k, :], 0.0, q=pool, alone=False)
            fill(QB[a:a + 64, k, :], 0.0, q=pool, alone=False)
        fill(NCh[:, :].bitcast(F32), 0.0, q=pool)
        t_b1 = fill(LF[:, :, :], 0.0, q=pool)

        def q_dsts(Q, tile, cols):
            return [((0, 64), Q[0:64, 2 * tile, cols[0]:cols[1]]), ((64, 128), Q[64:128, 2 * tile + 1, cols[0]:cols[1]])]

        starts = [0] + [M + 128 * i for i in range(4)]

        def evac_copy(dst, src, k_, tok, *waits, scale=1.0, q=None):
            t = copy_act(dst, src, tok, *waits, scale=scale, alone=False) if q is None else \
                vcopy(dst, src, tok, *waits, alone=False)
            psum.free(k_, t)
            return t

        for l in range(2):
            full = l == 0
            n_q, c_q = (L, 0) if full else (T, M)
            ph = phase()
            if l == 0:
                for k in range(KT):
                    square(k, h[:, k, :], t_x[k // 2])
                    if k == 3 or k == 5:
                        split_chunk()
            x_toks = norm(f"g_norm{l}", h, 0, L, 2, xh, xl, ph)
            halves_q = 2 if full else 1

            def roped(dsts, cos_cols, n, scale):
                def evac(k_, o, tok):
                    i = xb_k[0]
                    xb_k[0] ^= 1
                    x_ = xb[:, i, 0:n]
                    hv = 2 if n > 512 else 1
                    t = copy_act(three(x_, n, hv), o, tok, xb_free[i], scale=scale, alone=False)
                    psum.free(k_, t)
                    yield True
                    a, b, c = rope(x_, t, n, C("cos", *cos_cols), C("sin", *cos_cols), dsts, ph, t_cst)
                    xb_free[i] = [a, b]
                return evac

            cols = (c_q, c_q + n_q)

            def v_evac(V, c):
                def evac(i, ps, tok):
                    rows = 16 if i == 0 else 128
                    dst, src = V[0:rows, i, 256 * c:256 * c + 256], ps[0:rows, 0:256]
                    if i % 2:
                        return copy_act(dst, src, tok, ph, alone=False)
                    return vcopy(dst, src, tok, ph, alone=False)
                return evac

            def fq_evac(c):
                def evac(k_, o, tok):
                    for j, ((p0, p1), dst) in enumerate(q_dsts(QB, c, cols)):
                        t = copy_act(three(dst, n_q, halves_q), o[p0:p1, :, :], tok, ph, t_b1, scale=0.125, alone=False)
                    psum.free(k_, t)
                return evac

            def fk_evac(c):
                def evac(k_, o, tok):
                    evac_copy(three(KB[:, c, :], L, 2), o, k_, tok, ph, q=dve)
                return evac
            for c in range(4):
                feature(x_toks, n_q, c_q, roped(q_dsts(QA, c, cols), cols, n_q, 0.125))
                feature(x_toks, n_q, c_q, fq_evac(c))
            for c in range(4):
                feature(x_toks, L, 0, roped([((0, 128), KA[:, c, :])], (0, L), L, 1.0))
                feature(x_toks, L, 0, fk_evac(c))
            for c in range(2):
                token_tiles(x_toks, starts, 256, v_evac(VA, c))
            token_tiles(x_toks, starts, 256, v_evac(VB, 0))
            if full:
                lambdas()

            def last_v(i, ps, tok):
                rows = 16 if i == 0 else 128
                t = vcopy(VB[0:rows, i, 256:512], ps[0:rows, 0:256], tok, ph, alone=False)
                t2 = tt(dve, LF[0:rows, 0, 8 * i:8 * i + 8], ps[0:rows, 256:264], P_(f"fb{l}")[0:rows], ALU.add,
                        tok, ph, t_par)
                return [t, t2]
            token_tiles(x_toks, starts, 264, last_v)
            z_, a_, b_ = LF[:, 0, :], LF[:, 1, :], LF[:, 2, :]
            t = stt(a_, z_, -1.0, z_, ALU.mult, ALU.max)
            t = copy_act(a_, a_, t, func=ACT.Exp, scale=-1.0)
            t = copy_act(a_, a_, t, func=ACT.Ln, bias=1.0)
            t = stt(b_, z_, 0.0, a_, ALU.min, ALU.subtract, t)
            k_, ps, w = psum.take()
            tr(ps[0:8, 112:128], LF[0:16, 2, 0:8], w, t, t_ident)
            for i in range(4):
                t = tr(ps[0:8, 128 * (i + 1):128 * (i + 2)], LF[:, 2, 8 * i + 8:8 * i + 16], signal=(i == 3))
            fill(onesr, 1.0, Pfree[0])
            ncm = bufs["P"][0:8, 1, :]
            t = scan(ncm, onesr, ps[0:8, 112:640], t, Pfree[1])
            psum.free(k_, t)
            Pfree[0] = [t]
            t = copy_act(NCh[0:8, :], ncm, t, ph, t_b1)
            t_nc = tt(dve, NCh[32:40, :], ncm, NCh[0:8, :].bitcast(F32), ALU.subtract, t)
            Pfree[1] = t_nc

            ready = phase()

            def gate_evac(c):
                def evac(k_, o, tok):
                    t = copy_act(three(G[:, c, cols[0]:cols[1]], n_q, halves_q), o, tok, ph,
                                 func=ACT.Silu, alone=False)
                    psum.free(k_, t)
                return evac
            for c in range(8):
                feature(x_toks, n_q, c_q, gate_evac(c))
            table(LN_EXP)
            att = phase()
            ao_toks = {"diff": [], "fox": []}
            units = []

            def head_end(l, kind, i, ok, O, nq, c0, par_, t_pv, att):
                def used(t):
                    psum.free(ok, t)
                gate = G[:, 0:4, c0:c0 + nq] if kind == "diff" else G[:, 4:8, c0:c0 + nq]
                if kind == "diff":
                    f = flip[0]
                    sq = osb[0:nq, f, 0:512]
                    ms = small[0:nq, 48:52] if i >= 0 else small[0:nq, 56:60]
                    t = copy_act(sq, O, t_pv, osb_free[f], func=ACT.Square, alone=False)
                    yield True
                    t = reduce(ms, sq.rearrange("p (a b) -> p a b", a=4), ALU.add, t, alone=False)
                    yield True
                    if i >= 0:
                        q0 = small[:, 52:56]
                        recip(q0, rs[:, par_, 0:8:2])
                        rs_free[par_] = dve.last()
                        tt(dve, ms, ms, q0, ALU.mult)
                        t = tt(dve, ms, ms, q0, ALU.mult)
                    t = copy_act(ms, ms, t, func=ACT.Ln, scale=1.0 / 128, bias=1e-5, alone=False)
                    t = copy_act(ms, ms, t, func=ACT.Exp, scale=-0.5, alone=False)
                    yield True
                    if i >= 0:
                        t = tt(dve, ms, ms, q0, ALU.mult, t)
                    g = finish_tile(O, t, nq, 4, ms.unsqueeze(2).to_broadcast([nq, 4, 128]), False, 4, 0, c0, gate,
                                    gsub[l], ao_toks[kind], used, att)
                elif i < 0:
                    g = finish_tile(O, t_pv, nq, 8, None, True, 4, 4, c0, gate, None, ao_toks[kind], used, att)
                else:
                    recip(rr[:, par_, 0:8], rs[:, par_, 0:8], t_pv, alone=False)
                    rs_free[par_] = dve.last()
                    g = finish_tile(O, t_pv, nq, 8, rr[:, par_, 0:8].unsqueeze(2).to_broadcast([128, 8, 64]), False,
                                    4, 4, c0, gate, None, ao_toks[kind], used, att)
                yield from g

            outs = {}
            pair = []

            def unit(l, kind, i, m, Q, K, V, c0, ready, att, t_nc):
                par_ = (i + 1) % 2
                n = M + 128 * (i + 1)
                blocks = [(0, M)] + [(M + 128 * j, M + 128 * j + 128) for j in range(i + 1)]
                nh, hd = (4, 128) if kind == "diff" else (8, 64)

                def score():
                    ex = None
                    if kind == "fox":
                        ex = (pickR[:, m:m + 1].to_broadcast([128, 128]), lambda a, b: (NCh[:, a:b],))
                    return scores(Q[:, m, c0:c0 + 128], lambda a, b: [K[:, m // 2, a:b]], n, True, ex,
                                  causalR if kind == "fox" else chunkR, [ready, t_nc])

                def pv_of(hh):
                    def pv(buf, t3):
                        if hh == 0:
                            outs[(kind, i)] = psum.take(1)
                        ok, ops, ow = outs[(kind, i)]
                        for j, (a, b) in enumerate(blocks):
                            tv = mm(ops[:, hd * hh:hd * hh + hd], buf[0:b - a, 128 * j:128 * j + 128],
                                    V[0:b - a, j, hd * hh:hd * hh + hd], j == 0, j == len(blocks) - 1,
                                    ow, t3, signal=(j == len(blocks) - 1))
                        return tv
                    return pv

                def end(tok):
                    ok, ops, ow = outs[(kind, i)]
                    return head_end(l, kind, i, ok, ops[:, 0:512], 128, c0, par_, tok, att)

                def job(p, t):
                    if kind == "fox":
                        return dict(p=p, t=t, blocks=blocks, pv=pv_of(m), end=end if m == 7 else None, every=1000)
                    pair.append((p, t))
                    if m % 2 == 0:
                        return None
                    (p0, ta), (p1, tb) = pair
                    del pair[:]
                    q = rr[:, par_, m:m + 1]
                    P = bufs["P"]
                    recip(q, rs[:, par_, m:m + 1], ta, tb, alone=False)
                    t = stt(q, q, neglam[l], rs[:, par_, m - 1:m], ALU.mult, ALU.mult, t_lam[0])
                    t = stt(P[:, p0, 0:n], P[:, p1, 0:n], q, P[:, p0, 0:n], ALU.mult, ALU.add)
                    Pfree[p1] = [t]
                    return dict(p=p0, t=t, blocks=blocks, pv=pv_of(m // 2), end=end if m == 7 else None, lag=2, every=4)
                return dict(ahead=1 if i == 3 else 2, score=score, sum=rs[:, par_, m:m + 1],
                            sum_waits=lambda: [rs_free[par_]], job=job)

            def meta_queries(l, kind, Q, K, V, ready, att, t_nc):
                nh, hd = (4, 128) if kind == "diff" else (8, 64)
                sk, sps, sw = psum.take(1)
                for m in range(8):
                    o = sps[0:16, 16 * m:16 * m + 16]
                    if kind == "diff":
                        t = mm(o, Q[:, m, 0:16], K[:, m // 2, 0:16], True, True, sw, ready, signal=m == 7)
                    else:
                        mm(o, Q[:, m, 0:16], K[:, m // 2, 0:16], True, False, sw, ready)
                        mm(o, pickR[:, m:m + 1].bitcast(F32).to_broadcast([128, 16]),
                           NCh[:, 0:16].bitcast(F32), False, False, t_nc)
                        t = mm(o, ident[:, 0:16], causalR[:, 0:16].bitcast(F32), False, True, signal=m == 7)
                yield True
                S3 = sps[0:16, 0:128].rearrange("p (a b) -> p a b", a=8)
                Pv, PTv = rst[0:16, 0:128], rst[0:16, 128:256]
                P3 = Pv.rearrange("p (a b) -> p a b", a=8)
                mx = small[0:16, 32:40]
                t = reduce(mx, S3, ALU.max, t)
                t = tt(dve, P3, S3, mx.unsqueeze(2).to_broadcast([16, 8, 16]), ALU.subtract, t, rst_free[0])
                psum.free(sk, t)
                t = copy_act(Pv, Pv, t, func=ACT.Exp, alone=False)
                yield True
                t = reduce(mx, P3, ALU.add, t)
                t = recip(mx, mx)
                t = tt(dve, P3, P3, mx.unsqueeze(2).to_broadcast([16, 8, 16]), ALU.mult)
                if kind == "diff":
                    P4 = Pv.rearrange("p (a m b) -> p a m b", a=4, m=2)
                    t = stt(P4[:, :, 0, :], P4[:, :, 1, :], neglam[l][0:16], P4[:, :, 0, :], ALU.mult, ALU.add,
                            t_lam[0])
                yield True
                tk, tps, tw = psum.take(1)
                for hh in range(nh):
                    a = 16 * (2 * hh if kind == "diff" else hh)
                    t2 = tr(tps[0:16, 16 * hh:16 * hh + 16], Pv[:, a:a + 16], tw, t, signal=hh == nh - 1)
                t3 = vcopy(PTv[:, 0:16 * nh], tps[0:16, 0:16 * nh], t2, alone=False)
                psum.free(tk, t3)
                yield True
                ok, ops, ow = psum.take(1)
                for hh in range(nh):
                    t_pv = mm(ops[0:16, hd * hh:hd * hh + hd], PTv[:, 16 * hh:16 * hh + 16],
                              V[0:16, 0, hd * hh:hd * hh + hd], True, True, ow, t3, signal=True)
                rst_free[0] = t_pv
                yield True
                yield from head_end(l, kind, -1, ok, ops[0:16, 0:512], 16, 0, None, t_pv, att)

            for kind in ("diff", "fox"):
                Q, K, V = (QA, KA, VA) if kind == "diff" else (QB, KB, VB)
                for i in range(4):
                    us = [unit(l, kind, i, m, Q, K, V, M + 128 * i, ready, att, t_nc) for m in range(8)]
                    if full and i == 0:
                        us[1]["start"] = lambda a=(l, kind, Q, K, V, ready, att, t_nc): meta_queries(*a)
                    units += us
            attention(units)
            ao = [ao_toks["diff"]] * 4 + [ao_toks["fox"]] * 4

            def res_evac(c, scale=None):
                def evac(k_, o, tok):
                    hv = o.shape[1]
                    dst = three(h[:, c, cols[0]:cols[1]], n_q, hv)
                    t = tt(dve, dst, dst, o, ALU.add, tok, alone=False)
                    psum.free(k_, t)
                    square(c, h[:, c, cols[0]:cols[1]], t)
                    if not full:
                        gained_square(c, h[:, c, M:L], t)
                return evac
            for c in range(8):
                feature(ao, n_q, c_q, res_evac(c))
        one.close()

        ph = phase()
        r, t_r = rstd(T, 1)
        gg, r2 = small[:, 20:28], scratch[:, 2, 0:T]
        t_gg = tt(dve, gg, P_("g_final"), P_("g_ffn1"), ALU.mult, t_par)
        k_, ps, w = psum.take(1)
        t = mm(ps[:, 0:T], C("mean"), scratch[:, 3, 0:T], True, True, w, gsums[KT - 1], signal=True)
        t_g = t
        t = tt(dve, r2, ps[:, 0:T], r, ALU.mult, t, t_r, s_free[2])
        psum.free(k_, t)
        t = tt(dve, r2, r2, r, ALU.mult, t)
        t = copy_act(r2, r2, t, func=ACT.Ln, bias=1e-6, alone=False)
        t = copy_act(r2, r2, t, func=ACT.Exp, scale=-0.5)
        t_r2 = tt(dve, r2, r2, r, ALU.mult, t)
        s_free[3] = [t_g]

        def apply_final():
            for k in range(KT):
                t = stt(h[:, k, M:L], h[:, k, M:L], P_("g_final", k, k + 1), r, ALU.mult, ALU.mult, t_r, alone=False)
            rst_free[0] = t

        def ffn(gain, ph, again=False, extra=None, scale=None, after=None):
            st = ExitStack()
            name = "first" if again else "second"
            aH = sb(name + "aH", [128, FT, T], F32R, at=st)
            aL = sb(name + "aL", [128, FT, T], F32R, at=st)
            x_toks = norm(gain, h, M, T, 1, xh, xl, ph, scale=scale)
            if after is not None:
                after()
            act_toks = []
            for f in range(FT):
                k_, ps, w = psum.take()
                for s in range(2):
                    c, hh, ll, tw = chunk()
                    for k in range(KT):
                        a = 128 * k
                        t = mm3(ps[:, 512 * s:512 * s + 512], (hh[:, a:a + 128], ll[:, a:a + 128]),
                                (xh[:, k, M:L], xl[:, k, M:L]), k == 0, k == KT - 1, w, tw, x_toks[k],
                                signal=(k == KT - 1))
                    chunk_done(c, t)
                    if s == 0:
                        tg = t
                i = f % 2
                a = copy_act(xb[:, i, 0:T], ps[:, 0:512], tg, xb_free[i], func=ACT.Silu, alone=False)
                b = tt(dve, tmpn[:, i, 0:T], xb[:, i, 0:T], ps[:, 512:1024], ALU.mult, a, t, tmp_free[i], alone=False)
                psum.free(k_, b)
                xb_free[i] = b
                p, q = split(aH[:, f, :], aL[:, f, :], tmpn[:, i, 0:T], b, ph)
                tmp_free[i] = [p, q]
                act_toks.append([p, q])
                if extra is not None:
                    next(extra, None)
            for m in range(KT):
                k_, ps, w = psum.take()
                for f0, nf in ((0, 8), (8, 8), (16, 6)):
                    c, hh, ll, tw = chunk()
                    for kk in range(nf):
                        f = f0 + kk
                        t = mm3(ps[:, 0:512], (hh[:, 128 * kk:128 * kk + 128], ll[:, 128 * kk:128 * kk + 128]),
                                (aH[:, f, :], aL[:, f, :]), f == 0, f == FT - 1, w, tw, act_toks[f], signal=(kk == nf - 1))
                    chunk_done(c, t)
                t = stt(h[:, m, M:L], ps[:, 0:512], 0.5, h[:, m, M:L], ALU.mult, ALU.add, t, alone=False)
                psum.free(k_, t)
                if again:
                    square(m, h[:, m, M:L], t)
            table(LN_EXP)
            st.close()

        mid = ExitStack()
        cs = sb("cs", [128, 2, T], at=mid)
        cos2, sin2 = cs[:, 0, :], cs[:, 1, :]
        ph = phase()
        t_cs = [None]

        def rotary():
            ang, kk_, mm_ = scratch[:, 0, 0:T], scratch[:, 1, 0:T], scratch[:, 2, 0:T]
            posi = scratch[:, 3, 0:T].bitcast(I32)
            t_pos = load("d_pos", posi, pos.partition_broadcast(128), ph)
            t = vcopy(ang, posi, t_pos, s_free[0], s_free[1], s_free[2])
            ts(ang, ang, C("freq"), None, ALU.mult, ALU.bypass)
            two_pi = 2.0 * math.pi
            MAGIC = 12582912.0

            def pieces(v, unit):
                res, rest = [], v
                for j in range(3):
                    step = 2.0 ** (math.floor(math.log2(abs(v))) - 7 - 8 * j)
                    q = math.floor(rest / step) * step
                    if q:
                        res.append(q)
                    rest -= q
                res.append(float(np.float32(rest)))
                return res

            yield
            for unit in (4096.0, 1.0):
                ts(kk_, ang, float(np.float32(1.0 / (two_pi * unit))), MAGIC, ALU.mult, ALU.add)
                ts(kk_, kk_, -MAGIC, None, ALU.add, ALU.bypass)
                for v in pieces(two_pi * unit, unit):
                    stt(ang, kk_, -v, ang, ALU.mult, ALU.add)
                    yield
            t = ts(ang, ang, math.pi, -math.pi, ALU.min, ALU.max)
            t1 = copy_act(cs[:, 1, :], ang, t, func=ACT.Sin)
            t = stt(mm_, ang, -1.0, ang, ALU.mult, ALU.max)
            t = ts(mm_, mm_, -1.0, math.pi / 2, ALU.mult, ALU.add)
            t_cs[0] = copy_act(cs[:, 0, :], mm_, t, func=ACT.Sin)
            for k in range(4):
                s_free[k] = [t_cs[0], t]

        s_free[2] = s_free[2] + [t_r2]
        ffn(gg, ph, True, rotary(), (r2, [t_r2, t_gg]), apply_final)

        two = ExitStack()
        cst2[0] = sb("cst2", [128, NCONST - NC1], at=two)
        strictR = sb("strictR", [128, 128], F32R, at=two)[:, :]
        QS = sb("QS", [128, 8, T], at=two)
        KS = sb("KS", [128, 4, T], at=two)
        VSB = sb("VSB", [128, 4, 4, 4, 64], at=two)
        nsa = ExitStack()
        QN = sb("QN", [128, 8, T], F32R, at=nsa)
        KSW = sb("KSW", [128, 2, 2, 2, T], F32R, at=nsa)
        VSW = sb("VSW", [128, 4, 256], at=nsa)
        Gt = sb("Gt", [128, 4, 24], at=nsa)
        KC = sb("KC", [128, 2, 32], at=nsa)
        VC = sb("VC", [128, 8, 64], at=nsa)
        OA = sb("OA", [128, 2, 512], at=nsa)
        cmp_ = ExitStack()
        X2 = sb("X2", [128, 2, T], at=cmp_)
        Y = [sb(f"Y{i}", [128, 2, 66, 8], at=cmp_) for i in range(2)]
        kcx = sb("kcx", [128, 128], at=cmp_)
        hid = sb("hid", [128, 2, 2, 64], at=cmp_)
        ph = phase()
        t_c2 = load("d_cst2", cst2[0][:, :], const[:, NC1:NCONST], ph)
        x_toks = norm("g_mix", h, M, T, 1, xh, xl, ph)
        for k in range(8):
            a = 64 * (1 - k % 2)
            fill(QS[a:a + 64, k, :], 0.0, ph, alone=False)
        fill(VC[:, :, :], 0.0, ph, alone=False)
        t_z = fill(VSB[:, :, :, :, :], 0.0, ph, alone=False)

        def head_norm(src, i, t_src, n, gain, dst, *waits):
            at = 256 * i if n <= 256 else 0
            s = scratch[:, 3, at:at + n]
            t = copy_act(s, src, t_src, s_free[3], func=ACT.Square)
            yield True
            k_, ps, w = psum.take(1)
            t = mm(ps[:, 0:n], C("blk"), s, True, True, w, t, signal=True)
            t = copy_act(s, ps[:, 0:n], t, func=ACT.Ln, bias=1e-6)
            psum.free(k_, t)
            t = copy_act(s, s, t, func=ACT.Exp, scale=-0.5)
            t = stt(dst, src, gain, s, ALU.mult, ALU.mult, t, *waits)
            s_free[3] = [t]
            return t

        def normed_roped(gain, dsts, n=T, do_rope=True):
            def evac(k_, o, tok):
                i = xb_k[0]
                xb_k[0] ^= 1
                x_ = xb[:, i, 0:n]
                t = copy_act(x_, o[:, 0, :] if len(o.shape) == 3 else o, tok, xb_free[i], alone=False)
                psum.free(k_, t)
                t = yield from head_norm(x_, i, t, n, gain, x_)
                yield True
                if do_rope:
                    u = t1b[:, 0, 0:n]
                    a, b, c = rope(x_, t, n, cos2, sin2, [((0, 128), u)], ph, t_cs[0])
                    xb_free[i] = [a, b]
                    s_free[0] = []
                    for (p0, p1), highs, lows in dsts:
                        for dst in highs:
                            t = copy_act(dst, u[p0:p1, :], c, ph, alone=False)
                            s_free[0].append(t)
                        for dst in lows:
                            s_free[0].append(tt(dve, dst, u[p0:p1, :], highs[0].bitcast(F32), ALU.subtract, t, c, ph,
                                                alone=False))
                else:
                    for (p0, p1), dst in dsts:
                        t2 = vcopy(dst, xb[p0:p1, i, 0:n], t, ph, alone=False)
                    xb_free[i] = [t2]
            return evac

        halves_ = ((0, 64), (64, 128))

        def qn_dsts(c):
            return [((a, b), [QN[a:b, 2 * c + g, :]], [QN[a_:b_, 2 * c + g, :]])
                    for g, (a, b), (a_, b_) in zip((0, 1), halves_, halves_[::-1])]

        def kn_dsts(c):
            return [((a, b), [KSW[a:b, c, g, 0, :], KSW[a_:b_, c, g, 0, :]], [KSW[a:b, c, g, 1, :], KSW[a_:b_, c, g, 1, :]])
                    for g, (a, b), (a_, b_) in zip((0, 1), halves_, halves_[::-1])]

        def qs_evac(c):
            def evac(k_, o, tok):
                for (p0, p1), dst in q_dsts(QS, c, (0, T)):
                    t = copy_act(dst, o[p0:p1, 0, :], tok, ph, t_z, scale=0.125, alone=False)
                psum.free(k_, t)
            return evac

        def ks_evac(c):
            def evac(k_, o, tok):
                evac_copy(KS[:, c, :], o[:, 0, :], k_, tok, ph, q=dve)
            return evac

        fill(Y[0][:, :, 64:66, :], 0.0, ph, q=pool)
        zz = fill(Y[1][:, :, 64:66, :], 0.0, q=pool)
        x2_free, t_y, got = None, [], []
        for s in range(2):
            feature(x_toks, T, M, lambda k_, o, tok: got.append((k_, o[:, 0, :], tok)))
        for s in range(2):
            k_, src, tok = got[s]
            w = [tok, ph, x2_free]
            copy_act(X2[0:64, 0, :], src[0:64, :], *w, alone=False)
            b = copy_act(X2[0:64, 1, :], src[64:128, :], *w, alone=False)
            vcopy(X2[64:128, 0, 0:T - 1], src[0:64, 1:T], b, *w, alone=False)
            d = vcopy(X2[64:128, 1, 0:T - 1], src[64:128, 1:T], b, *w, alone=False)
            psum.free(k_, b, d)
            pe_ = P_("pe_k" if s == 0 else "pe_v")
            xin = X2[:, :, :].rearrange("p h (n j) -> p (h n) j", j=16)[:, :, 0:16:2]
            for v in range(2):
                x2_free = tt(dve, Y[s][:, v, 0:64, :], xin,
                             pe_[:, 8 * v:8 * v + 8].unsqueeze(1).to_broadcast([128, 64, 8]), ALU.add, b, d)
            t_y.append([x2_free, zz])

        t_hid = [None, None]
        cbank = [None]

        def compress():
            for s in range(2):
                cbank[0] = psum.take()
                k_, ps, w = cbank[0]
                for v in range(2):
                    for j0 in (0, 4):
                        c, ww, tw = whole_chunk()
                        for mt in range(2):
                            for jj in range(4):
                                j = j0 + jj
                                a0 = 256 * jj + 128 * mt
                                t = mm(ps[:, 512 * mt:512 * mt + 64], ww[:, a0:a0 + 128], Y[s][:, v, v:v + 64, j],
                                       v == 0 and j == 0, v == 1 and j == 7, w, tw, t_y[s], signal=(jj == 3))
                        whole_done(c, t)
                        if (v, j0) == (1, 4):
                            t_hid[s] = vcopy(hid[:, s, :, :], ps[:, :].rearrange("p (a b) -> p a b", a=2)[:, :, 0:64],
                                             t, ph, alone=False)
                            psum.free(k_, t_hid[s])
                        yield
        mlp = compress()

        for c in range(4):
            feature(x_toks, T, M, normed_roped(gq8, qn_dsts(c)))
            next(mlp)
            feature(x_toks, T, M, qs_evac(c))
            next(mlp)
        t_hid = copy_act(hid[:, :, :, :], hid[:, :, :, :], t_hid, func=ACT.Gelu_apprx_tanh)
        table(LN_EXP)
        for c in range(2):
            feature(x_toks, T, M, normed_roped(P_("g_ks") if c == 0 else P_("g_kw"), kn_dsts(c)))
        starts2 = [M + 128 * i for i in range(4)]

        def vsw_evac(i, ps, tok):
            t = copy_act(VSW[:, i, :], ps[:, 0:256], tok, ph, alone=False)
            return [t, gate_exp(0, i, ps, tok)]

        def gate_exp(br, i, ps, tok):
            return copy_act(Gt[:, i, 8 * br:8 * br + 8], ps[:, 256:264], tok, ph, func=ACT.Exp, scale=-1.0, alone=False)

        def vsb_evac(c):
            def evac(i, ps, tok):
                src = ps[:, 0:256].rearrange("p (a b d) -> p a b d", a=2, b=2)
                dst = VSB[:, i, 2 * c:2 * c + 2, 0:4:3, :]
                t = vcopy(dst, src, tok, t_z, alone=False)
                return [t, gate_exp(c + 1, i, ps, t)]
            return evac
        def compressed_keys():
            ce = small[:, 64:192].rearrange("p (c h n) -> p c h n", c=2, h=2)
            fill(small[:, 64:192], 0.0)
            for c in range(2):
                for hh in range(2):
                    t = vcopy(ce[:, c, hh, 0:31], cs[:, c, :].rearrange("p (n j) -> p n j", j=16)[:, 1:32, 15],
                              t_cs[0], alone=(c + hh == 0))
            t_ce = t
            k_, ps, w = psum.take(1)
            for mt in range(2):
                t = mm(ps[:, 0:64], P_("w2k", 128 * mt, 128 * mt + 128), hid[:, 0, mt, :], mt == 0, mt == 1, w, t_hid,
                       signal=(mt == 1))
            x_ = kcx[:, 0:64]
            t = copy_act(x_, ps[:, 0:64], t, ph, alone=False)
            psum.free(k_, t)
            k_, ps, w = psum.take(1)
            for g in range(2):
                for mt in range(2):
                    t2 = mm(ps[0:32, 64 * g:64 * g + 64], hid[:, 1, mt, 32 * g:32 * g + 32],
                            P_("w2v", 64 * mt, 64 * mt + 64), mt == 0, mt == 1, w, t_hid, signal=True)
            for m in range(8):
                r0, g = 32 * (m % 4), m % 2
                t2 = vcopy(VC[r0:r0 + 32, m, :], ps[0:32, 64 * g:64 * g + 64], t2, t_z, alone=False)
            psum.free(k_, t2)
            sq = kcx[:, 64:128]
            t3 = copy_act(sq, x_, t, func=ACT.Square)
            yield
            k_, ps, w = psum.take(1)
            t3 = mm(ps[:, 0:64], C("blk"), sq, True, True, w, t3, signal=True)
            t3 = copy_act(sq, ps[:, 0:64], t3, func=ACT.Ln, bias=1e-6, alone=False)
            psum.free(k_, t3)
            t3 = copy_act(sq, sq, t3, func=ACT.Exp, scale=-0.5)
            t = stt(x_, x_, P_("g_kc"), sq, ALU.mult, ALU.mult, t3)
            yield
            a, b, c = rope(x_, t, 64, small[:, 64:128], small[:, 128:192],
                           [((0, 64), kcx[0:64, 64:128]), ((64, 128), kcx[64:128, 64:128])], t_ce)
            for g, (a, b) in enumerate(halves_):
                for a_, b_ in halves_:
                    vcopy(KC[a_:b_, g, :], kcx[a:b, 64 + 32 * g:96 + 32 * g], c, alone=False)
            yield
        keys = compressed_keys()
        for evac in (vsw_evac, vsb_evac(0), vsb_evac(1)):
            token_tiles(x_toks, starts2, 264, evac, between=lambda: next(keys, None))
        ts(Gt[:, :, :], Gt[:, :, :], 1.0, None, ALU.add, ALU.bypass, act.last())
        t_gt = recip(Gt[:, :, :], Gt[:, :, :])
        t_strict = copy_act(strictR, C("strictT"), ph, t_c2)

        while pending:
            advance()
        drain(keys)
        ready = phase()
        for c in range(4):
            feature(x_toks, T, M, ks_evac(c))
        cmp_.close()
        att = phase()
        attention_buffers("2", nsa, ready)
        ao = []

        def compressed(i):
            oa, c0 = OA[:, i % 2, :], 128 * i
            sk, sps, sw = psum.take(1)
            mm(sps[:, 0:256], ident, C("cmpadd", 32 * i, 32 * i + 32).unsqueeze(1).to_broadcast([128, 8, 32]),
               True, False, sw, ready, t_c2)
            for m in range(8):
                t = mm(sps[:, 32 * m:32 * m + 32], QN[:, m, c0:c0 + 128].bitcast(F32), KC[:, m % 2, :], False, m == 7, signal=(m == 7))
            yield True
            S3 = sps[:, 0:256].rearrange("p (a b) -> p a b", a=8)
            Pv = scratch[:, 0, 0:256]
            P3 = Pv.rearrange("p (a b) -> p a b", a=8)
            mx = small[:, 32:40]
            t = reduce(mx, S3, ALU.max, t)
            yield True
            t = tt(dve, P3, S3, mx.unsqueeze(2).to_broadcast([128, 8, 32]), ALU.subtract, cfree[0], t)
            psum.free(sk, t)
            t = copy_act(Pv, Pv, t, func=ACT.Exp)
            yield True
            tt(dve, P3, P3, C("cmp01", 32 * i, 32 * i + 32).unsqueeze(1).to_broadcast([128, 8, 32]), ALU.mult, t)
            reduce(mx, P3, ALU.add)
            yield True
            ts(mx, mx, 1e-30, None, ALU.max)
            recip(mx, mx)
            tt(dve, mx, mx, Gt[:, i, 0:8], ALU.mult)
            t = tt(dve, P3, P3, mx.unsqueeze(2).to_broadcast([128, 8, 32]), ALU.mult)
            yield True
            r = flip_pe(None, t, [(0, 128), (128, 256)], src=Pv)
            cfree[0] = r[2]
            buf = scratch[:, 1, 0:256]
            t3 = copy_act(buf, r[1][:, 0:256], r[2], cfree[1], alone=False)
            psum.free(r[0], t3)
            yield True
            ok, ops, ow = psum.take(1)
            for m in range(8):
                tv = mm(ops[:, 64 * m:64 * m + 64], buf[:, 128 * (m // 4):128 * (m // 4) + 128], VC[:, m, :],
                        True, True, ow, t3, signal=(m == 7))
            cfree[1] = tv
            yield True
            t = copy_act(oa, ops[:, 0:512], tv, oa_free[0])
            oa_tok[0] = t
            psum.free(ok, t)

        cfree = [None, None]
        oa_tok = [None]
        nsa_out = {}

        def nsa_unit(i, br, m):
            c0 = 128 * i
            n = 128 * (i + 1)
            blocks = [(128 * j, 128 * j + 128) for j in range(i + 1)]

            def score():
                return scores(QN[:, m, c0:c0 + 128], lambda a, b: [KSW[:, br, m % 2, part, a:b] for part in range(2)], n, False, None, causalR, [ready])

            def pv(buf, t3):
                if m == 0:
                    nsa_out[(i, br)] = psum.take(1)
                ok, ops, ow = nsa_out[(i, br)]
                a = 128 * br + 64 * (m % 2)
                for j in range(i + 1):
                    tv = mm(ops[:, 64 * m:64 * m + 64], buf[:, 128 * j:128 * j + 128], VSW[:, j, a:a + 64],
                            j == 0, j == i, ow, t3, signal=(j == i))
                return tv

            def end(tok):
                ok, ops, ow = nsa_out[(i, br)]
                oa = OA[:, i % 2, :]
                r = rr[:, br, 0:8]
                rs_free[br] = ts(rs[:, br, 0:8], rs[:, br, 0:8], 1e-30, None, ALU.max, ALU.bypass, tok)
                rs_free[br] = recip(r, rs[:, br, 0:8])
                tt(dve, r, r, Gt[:, i, 8 * (br + 1):8 * (br + 1) + 8], ALU.mult)
                yield True
                u = scratch[:, 2, 0:512]
                t = tt(dve, u.rearrange("p (a b) -> p a b", a=8), ops[:, 0:512].rearrange("p (a b) -> p a b", a=8),
                       r.unsqueeze(2).to_broadcast([128, 8, 64]), ALU.mult, tok)
                psum.free(ok, t)
                yield True
                t = tt(dve, oa, oa, u, ALU.add, oa_tok[0], t)
                if br:
                    yield True
                    yield from finish_tile(oa, t, 128, 8, None, False, 4, 0, M + c0, None, None, ao, lambda t: None, att)

            def job(p, t):
                return dict(p=p, t=t, blocks=blocks, pv=pv, end=end if m == 7 else None, every=3)
            u = dict(ahead=2, score=score, sum=rs[:, br, m:m + 1], sum_waits=lambda: [rs_free[br]], job=job)
            if br == 0 and m == 0:
                u["start"] = lambda: compressed(i)
            return u

        attention([nsa_unit(i, br, m) for i in range(4) for br in range(2) for m in range(8)])

        nsa.close()
        att = phase()
        SPb = sb("SPb", [128, 2, 4, T], at=two)
        Ab = sb("Ab", [128, 2, 4, T], at=two)
        RT = sb("RT", [128, 2, T], at=two)
        sp_free = [[], []]
        rt_free = [None, None]
        af = [[], []]
        opair = {}
        st = {}

        def sb_scores(hd_, j):
            k_, ps, w = psum.take(1)
            q0 = 128 * j
            mm(ps[:, 0:T - q0], KS[:, hd_ // 2, q0:q0 + 128], QS[:, hd_, q0:T], True, False, w)
            t = mm(ps[:, 0:128], identR[:, :], strictR, False, True, t_strict, signal=True)
            st[(hd_, j)] = [k_, ps, t]

        def sb_softplus(hd_, j):
            k_, ps, t = st[(hd_, j)]
            u, n = hd_ % 2, T - 128 * j
            o, e_, sp = ps[:, 0:n], Ab[:, u, j, 0:n], SPb[:, u, j, 0:n]
            t2 = ts(sp, o, 0.0, None, ALU.max, ALU.bypass, t, sp_free[u], att, alone=False)
            t = stt(e_, sp, -2.0, o, ALU.mult, ALU.add, t2, af[u], alone=False)
            t = copy_act(e_, e_, t, func=ACT.Exp, alone=False)
            t = copy_act(e_, e_, t, func=ACT.Ln, bias=1.0, alone=False)
            st[(hd_, j)].append(t)

        def sb_add(hd_, j):
            u, n = hd_ % 2, T - 128 * j
            sp = SPb[:, u, j, 0:n]
            st[(hd_, j)][3] = tt(dve, sp, sp, Ab[:, u, j, 0:n], ALU.add, st[(hd_, j)][3], alone=False)

        def sb_suffix(hd_, j):
            k_, ps, _, t_sp = st[(hd_, j)]
            u, q0 = hd_ % 2, 128 * j
            n = T - q0
            sp = SPb[:, u, j, 0:n]
            t2 = mm(ps[:, 0:n], C("tri"), sp, False, True, t_sp, signal=True, onto=True)
            if j < 3:
                t2 = mm(ps[:, 128:n], C("negone"), RT[:, u, q0 + 128:T], False, True, rt_tok[u], signal=True, onto=True)
            if j == 3:
                rt_tok[u] = vcopy(RT[:, u, 384:512], sp, rt_free[u], t_sp, alone=False)
            elif j:
                vcopy(RT[:, u, q0:q0 + 128], sp[:, 0:128], t2, alone=False)
                rt_tok[u] = tt(dve, RT[:, u, q0 + 128:T], RT[:, u, q0 + 128:T], sp[:, 128:n], ALU.add, t2, rt_tok[u],
                               alone=False)
            else:
                rt_free[u] = t2
                sp_free[u] = [t2, rt_tok[u]]
            st[(hd_, j)].append(t2)

        def sb_exp(hd_, j):
            k_, ps, _, _, t2 = st[(hd_, j)]
            u, n = hd_ % 2, T - 128 * j
            t3 = copy_act(Ab[:, u, j, 0:n], ps[:, 0:n], t2, func=ACT.Exp, alone=False)
            psum.free(k_, t3)
            st[(hd_, j)].append(t3)

        def sb_values(hd_):
            u, tile_ = hd_ % 2, hd_ // 2
            if u == 0:
                opair[tile_] = psum.take(1)
            ok, ops, ow = opair[tile_]
            for j in range(4):
                vt = VSB[:, j, tile_, 0:2, :] if u == 0 else VSB[:, j, tile_, 2:4, :]
                t = mm(ops[:, 128 * j:T], vt.rearrange("p a b -> p (a b)"), Ab[:, u, j, 0:T - 128 * j],
                       u == 0 and j == 0, u == 1 and j == 3, ow, st[(hd_, 0)][5], signal=(j == 3))
            af[u] = [t]
            if u:
                f = flip[0]
                flip[0] ^= 1
                t = copy_act(fin[:, f, 0:512], ops[:, 0:512], t, fin_free[f], alone=False)
                psum.free(ok, t)
                a, b = split(xh[:, 4 + tile_, M:L], xl[:, 4 + tile_, M:L], fin[:, f, 0:512], t, att)
                fin_free[f] = [a, b]
                ao_sb.extend([a, b])

        ao_sb = []
        rt_tok = [None, None]
        seq = [(a, j) for a in range(8) for j in (3, 2, 1, 0)]
        sb_scores(*seq[0])
        sb_scores(*seq[1])
        for k in range(len(seq) + 3):
            if k < len(seq):
                sb_softplus(*seq[k])
            if 1 <= k < len(seq) + 1:
                sb_add(*seq[k - 1])
            if 2 <= k < len(seq) + 2:
                sb_suffix(*seq[k - 2])
            if k + 2 < len(seq):
                sb_scores(*seq[k + 2])
            if 2 <= k < len(seq) + 2:
                sb_exp(*seq[k - 2])
            if k >= 3 and seq[k - 3][1] == 0:
                sb_values(seq[k - 3][0])

        def res2(c):
            def evac(k_, o, tok):
                dst = h[:, c, M:L]
                t = tt(dve, dst, dst, o[:, 0, :], ALU.add, tok, alone=False)
                psum.free(k_, t)
                square(c, dst, t)
            return evac
        two.close()
        mid.close()

        mem = ExitStack()
        hm = sb("hm", [128, KT, 256], at=mem)
        mh = sb("mh", [128, KT, 256], F32R, at=mem)
        ml = sb("ml", [128, KT, 256], F32R, at=mem)
        KM = sb("KM", [128, 2, 256], at=mem)
        VM = sb("VM", [128, 2, 256], at=mem)
        QM = sb("QM", [128, 4, T], at=mem)
        ph = phase()
        attention_buffers("3", mem, ph)
        t_mem = load("d_mem", hm[:, :, :], memT, ph)
        fill(QM[:, :, :], 0.0, ph)
        m_sum = []

        def mem_square(k):
            acc, sq = scratch[:, 3, 0:256], scratch[:, 3, 256:512]
            dst = sq if k else acc
            t = copy_act(dst, hm[:, k, :], t_mem, m_sum[-1:] if k > 1 else s_free[3], func=ACT.Square, alone=False)
            if k:
                t = tt(dve, acc, acc, sq, ALU.add, t, m_sum[-1], alone=False)
            m_sum.append(t)
        for c in range(8):
            feature([ao] * 4 + [ao_sb] * 4, T, M, res2(c))
            if 1 <= c < 5:
                mem_square(2 * c - 2)
                mem_square(2 * c - 1)
            if c == 5:
                m_toks = norm("g_memkv", hm, 0, 256, 1, mh, ml, ph, sums=(scratch[:, 3, 0:256], m_sum[-1], 3))
        def vm_evac(i, ps, tok):
            return copy_act(VM[:, i, :], ps[:, 0:256], tok, ph, alone=False)
        token_tiles(m_toks, [0, 128], 256, vm_evac, xt=(mh, ml))
        x_toks = norm("g_memx", h, M, T, 1, xh, xl, ph)
        for c in range(2):
            feature(m_toks, 256, 0, normed_roped(P_("g_mk"), [((0, 128), KM[:, c, :])], n=256, do_rope=False),
                    xt=(mh, ml), steps=0)
        for c in range(2):
            feature(x_toks, T, M, normed_roped(gmq8, q_dsts(QM, c, (0, T)), do_rope=False), steps=2 - c)
        while pending:
            advance()
        att = phase()
        ao = []
        mem_out = {}

        def mem_unit(i, m):
            c0 = 128 * i

            def score():
                return scores(QM[:, m, c0:c0 + 128], lambda a, b: [KM[:, m // 2, a:b]], 256, False, None, None, [att])

            def pv(buf, t3):
                if m == 0:
                    mem_out[i] = psum.take(1)
                ok, ops, ow = mem_out[i]
                for j in range(2):
                    tv = mm(ops[:, 64 * m:64 * m + 64], buf[:, 128 * j:128 * j + 128], VM[:, j, 64 * m:64 * m + 64],
                            j == 0, j == 1, ow, t3, signal=(j == 1))
                return tv

            def end(tok):
                ok, ops, ow = mem_out[i]
                r = rr[:, i % 2, 0:4]
                rs_free[i % 2] = recip(r, rs[:, i % 2, 0:4], tok)
                yield from finish_tile(ops[:, 0:256], tok, 128, 4, r.unsqueeze(2).to_broadcast([128, 4, 64]), False, 2, 0,
                                       M + c0, None, None, ao, lambda t: psum.free(ok, t), att)

            def job(p, t):
                return dict(p=p, t=t, blocks=[(0, 128), (128, 256)], pv=pv, end=end if m == 3 else None, every=3)
            return dict(ahead=2, score=score, sum=rs[:, i % 2, m:m + 1], sum_waits=lambda: [rs_free[i % 2]], job=job)

        attention([mem_unit(i, m) for i in range(4) for m in range(4)])
        for half in range(2):
            c, hh, ll, tw = chunk()
            for mm_i in range(4):
                m = 4 * half + mm_i

                def wt(part, k, m=mm_i, hh=hh, ll=ll):
                    return (hh, ll)[part][:, 512 * k + 128 * m:512 * k + 128 * m + 128]
                k_, o, tok = tile_feature(wt, (xh, xl), [ao] * 2, T, M, tw, nk=2)
                t = tt(dve, h[:, m, M:L], h[:, m, M:L], o[:, 0, :], ALU.add, tok, alone=False)
                psum.free(k_, t)
                square(m, h[:, m, M:L], t)
            chunk_done(c, tok)
        mem.close()

        ffn("g_ffn2", phase())
        s_out = sem("d_out")
        sync(lambda e: e.dma_start(out, h[:, :, M:L]).then_inc(s_out, 16), dve.last(), alone=False, signal=False)
        sync(lambda e: e.wait_ge(s_out, 16), alone=False, signal=False)
        assert at["use"] == len(sizes)

        block = ctx.enter_context(nc.Block())

        @block.sync
        def _(e):
            sync.emit(e)

        @block.scalar
        def _(e):
            act.emit(e)

        @block.vector
        def _(e):
            dve.emit(e)

        @block.gpsimd
        def _(e):
            pool.emit(e)

        @block.tensor
        def _(e):
            pe.emit(e)


def constants():
    c = np.zeros((128, NCONST), np.float32)

    def put(name, v):
        c[:, CONST[name][0]:CONST[name][1]] = v
    i = np.arange(128)
    put("ident", np.eye(128))
    put("mean", 1.0 / D)
    put("blk", (i[:, None] // 64 == i[None, :] // 64) / 64.0)
    rot = np.zeros((128, 128))
    for b in (0, 64):
        for d in range(8):
            rot[b + d + 8, b + d] = -1.0
            rot[b + d, b + d + 8] = 1.0
    put("rot", rot)
    put("causal", np.where(i[None, :] > i[:, None], NEG, 0.0))
    put("strictT", np.where(i[:, None] >= i[None, :], NEG, 0.0))
    put("chunk", np.where((i[None, 64:] >= 64) & (i[:, None] < 64), NEG, 0.0))
    put("pick", (i[:, None] == np.arange(8)) | (i[:, None] == 32 + np.arange(8)))
    put("tri", np.where(i[:, None] >= i[None, :], -1.0, 0.0))
    put("negone", -1.0)
    n = np.arange(32)
    q = i[:, None, None] + 128 * np.arange(4)[None, :, None]
    seen = (16 * n[None, None, :] + 31 <= q) & (n[None, None, :] < 31)
    put("cmpadd", np.where(seen, 0.0, NEG).reshape(128, 128))
    put("cmp01", np.where(seen, 1.0, 0.0).reshape(128, 128))
    d = i % 64
    theta = np.float32(500000.0)
    f8 = theta ** (-np.arange(0, 16, 2, dtype=np.float32) / np.float32(16))
    put("freq", np.where(d < 16, f8[d % 8], 0.0)[:, None])
    inv = (np.float32(1.0) / (theta ** (np.arange(0, 16, 2, dtype=np.float32) / np.float32(16)))).astype(np.float32)
    ang = np.where(d < 16, inv[d % 8], 0.0).astype(np.float32)[:, None] * np.arange(L, dtype=np.float32)[None, :]
    put("cos", np.cos(ang.astype(np.float64)))
    put("sin", np.sin(ang.astype(np.float64)))
    return c


def rows(w):
    return w.reshape(w.shape[0] // 128, 128, w.shape[1]).transpose(1, 0, 2)


def by_cols(w, width=128):
    r = rows(w)
    return [r[:, :, a:a + width].reshape(-1) for a in range(0, w.shape[1], width)]


def by_halves(w):
    r = rows(w)
    return [r[:, 0:4].reshape(-1), r[:, 4:8].reshape(-1)]


def pieces_of(w, sizes):
    at, out = 0, []
    for n in sizes:
        out.append(w[:, at:at + n])
        at += n
    return out


def weights(a):
    out = []
    for l in range(2):
        dq, dk, dv, dg, fq, fk, fv, ff, fg = pieces_of(a["w_in"][l], (512,) * 7 + (8, 512))
        for d, f in ((dq, fq), (dk, fk)):
            for pair in zip(by_cols(d), by_cols(f)):
                out += pair
        out += by_halves(dv[:, 0:256]) + by_halves(dv[:, 256:512])
        out += by_halves(fv[:, 0:256]) + by_halves(np.concatenate([fv[:, 256:512], ff], axis=1))
        out += by_cols(dg) + by_cols(fg)
        out += by_cols(a["w_out"][l])

    def ffn(wg, wu, wd):
        r = []
        for g, u in zip(by_cols(wg), by_cols(wu)):
            r += [g, u]
        d = rows(wd)
        for m in range(8):
            for f0, f1 in ((0, 8), (8, 16), (16, 22)):
                r.append(d[:, f0:f1, 128 * m:128 * m + 128].reshape(-1))
        return r
    out += ffn(a["ffn1_wg_2"][0], a["ffn1_wu_2"][0], a["ffn1_wd_2"][0])
    q, kc, vc, ks, vs, kw, vw, gt, qs, kk, vv = pieces_of(a["w_in_2"][0], (512,) + (128,) * 6 + (24, 512, 512, 512))
    heads = [m // 2 + 4 * (m % 2) for m in range(8)]
    w1 = []
    for name in ("cmp_w1_k_2", "cmp_w1_v_2"):
        r = rows(a[name][0])
        w1 += [r[:, j:j + 4].reshape(-1) for j in range(0, 16, 4)]
    gt = gt.reshape(D, 8, 3)[:, heads].transpose(0, 2, 1).reshape(D, 24)
    seq = []
    for pair in zip(by_cols(q.reshape(D, 8, 64)[:, heads].reshape(D, 512)), by_cols(qs)):
        seq += pair
    rest = by_cols(ks) + by_cols(kw)
    for c, v in enumerate(([vs, vw], [vv[:, 0:256]], [vv[:, 256:512]])):
        rest += by_halves(np.concatenate(v + [gt[:, 8 * c:8 * c + 8]], axis=1))
    out += by_cols(kc) + by_cols(vc)
    for pair in zip(seq, w1):
        out += pair
    out += rest + by_cols(kk)
    wo = a["w_out_2"][0]
    out += by_cols(np.concatenate([wo[0:512].reshape(8, 64, D)[heads].reshape(512, D), wo[512:]], axis=0))
    out += by_halves(a["mem_wv_2"][0]) + by_cols(a["mem_wk_2"][0]) + by_cols(a["mem_wq_2"][0])
    out += by_cols(a["mem_wo_2"][0], 512)
    out += ffn(a["ffn2_wg_2"][0], a["ffn2_wu_2"][0], a["ffn2_wd_2"][0])
    return np.concatenate(out)


def params(a):
    parts = {}

    def col(g):
        return g.reshape(8, 128).T
    parts["g_norm0"], parts["g_norm1"] = col(a["norm_gain"][0]), col(a["norm_gain"][1])
    parts["g_final"] = col(a["final_gain"])
    for n, k in (("g_ffn1", "ffn1_norm_2"), ("g_mix", "mix_norm_2"), ("g_memx", "mem_x_norm_2"),
                 ("g_memkv", "mem_kv_norm_2"), ("g_ffn2", "ffn2_norm_2")):
        parts[n] = col(a[k][0])
    for l in range(2):
        parts[f"g_sub{l}"] = a["subln_gain"][l][:, None]
        parts[f"fb{l}"] = np.broadcast_to(a["forget_bias"][l][None, :], (128, 8))
        parts[f"lam{l}"] = np.stack([np.concatenate([a["lambda_q1"][l], a["lambda_q2"][l]]),
                                     np.concatenate([a["lambda_k1"][l], a["lambda_k2"][l]])], axis=1)
    for n, k in (("g_q", "nsa_q_norm_2"), ("g_kc", "nsa_kc_norm_2"), ("g_ks", "nsa_ks_norm_2"),
                 ("g_kw", "nsa_kw_norm_2"), ("g_mq", "mem_q_norm_2"), ("g_mk", "mem_k_norm_2")):
        parts[n] = np.concatenate([a[k][0], a[k][0]])[:, None]
    for n, k in (("pe_k", "cmp_pos_k_2"), ("pe_v", "cmp_pos_v_2")):
        parts[n] = a[k][0].reshape(16, 128).T
    w2 = rows(a["cmp_w2_k_2"][0])
    parts["w2k"] = np.concatenate([w2, w2], axis=2).reshape(128, 256)
    parts["w2v"] = rows(a["cmp_w2_v_2"][0]).reshape(128, 128)
    return np.concatenate([parts[n] for n in PARAM], axis=1)


def kernel(**inputs):
    import concourse.bacc as bacc
    from concourse.bass_utils import run_bass_kernel_spmd as run

    a = {k: np.asarray(v) for k, v in inputs.items()}
    hT = np.concatenate([a["meta_tokens"], a["x"][0]], axis=0).T
    arrays = {
        "wstream": weights(a),
        "xT": rows(hT),
        "memT": rows(a["mem_2"][0].T),
        "pos": a["positions_2"].reshape(T),
        "const": constants(),
        "param": params(a),
    }
    arrays = {k: np.ascontiguousarray(v) for k, v in arrays.items()}
    nc = bacc.Bacc("TRN2", target_bir_lowering=False, num_devices=1)
    args = [nc.dram_tensor(k, v.shape, mybir.dt.from_np(v.dtype), kind="ExternalInput").ap() for k, v in arrays.items()]
    args.append(nc.dram_tensor("out", (128, KT, T), F32, kind="ExternalOutput").ap())
    program(nc, *args)
    r = run(nc, [arrays], core_ids=[0])
    got = r.results[0]["out"]
    return got.transpose(2, 1, 0).reshape(1, T, D)
```
